# Optimizing a Trainium2 kernel written in Bass

```python
import math, functools
import jax, jax.numpy as jnp
from jax import lax
import numpy as np

D_MODEL = 1024
BATCH = 1
SEQ = 1024
DEPTH = 2
DEC_BATCH = 8
DEC_SEQ = 4
PAST_LEN = 512
PAGE_SIZE = 128

MIX_W = D_MODEL
A_W = MIX_W // 2
B_W = MIX_W // 2
C_W = MIX_W // 2
ATT_W = MIX_W // 2
CHUNK = 128
A_GROUPS = A_W // CHUNK
A_GROUP_W = A_W // A_GROUPS
CONV_W = 3
POOL_WINDOWS = (2, 4, 8, 16)
C_GROUPS = len(POOL_WINDOWS)
C_GROUP_W = C_W // C_GROUPS
POOL_HIST = max(POOL_WINDOWS) - 1
HEAD_DIM = 64
N_HEADS = ATT_W // HEAD_DIM
IDX_HEADS = 8
IDX_DIM = 64
TOPK_MAX = 256
Q_BLOCK = 128
ROPE_THETA = 500000.0
D_FF = ((8 * D_MODEL // 3 + 127) // 128) * 128
N_EVEN = (DEPTH + 1) // 2
N_ODD = DEPTH // 2
ALPHA = (2.0 * DEPTH) ** 0.25
BETA = (8.0 * DEPTH) ** -0.25
LN_EPS = 1e-5
ATT_SCALE = HEAD_DIM ** -0.5

E_U = 0
E_V = E_U + A_W
E_B = E_V + A_W
E_C = E_B + B_W
E_H = E_C + B_W
EVEN_COLS = E_H + B_W
O_P = 0
O_Q = O_P + C_W
O_K = O_Q + ATT_W
O_V = O_K + ATT_W
O_QI = O_V + ATT_W
O_KI = O_QI + IDX_HEADS * IDX_DIM
O_WI = O_KI + IDX_DIM
ODD_COLS = O_WI + IDX_HEADS

kernel_name = 'hybrid_gmlp_conv_pool_dsa_step'

def layer_norm(x, g, b):
    xf = x.astype(jnp.float32)
    mu = jnp.mean(xf, axis=-1, keepdims=True)
    var = jnp.mean(jnp.square(xf - mu), axis=-1, keepdims=True)
    y = (xf - mu) * lax.rsqrt(var + LN_EPS)
    return (y * g.astype(jnp.float32) + b.astype(jnp.float32)).astype(x.dtype)

def causal_dwconv(ext, w):
    t = ext.shape[1] - (CONV_W - 1)
    out = ext[:, CONV_W - 1:] * w[CONV_W - 1]
    for j in range(CONV_W - 1):
        out = out + ext[:, j:j + t] * w[j]
    return out

def partial_rope(x, pos):
    d = x.shape[-1]
    rot = d // 4
    half = rot // 2
    inv = jnp.power(jnp.float32(ROPE_THETA), -jnp.arange(half, dtype=jnp.float32) * 2.0 / rot)
    ang = pos.astype(jnp.float32)[:, None] * inv[None, :]
    cos = jnp.cos(ang)[None, :, None, :]
    sin = jnp.sin(ang)[None, :, None, :]
    x1 = x[..., :half].astype(jnp.float32)
    x2 = x[..., half:rot].astype(jnp.float32)
    r1 = (x1 * cos - x2 * sin).astype(x.dtype)
    r2 = (x2 * cos + x1 * sin).astype(x.dtype)
    return jnp.concatenate([r1, r2, x[..., rot:]], axis=-1)

def chunk_spatial_gate(u, v, w_s, b_s):
    n, t, _ = v.shape
    n_ch = -(-t // CHUNK)
    pad = n_ch * CHUNK - t
    vp = jnp.pad(v, ((0, 0), (0, pad), (0, 0))).reshape(n, n_ch, CHUNK, A_GROUPS, A_GROUP_W)
    mask = jnp.tril(jnp.ones((CHUNK, CHUNK), dtype=bool))
    w_c = jnp.where(mask[None], w_s, jnp.zeros_like(w_s))
    mix = jnp.einsum('gts,bnsgc->bntgc', w_c, vp) + b_s.T[:, :, None]
    mix = mix.reshape(n, n_ch * CHUNK, A_W)[:, :t]
    return u * mix

def multiscale_pool(ext, pos):
    t = pos.shape[0]
    csum = jnp.cumsum(ext.astype(jnp.float32), axis=1)
    cs = jnp.concatenate([jnp.zeros_like(csum[:, :1]), csum], axis=1)
    end = cs[:, POOL_HIST + 1:]
    outs = []
    for g, w in enumerate(POOL_WINDOWS):
        sl = slice(g * C_GROUP_W, (g + 1) * C_GROUP_W)
        start = cs[:, POOL_HIST + 1 - w:POOL_HIST + 1 - w + t, sl]
        cnt = jnp.minimum(w, pos + 1).astype(jnp.float32)[None, :, None]
        outs.append((end[..., sl] - start) / cnt)
    mean = jnp.concatenate(outs, axis=-1)
    return (mean - ext[:, POOL_HIST:].astype(jnp.float32)).astype(ext.dtype)

def index_select(qi, wi, ki_all, pos_q, k_sel):
    dots = jax.nn.relu(jnp.einsum('nthd,nsd->nths', qi, ki_all))
    score = jnp.einsum('nth,nths->nts', wi, dots).astype(jnp.float32)
    admissible = jnp.arange(ki_all.shape[1])[None, :] <= pos_q[:, None]
    score = jnp.where(admissible[None], score, -jnp.inf)
    _, idx = lax.top_k(score, k_sel)
    return idx

def sparse_attend(q, ks, vs, idx, pos_q):
    logits = jnp.einsum('nthd,ntkhd->nthk', q, ks).astype(jnp.float32) * ATT_SCALE
    valid = (idx <= pos_q[None, :, None])[:, :, None, :]
    p = jax.nn.softmax(jnp.where(valid, logits, -jnp.inf), axis=-1).astype(q.dtype)
    return jnp.einsum('nthk,ntkhd->nthd', p, vs)

def dsa_prompt(q, k, v, qi, ki, wi):
    n, s = q.shape[:2]
    k_sel = min(TOPK_MAX, s // 4)
    nb = s // Q_BLOCK
    nidx = jnp.arange(n)[:, None, None]

    def block(args):
        qb, qib, wib, start = args
        pos_q = start + jnp.arange(Q_BLOCK, dtype=jnp.int32)
        idx = index_select(qib, wib, ki, pos_q, k_sel)
        return sparse_attend(qb, k[nidx, idx], v[nidx, idx], idx, pos_q)

    to_blocks = lambda a: a.reshape(n, nb, Q_BLOCK, *a.shape[2:]).swapaxes(0, 1)
    starts = jnp.arange(nb, dtype=jnp.int32) * Q_BLOCK
    out = lax.map(block, (to_blocks(q), to_blocks(qi), to_blocks(wi), starts))
    return out.swapaxes(0, 1).reshape(n, s, N_HEADS, HEAD_DIM)

def dsa_sample(q, k, v, qi, ki, wi, *, layer, cache_k, cache_v, cache_kidx, page_table):
    n, t = q.shape[:2]
    past_len = page_table.shape[1] * PAGE_SIZE
    k_sel = min(TOPK_MAX, (past_len + t) // 4)
    ki_past = cache_kidx[layer, page_table].reshape(n, past_len, IDX_DIM)
    ki_all = jnp.concatenate([ki_past, ki], axis=1)
    pos_q = past_len + jnp.arange(t, dtype=jnp.int32)
    idx = index_select(qi, wi, ki_all, pos_q, k_sel)
    nidx = jnp.arange(n)[:, None, None]
    in_past = (idx < past_len)[..., None, None]
    pidx = jnp.minimum(idx, past_len - 1)
    phys = page_table[nidx, pidx // PAGE_SIZE]
    off = pidx % PAGE_SIZE
    nnew = jnp.clip(idx - past_len, 0, t - 1)
    ks = jnp.where(in_past, cache_k[layer, phys, off], k[nidx, nnew])
    vs = jnp.where(in_past, cache_v[layer, phys, off], v[nidx, nnew])
    return sparse_attend(q, ks, vs, idx, pos_q)

def even_mixer(x, conv_hist, w_in, a_ln_g, a_ln_b, a_ws, a_bs, b_conv_w, w_out):
    h = x @ w_in
    u = jax.nn.gelu(h[..., E_U:E_V])
    v = layer_norm(jax.nn.gelu(h[..., E_V:E_B]), a_ln_g, a_ln_b)
    a_out = chunk_spatial_gate(u, v, a_ws, a_bs)
    ext = jnp.concatenate([conv_hist, h[..., E_C:E_H] * h[..., E_H:EVEN_COLS]], axis=1)
    b_out = h[..., E_B:E_C] * causal_dwconv(ext, b_conv_w)
    y = jnp.concatenate([a_out, b_out], axis=-1) @ w_out
    return y, v, ext[:, -(CONV_W - 1):]

def odd_mixer(x, pool_hist, pos, attn_fn, w_in, c_w, c_scale, w_out):
    n, t, _ = x.shape
    h = x @ w_in
    q = partial_rope(h[..., O_Q:O_K].reshape(n, t, N_HEADS, HEAD_DIM), pos)
    k = partial_rope(h[..., O_K:O_V].reshape(n, t, N_HEADS, HEAD_DIM), pos)
    v = h[..., O_V:O_QI].reshape(n, t, N_HEADS, HEAD_DIM)
    qi = partial_rope(h[..., O_QI:O_KI].reshape(n, t, IDX_HEADS, IDX_DIM), pos)
    ki = partial_rope(h[..., O_KI:O_WI][:, :, None, :], pos)[:, :, 0]
    wi = h[..., O_WI:ODD_COLS]
    ext = jnp.concatenate([pool_hist, h[..., O_P:O_Q]], axis=1)
    pooled = multiscale_pool(ext, pos).reshape(n, t, C_GROUPS, C_GROUP_W)
    c_out = jnp.einsum('ntgc,gcd->ntgd', pooled, c_w).reshape(n, t, C_W) * c_scale
    att = attn_fn(q, k, v, qi, ki, wi).reshape(n, t, ATT_W)
    y = jnp.concatenate([c_out, att], axis=-1) @ w_out
    return y, ext[:, -POOL_HIST:], k, v, ki

def conv_ffn(x, hist, w_up, conv_w, conv_b, w_down):
    hu = x @ w_up
    ext = jnp.concatenate([hist, hu], axis=1)
    hc = causal_dwconv(ext, conv_w) + conv_b
    y = (jax.nn.silu(hc[..., :D_FF]) * hc[..., D_FF:]) @ w_down
    return y, ext[:, -(CONV_W - 1):]

def setup_inputs(seed: int = 0) -> dict:
    key = jax.random.key(seed)
    ks = jax.random.split(key, 32)
    n_pages = PAST_LEN // PAGE_SIZE
    n_pool = (5 * DEC_BATCH * n_pages) // 4
    nrm = lambda k, shape, s=1.0: s * jax.random.normal(k, shape, jnp.float32)
    perm = jax.random.permutation(ks[0], n_pool)
    page_table = perm[:DEC_BATCH * n_pages].reshape(DEC_BATCH, n_pages).astype(jnp.int32)
    return {
        'x_prompt': nrm(ks[1], (BATCH, SEQ, D_MODEL)),
        'x_sample': nrm(ks[2], (DEC_BATCH, DEC_SEQ, D_MODEL)),
        'state_b_conv': nrm(ks[3], (N_EVEN, DEC_BATCH, CONV_W - 1, B_W)),
        'state_c_pool': nrm(ks[4], (N_ODD, DEC_BATCH, POOL_HIST, C_W)),
        'cache_k': nrm(ks[5], (N_ODD, n_pool, PAGE_SIZE, N_HEADS, HEAD_DIM)),
        'cache_v': nrm(ks[6], (N_ODD, n_pool, PAGE_SIZE, N_HEADS, HEAD_DIM)),
        'cache_kidx': nrm(ks[7], (N_ODD, n_pool, PAGE_SIZE, IDX_DIM)),
        'state_ffn_conv': nrm(ks[8], (DEPTH, DEC_BATCH, CONV_W - 1, 2 * D_FF)),
        'page_table': page_table,
        'w_in_even': nrm(ks[9], (N_EVEN, D_MODEL, EVEN_COLS), D_MODEL ** -0.5),
        'a_ln_g': 1.0 + nrm(ks[10], (N_EVEN, A_W), 0.1),
        'a_ln_b': nrm(ks[11], (N_EVEN, A_W), 0.1),
        'a_ws': nrm(ks[12], (N_EVEN, A_GROUPS, CHUNK, CHUNK), CHUNK ** -0.5),
        'a_bs': 1.0 + nrm(ks[13], (N_EVEN, A_GROUPS, CHUNK), 0.1),
        'b_conv_w': nrm(ks[14], (N_EVEN, CONV_W, B_W), CONV_W ** -0.5),
        'w_out_even': nrm(ks[15], (N_EVEN, A_W + B_W, D_MODEL), BETA * (A_W + B_W) ** -0.5),
        'w_in_odd': nrm(ks[16], (N_ODD, D_MODEL, ODD_COLS), D_MODEL ** -0.5),
        'c_w': nrm(ks[17], (N_ODD, C_GROUPS, C_GROUP_W, C_GROUP_W), C_GROUP_W ** -0.5),
        'c_scale': 1.0 + nrm(ks[18], (N_ODD, C_W), 0.1),
        'w_out_odd': nrm(ks[19], (N_ODD, C_W + ATT_W, D_MODEL), BETA * (C_W + ATT_W) ** -0.5),
        'ln_mix_g': 1.0 + nrm(ks[20], (DEPTH, D_MODEL), 0.1),
        'ln_mix_b': nrm(ks[21], (DEPTH, D_MODEL), 0.1),
        'ffn_w_up': nrm(ks[22], (DEPTH, D_MODEL, 2 * D_FF), D_MODEL ** -0.5),
        'ffn_conv_w': nrm(ks[23], (DEPTH, CONV_W, 2 * D_FF), CONV_W ** -0.5),
        'ffn_conv_b': nrm(ks[24], (DEPTH, 2 * D_FF), 0.02),
        'ffn_w_down': nrm(ks[25], (DEPTH, D_FF, D_MODEL), BETA * D_FF ** -0.5),
        'ln_ffn_g': 1.0 + nrm(ks[26], (DEPTH, D_MODEL), 0.1),
        'ln_ffn_b': nrm(ks[27], (DEPTH, D_MODEL), 0.1),
    }

def reference(x_prompt, x_sample, state_b_conv, state_c_pool, cache_k, cache_v, cache_kidx,
              state_ffn_conv, page_table, w_in_even, a_ln_g, a_ln_b, a_ws, a_bs, b_conv_w,
              w_out_even, w_in_odd, c_w, c_scale, w_out_odd, ln_mix_g, ln_mix_b, ffn_w_up,
              ffn_conv_w, ffn_conv_b, ffn_w_down, ln_ffn_g, ln_ffn_b):
    xp, xs = x_prompt, x_sample
    n_p, seq = xp.shape[:2]
    n_s, t_s = xs.shape[:2]
    pos_p = jnp.arange(seq, dtype=jnp.int32)
    pos_s = PAST_LEN + jnp.arange(t_s, dtype=jnp.int32)
    a_v_s, b_p, b_s, c_p, c_s = [], [], [], [], []
    k_p, v_p, ki_p, k_s, v_s, ki_s = [], [], [], [], [], []
    f_p, f_s = [], []
    for layer in range(DEPTH):
        if layer % 2 == 0:
            e = layer // 2
            wts = (w_in_even[e], a_ln_g[e], a_ln_b[e], a_ws[e], a_bs[e], b_conv_w[e], w_out_even[e])
            yp, _, bp = even_mixer(xp, jnp.zeros((n_p, CONV_W - 1, B_W), xp.dtype), *wts)
            ys, av, bs = even_mixer(xs, state_b_conv[e], *wts)
            a_v_s.append(av)
            b_p.append(bp)
            b_s.append(bs)
        else:
            o = layer // 2
            wts = (w_in_odd[o], c_w[o], c_scale[o], w_out_odd[o])
            yp, cp, kp, vp, kip = odd_mixer(xp, jnp.zeros((n_p, POOL_HIST, C_W), xp.dtype),
                                            pos_p, dsa_prompt, *wts)
            attn_s = functools.partial(dsa_sample, layer=o, cache_k=cache_k, cache_v=cache_v,
                                       cache_kidx=cache_kidx, page_table=page_table)
            ys, cs, kss, vss, kis = odd_mixer(xs, state_c_pool[o], pos_s, attn_s, *wts)
            c_p.append(cp)
            c_s.append(cs)
            k_p.append(kp)
            v_p.append(vp)
            ki_p.append(kip)
            k_s.append(kss)
            v_s.append(vss)
            ki_s.append(kis)
        xp = layer_norm(ALPHA * xp + yp, ln_mix_g[layer], ln_mix_b[layer])
        xs = layer_norm(ALPHA * xs + ys, ln_mix_g[layer], ln_mix_b[layer])
        fw = (ffn_w_up[layer], ffn_conv_w[layer], ffn_conv_b[layer], ffn_w_down[layer])
        fp, hp = conv_ffn(xp, jnp.zeros((n_p, CONV_W - 1, 2 * D_FF), xp.dtype), *fw)
        fs, hs = conv_ffn(xs, state_ffn_conv[layer], *fw)
        f_p.append(hp)
        f_s.append(hs)
        xp = layer_norm(ALPHA * xp + fp, ln_ffn_g[layer], ln_ffn_b[layer])
        xs = layer_norm(ALPHA * xs + fs, ln_ffn_g[layer], ln_ffn_b[layer])
    return (xp, xs, jnp.stack(a_v_s), jnp.stack(b_p), jnp.stack(b_s), jnp.stack(c_p), jnp.stack(c_s),
            jnp.stack(k_p), jnp.stack(v_p), jnp.stack(ki_p), jnp.stack(k_s), jnp.stack(v_s), jnp.stack(ki_s),
            jnp.stack(f_p), jnp.stack(f_s))


_drawn_inputs = setup_inputs


def setup_inputs(seed=0):
    import zlib

    import numpy as np

    out = dict(_drawn_inputs(seed))
    spreads = {}
    factors = {'a_bs': 3.134, 'c_scale': 2.808, 'ffn_conv_b': 6.36}
    for name, (base, spread) in spreads.items():
        noise = np.random.default_rng([zlib.crc32(name.encode()), seed]).standard_normal(out[name].shape)
        drawn = base * np.exp(spread * noise) if base else spread * noise
        out[name] = __import__('jax').numpy.asarray(drawn.astype(out[name].dtype))
    for name, factor in factors.items():
        out[name] = (out[name] * factor).astype(out[name].dtype)
    return out
```

```python
from contextlib import ExitStack

import concourse.bass as bass
from concourse import mybir

ALU = mybir.AluOpType
ACT = mybir.ActivationFunctionType
AXX = mybir.AxisListType.X
F32 = mybir.dt.float32
F32R = mybir.dt.float32r
BF16 = mybir.dt.bfloat16
I32 = mybir.dt.int32
U32 = mybir.dt.uint32

P = 128
NP = 1024
SEQS, DEC = 8, 4
NS = SEQS * DEC
NT = NP + NS
TC, TW = 3, 352
D = 1024
KD = D // P
FC = 22
HEADS, HD = 8, 64
IDX = 64
PAGES, PAGE = 4, 128
PAST = PAGES * PAGE
POOLED = 40
TOPK_P, TOPK_S = 256, 129
HIST = 2
EXTW = HIST + NP + SEQS * (HIST + DEC)
CW = EXTW - HIST
PH = 15
PEXT = PH + NP + SEQS * (PH + DEC)
ALPHA = 4.0 ** 0.25
EPS = 1e-5
BLOCKS = (4, 6, 6, 6)
SK = PAST + NS

IN0, OUT0 = 0, 20
UP0 = OUT0 + KD
FFN_SLABS = 2 * FC + len(BLOCKS) * KD
IN1 = UP0 + FFN_SLABS
OUT1 = IN1 + 22
UP1 = OUT1 + KD
SLABS = UP1 + FFN_SLABS

TAKEN = -3.4e38
BARRED = -3.0e38
FAR = -1.0e30


def build(nc, io):
    with ExitStack() as ctx:
        def sem(name):
            return ctx.enter_context(nc.semaphore(name))

        top = [1152]

        def at(name, shape, dt, offset):
            return nc.alloc_sbuf_tensor_at(name, shape, dt, offset=offset)

        def size(shape, dt):
            n = 2 if dt == BF16 else 4
            for s in shape[1:]:
                n *= s
            return (n + 31) // 32 * 32

        def fixed(name, shape, dt):
            t = at(name, shape, dt, top[0])
            top[0] += size(shape, dt)
            return t

        def region(start, *tensors):
            out = []
            for name, shape, dt in tensors:
                out.append(at(name, shape, dt, start))
                start += size(shape, dt)
            return out, start

        x_off = top[0]
        XH = fixed("XH", [P, KD, NT], F32R)
        xl_off = top[0]
        XL = fixed("XL", [P, KD, NT], F32R)
        z_off = top[0]
        Z = fixed("Z", [P, KD, NT], F32)
        RAW = [fixed(f"RAW{j}", [P, KD, P], F32) for j in range(2)]
        WH = [fixed(f"WH{j}", [P, KD, P], F32R) for j in range(2)]
        WL = [fixed(f"WL{j}", [P, KD, P], F32R) for j in range(2)]
        ident = fixed("ident", [P, P], F32)
        onesd = fixed("onesd", [P, P], F32)
        lnp = fixed("lnp", [P, 4, 2, KD], F32)
        epst = fixed("epst", [P, 1], F32)
        wtok = fixed("wtok", [P, 9, HEADS], F32)
        G = top[0]
        END = nc.sbuf_usable_end
        ROW = NT * 4
        T6 = G + 16 * ROW
        W6 = (EXTW * 4 + 31) // 32 * 32
        PAREA = T6 + 6 * W6

        MH = at("MH", [P, KD, NT], F32R, G)
        ML = at("ML", [P, KD, NT], F32R, G + 8 * ROW)
        gv = [at(f"gv{j}", [P, NT], F32, G + j * ROW) for j in range(2)]
        (lng, lnb), _ = region(G + 8 * ROW, ("lng", [P, 512], F32), ("lnb", [P, 512], F32))
        U = at("U", [P, 4, NT], F32, z_off)
        vtok = at("vtok", [P, 8, 512], F32, z_off + 4 * ROW)
        cf = at("cf", [P, NT], F32, T6)
        bext = at("bext", [P, EXTW], F32, T6 + W6)
        bcv = at("bcv", [P, CW], F32, T6 + 2 * W6)
        (vst, vmv, vrs, bh), _ = region(T6 + 3 * W6, ("vst", [P, 9, 6], F32), ("vmv", [P, 9, 2], F32),
                                        ("vrs", [P, 9], F32), ("bh", [P, 4, SEQS, 2], F32))
        (vtoks, wsT, bsb, bd, bw, bst), pend = region(
            PAREA, ("vtoks", [NS, 512], F32), ("wsT", [P, 4, P], F32), ("bsb", [P, 4, P], F32),
            ("bd", [NS, 4, NS], F32), ("bw", [P, 4, 3], F32),
            ("bst", [P, 4, 18], F32))
        assert pend <= END, (pend, END)

        NB = max(BLOCKS)
        HH = at("HH", [P, NB, NT], F32R, G)
        HL = at("HL", [P, NB, NT], F32R, G + NB * ROW)
        (fpar, fhist, fst), fend = region(G + 2 * NB * ROW, ("fpar", [P, 2 * FC, 4], F32),
                                          ("fhist", [P, 2 * FC, SEQS, 2], F32), ("fst", [P, 2 * FC, 18], F32))
        assert fend <= T6
        ext = [at(f"ext{j}", [P, EXTW], F32, T6 + j * W6) for j in range(2)]
        cv = [at(f"cv{j}", [P, CW], F32, T6 + (2 + j) * W6) for j in range(2)]
        sg = at("sg", [P, CW], F32, T6 + 4 * W6)
        hf = at("hf", [P, NT], F32, T6 + 5 * W6)

        zs = at("zs", [P, NT], F32, T6 + 2 * W6)
        zq = at("zq", [P, NT], F32, T6 + 3 * W6)
        sq = at("sq", [P, NT], F32, T6 + 4 * W6)
        mean = at("mean", [P, NT], F32, T6)
        msq = at("msq", [P, NT], F32, T6 + W6)
        rstd = at("rstd", [P, NT], F32, T6 + 5 * W6)

        (Q, K, VT, VS, KI), qi_off = region(
            G, ("Q", [P, 4, NT], F32), ("K", [P, 4, NT], F32), ("VT", [P, 8, 512], F32),
            ("VS", [NS, 512], F32), ("KI", [P, NT], F32))
        QI = at("QI", [P, 4, NT], F32, qi_off)
        E0 = qi_off + 4 * ROW
        (RC, RS, qf0, qf1, sh, cw, csc, icnt), eend = region(
            E0, ("RC", [P, NT], F32), ("RS", [P, NT], F32), ("qf0", [P, NT], F32), ("qf1", [P, NT], F32),
            ("sh", [P, NT], F32), ("cw", [P, 4, P], F32), ("csc", [P, 4], F32), ("icnt", [P, 4, 16], F32))
        assert eend <= END, (eend, END)
        qf = [qf0, qf1]
        (pe0, pe1, pe2), pe_end = region(E0, *[(f"pe{j}", [P, PEXT], F32) for j in range(3)])
        assert pe_end <= E0 + 5 * ROW
        (phist, pst), _ = region(z_off + 4 * ROW, ("phist", [P, 4, SEQS, PH], F32),
                                 ("pst", [P, 4, 9, PH], F32))
        (MB, SC, R0, R1), ie = region(E0, ("MB", [P, 36 * P], BF16), ("SC", [P, NP], F32),
                                      ("R0", [P, NP], F32), ("R1", [P, NP], F32))
        (m8, identb, rep, nmx, psm, prc), ie = region(
            E0 + 9216 + 4 * 4096, ("m8", [P, 8], F32), ("identb", [P, P], BF16), ("rep", [NS, SEQS, NS], F32),
            ("nmx", [P, 2], F32), ("psm", [P, 2], F32), ("prc", [P, 2], F32))
        atts = at("atts", [P, 4, NS], F32, qi_off + 16384)
        assert ie <= END, (ie, END)
        RR = [R0, R1]
        PR = [at(f"PR{j}", [P, NP], F32, E0 + 9216 + j * 4096) for j in range(2)]
        PT = [at(f"PT{j}", [P, 8, P], F32, E0 + 9216 + (2 + j) * 4096) for j in range(2)]
        (kix0, kix1, ra, rb, ssc, sbias, iota, QIB, hsum, cmask, wrow, sidx, sidf, s8), se = region(
            x_off + 4 * ROW, ("kix0", [P, PAST], F32), ("kix1", [P, PAST], F32), ("ra", [P, SK], F32),
            ("rb", [P, SK], F32), ("ssc", [NS, SK], F32), ("sbias", [NS, SK], F32), ("iota", [NS, SK], F32),
            ("QIB", [P, SEQS, NS], F32), ("hsum", [P, 2, NS], F32), ("cmask", [NS, NS], F32),
            ("wrow", [P, 2], F32), ("sidx", [NS, 8], U32), ("sidf", [NS, 1], F32), ("s8", [NS, 8], F32))
        assert se <= x_off + 8 * ROW, se - x_off - 8 * ROW
        kix, rab = [kix0, kix1], [ra, rb]
        KP = [at("KP0", [P, 4, PAST], F32, xl_off + 4 * ROW), at("KP1", [P, 4, PAST], F32, qi_off)]
        VP = [at("VP0", [P, PAGES, 512], F32, xl_off + 4 * ROW + 8192), at("VP1", [P, PAGES, 512], F32, qi_off + 8192)]
        (QB, sp_, spt, smx, ssm, src), _ = region(
            E0 + 9216, ("QB", [P, 4, SEQS, NS], F32), ("sp", [P, SK], F32), ("spt", [P, 5, NS], F32),
            ("smx", [P, 2], F32), ("ssm", [P, 2], F32), ("srcp", [P, 2], F32))
        ptab = at("ptab", [1, SEQS * PAGES], I32, xl_off + 4 * ROW + 16384)

        PS = ctx.enter_context(nc.psum_tensor("PS", [P, 8, 512], F32))

        def bank_set(j):
            return PS[:, 3 * j:3 * j + 3, 0:TW]

        def turn_bank(f):
            return PS[:, 6 + f % 2, :]

        wis = nc.dram_tensor("wi_rows", (SEQS, HEADS, DEC), F32, kind="Internal").ap()

        loaded = [sem("slab_loaded0"), sem("slab_loaded1")]
        w_hi, w_lo = sem("slab_high_split"), sem("slab_rest_split")
        mm_done = sem("slab_multiplied")
        evac_done = [sem("banks_emptied0"), sem("banks_emptied1")]
        consts_in, mix_in, x_in = sem("consts_in"), sem("mixer_params_in"), sem("x_in")
        x_hi, x_lo = sem("x_high"), sem("x_rest")
        turned, turn_evac = sem("turned"), sem("turned_emptied")
        vstat, vagg, vsd, vln, vnorm = (sem(n) for n in ("v_stats", "v_aggregated", "v_deviation", "v_ln_step", "v_normed"))
        masked = sem("gate_weights_masked")
        gate_f, mix_hi, mix_lo = sem("mix_rows"), sem("mix_high"), sem("mix_rest")
        bhist, btap, bconv, bstd = sem("b_history"), sem("b_tap"), sem("b_conv"), sem("b_state")
        z_pre, sq_done, zs_done, zq_done = (sem(n) for n in ("z_input", "z_squared", "z_summed", "squares_summed"))
        ln_mean, ln_sq, ln_a, ln_var, ln_sd, ln_rstd, ln_sub, ln_d, ln_z = (
            sem("ln_" + n) for n in ("mean", "meansq", "copies", "var", "dev", "rstd", "centred", "scaled", "out"))
        fpar_in, ext_hist, tap, conv_done, st_done, silu_done, hmul, h_hi, h_lo = (
            sem("ffn_" + n) for n in ("params_in", "history", "tap", "conv", "state", "silu", "hidden", "hidden_high", "hidden_rest"))
        out_done = sem("outputs_written")
        fst_out = sem("ffn_state_written")
        rope_in, l1_in, phist_in, phist_set, pwin, pooled, pst_set, pst_out = (
            sem(n) for n in ("rope_tables_in", "l1_params_in", "pool_history_in", "pool_history_set", "pool_window",
                             "pooled", "pool_state_set", "pool_state_written"))
        pool_zero = sem("pool_row_cleared")
        shuf, shufs, rcos, roped = (sem(n) for n in ("rope_partner", "rope_sine", "rope_cosine", "rope_done"))
        cmm, c_hi, cevac = sem("c_multiplied"), sem("c_high"), sem("c_rest")
        wi_out, wi_in, wt_set = sem("wi_rows_out"), sem("wi_rows_in"), sem("wi_turned")
        sconst_in, qib_zero, qib_set, pt_in = (sem(n) for n in ("sample_consts_in", "qib_cleared", "qib_set", "page_table_in"))
        kix_in = [sem("index_pages_in0"), sem("index_pages_in1")]
        sdot, srelu, ssum, ssc_set, stop_, sidx_set, sb_set = (
            sem("s_" + n) for n in ("dots", "relu", "head_sums", "scores", "top", "last", "bias"))
        dot_mm, dot_relu, sc_acc, sc_barred, top_, mb_set, mb_early = (
            sem("i_" + n) for n in ("dots", "relu", "scores", "barred", "top", "bias", "causal_bias"))
        kv_in = [sem("pages_in0"), sem("pages_in1")]
        qb_zero, qb_set = sem("qb_cleared"), sem("qb_set")
        slg, smax, sexp, ssump, snorm, stp, ste, spv, satt = (
            sem("sa_" + n) for n in ("logits", "max", "exp", "rsum", "probs", "turned", "probs_turned", "values", "out"))
        lg, amax, aexp, asum, anorm, atp, ate, apv, ao_hi, ao_lo = (
            sem("pa_" + n) for n in ("logits", "max", "exp", "rsum", "probs", "turned", "probs_turned", "values", "high", "rest"))
        kv_out = sem("kv_written")

        block = ctx.enter_context(nc.Block())

        def val(i, per, base):
            return base if i is None else i * per + base

        def wait_emptied(eng, n, i=None, per=0):
            eng.wait_ge(evac_done[n % 2], val(i, per // 2, n // 2 + 2))

        def three(ap):
            return ap.rearrange("p (c t) -> p c t", c=TC)

        def row_of(t, index):
            return t[:, bass.ds(index, 1), :].rearrange("p a t -> p (a t)")

        def sample_cols(row, first, width, n):
            a = first + NP
            return row[:, a:a + SEQS * width].rearrange("p (s w) -> p s w", s=SEQS)[:, :, width - n:width]

        def parts(row, hist=0):
            return [row[:, hist:hist + 2 * TW].rearrange("p (c t) -> p c t", c=2),
                    row[:, hist + 2 * TW:hist + NP],
                    sample_cols(row, hist, hist + DEC, DEC)]

        def bank_parts(j):
            bank = bank_set(j)
            return [bank[:, 0:2, :], bank[:, 2, 0:NP - 2 * TW],
                    bank[:, 2, NP - 2 * TW:TW].rearrange("p (s q) -> p s q", s=SEQS)]

        def pair(p, n, rows=P):
            return PS[0:rows, 2 * p:2 * p + 2, :].rearrange("p b t -> p (b t)")[:, 0:n]

        def mask_cols(b):
            return slice(P * b * (b + 1) // 2, P * (b + 1) * (b + 2) // 2)

        @block.sync
        def _(sp):
            sp.dma_start(RAW[0][:, :, :], io["slabs"][0]).then_inc(loaded[0], 16)
            sp.dma_start(RAW[1][:, :, :], io["slabs"][1]).then_inc(loaded[1], 16)

            def stream(first, last):
                with sp.Fori(0, (last - first) // 2) as i:
                    for j in range(2):
                        sp.wait_ge(w_hi, i * 2 + (first + j - 1))
                        sp.wait_ge(w_lo, i * 2 + (first + j - 1))
                        sp.dma_start(RAW[j][:, :, :],
                                     io["slabs"][bass.ds(i * 2 + (first + j), 1)].rearrange("a p k n -> p (a k) n")
                                     ).then_inc(loaded[j], 16)

            stream(2, OUT1 + 2)
            sp.wait_ge(pt_in, 16)

            def page(s, g):
                return sp.value_load(ptab[0:1, bass.ds(s * PAGES + g, 1)], min_val=0, max_val=POOLED - 1)

            def index_pages(i, s):
                for g in range(PAGES):
                    pg = page(val(i, 2, s), g)
                    sp.dma_start(kix[s % 2][:, g * PAGE:(g + 1) * PAGE],
                                 io["kidx"][bass.ds(pg, 1)].rearrange("a p s -> p (a s)")).then_inc(kix_in[s % 2], 16)

            for s in range(2):
                index_pages(None, s)
            with sp.Fori(0, SEQS // 2 - 1) as i:
                for j in range(2):
                    sp.wait_ge(sdot, i * 2 + (j + 1))
                    index_pages(i, 2 + j)

            def kv_pages(i, s):
                for g in range(PAGES):
                    pg = page(val(i, 2, s), g)
                    sp.dma_start(KP[s % 2][:, :, g * PAGE:(g + 1) * PAGE],
                                 io["ck"][bass.ds(pg, 1)].rearrange("a p c s -> p (a c) s")).then_inc(kv_in[s % 2], 16)
                    sp.dma_start(VP[s % 2][:, g, :],
                                 io["cv"][bass.ds(pg, 1)].rearrange("a p c -> p (a c)")).then_inc(kv_in[s % 2], 16)

            sp.wait_ge(cevac, 4)
            kv_pages(None, 0)
            sp.wait_ge(dot_mm, 48)
            kv_pages(None, 1)
            with sp.Fori(0, SEQS // 2 - 1) as i:
                for j in range(2):
                    sp.wait_ge(spv, i * 2 + (j + 1))
                    kv_pages(i, 2 + j)
            stream(OUT1 + 2, SLABS)

        @block.tensor
        def _(pe):
            def slab(n, kc, hi, lo, i=None, per=0, order=None, wait_k=None):
                j = n % 2
                pe.wait_ge(w_lo, val(i, per, n + 1))
                pe.wait_ge(evac_done[j], val(i, per // 2, n // 2 + 1))
                ks = list(order or range(kc))
                for k in ks:
                    if wait_k and k in wait_k:
                        pe.wait_ge(*wait_k[k])
                    first, last = k == ks[0], k == ks[-1]
                    for c in range(TC):
                        o = bank_set(j)[:, c, :]
                        pe.matmul(o, WH[j][:, k, :], hi[:, k, c * TW:(c + 1) * TW], start=first, stop=False)
                        pe.matmul(o, WH[j][:, k, :], lo[:, k, c * TW:(c + 1) * TW], start=False, stop=False)
                    for c in range(TC):
                        mm = pe.matmul(bank_set(j)[:, c, :], WL[j][:, k, :], hi[:, k, c * TW:(c + 1) * TW],
                                       start=False, stop=last)
                mm.then_inc(mm_done, 1)

            def slabs(first, count, kc, hi, lo, order=None):
                with pe.Fori(0, count // 2) as i:
                    for j in range(2):
                        slab(first + j, kc, hi, lo, i, 2, order)

            def turn(row, f, i=None, per=0):
                for part in range(3):
                    pe.wait_ge(turn_evac, val(i, per, f + part + 1))
                    for b in range(4 if part < 2 else 1):
                        t = part * 4 + b
                        w = P if t < 8 else NS
                        mm = pe.transpose(turn_bank(f + part)[0:w, b * P:(b + 1) * P], row[:, t * P:t * P + w], ident[:, :])
                    mm.then_inc(turned, 1)

            def turned_slabs(first, f, rows):
                with pe.Fori(0, 2) as i:
                    for j in range(2):
                        slab(first + j, KD, XH, XL, i, 2)
                    for j in range(2):
                        wait_emptied(pe, first + j, i, 2)
                        turn(rows[j], f + 3 * j, i, 6)

            def norm_sums(l, n):
                pe.wait_ge(zs_done, 9 * l)
                wait_emptied(pe, n - 2)
                wait_emptied(pe, n - 1)
                for c in range(TC):
                    mm = pe.matmul(bank_set(0)[:, c, :], onesd[:, :], zs[:, c * TW:(c + 1) * TW], start=True, stop=True)
                mm.then_inc(ln_mean, 1)
                pe.wait_ge(zq_done, 9 * l)
                for c in range(TC):
                    mm = pe.matmul(bank_set(1)[:, c, :], onesd[:, :], zq[:, c * TW:(c + 1) * TW], start=True, stop=True)
                mm.then_inc(ln_sq, 1)

            def ffn(first, layer):
                n, chunks = first, layer * FC
                for nb in BLOCKS:
                    slabs(n, 2 * nb, KD, XH, XL)
                    n += 2 * nb
                    chunks += nb
                    slab(n, nb, HH, HL, wait_k={0: (h_lo, chunks - 2), nb - 2: (h_lo, chunks - 1), nb - 1: (h_lo, chunks)})
                    slab(n + 1, nb, HH, HL)
                    slabs(n + 2, KD - 2, nb, HH, HL)
                    n += KD

            pe.wait_ge(x_lo, KD)
            pe.wait_ge(consts_in, 16)
            turned_slabs(0, 0, gv)
            slabs(4, 4, KD, XH, XL)
            pe.wait_ge(vnorm, 9)
            pe.wait_ge(masked, 2)
            for g in range(4):
                for part in range(3):
                    f = 12 + 3 * g + part
                    pe.wait_ge(turn_evac, f + 1)
                    o = turn_bank(f)
                    for b in range(4 if part < 2 else 1):
                        if part < 2:
                            mm = pe.matmul(o[:, b * P:(b + 1) * P], vtok[:, part * 4 + b, g * P:(g + 1) * P],
                                           wsT[:, g, :], start=True, stop=True)
                        else:
                            mm = pe.matmul(o[:, 0:NS], vtoks[:, g * P:(g + 1) * P], bd[:, g, :], start=True, stop=True)
                    mm.then_inc(turned, 1)
            slabs(8, 12, KD, XH, XL)
            pe.wait_ge(mix_lo, KD)
            slabs(OUT0, KD, KD, MH, ML, order=[4, 5, 6, 7, 0, 1, 2, 3])
            norm_sums(1, UP0)
            pe.wait_ge(x_lo, 2 * KD)
            ffn(UP0, 0)
            norm_sums(2, IN1)
            pe.wait_ge(x_lo, 3 * KD)
            slabs(IN1, 4, KD, XH, XL)
            turned_slabs(IN1 + 4, 24, qf)
            slabs(IN1 + 8, 14, KD, XH, XL)
            wait_emptied(pe, OUT1 - 1)
            pe.wait_ge(turn_evac, 37)
            for t in range(8):
                mm = pe.transpose(turn_bank(36)[:, t * HEADS:(t + 1) * HEADS], qf[1][0:HEADS, t * P:(t + 1) * P],
                                  ident[0:HEADS, 0:HEADS])
            mm.then_inc(turned, 1)
            pe.wait_ge(l1_in, 48)
            wait_emptied(pe, OUT1 - 2)
            for g in range(4):
                if g >= 2:
                    pe.wait_ge(cevac, g - 1)
                else:
                    pe.wait_ge(pooled, 4)
                for c in range(TC):
                    mm = pe.matmul(bank_set(g % 2)[:, c, :], cw[:, g, :], Z[:, g, c * TW:(c + 1) * TW], start=True, stop=True)
                mm.then_inc(cmm, 1)
            pe.wait_ge(cevac, 4)
            pe.wait_ge(qib_set, 8)
            pe.wait_ge(sconst_in, 64)
            for s in range(SEQS):
                pe.wait_ge(kix_in[s % 2], 64 * (s // 2 + 1))
                o = PS[32 * (s % 4):32 * (s % 4) + 32, :, :]
                g = 2 * (s // 4)
                pe.matmul(o[:, g, :], QIB[:, s, :], kix[s % 2][:, :], start=True, stop=True)
                pe.matmul(o[:, g + 1, 0:NS], QIB[:, s, :], KI[:, NP:NT], start=True, stop=True).then_inc(sdot, 1)
            pe.wait_ge(srelu, 2)
            for half, cols in ((4, slice(0, PAST)), (5, slice(PAST, SK))):
                for g in range(2):
                    mm = pe.matmul(PS[0:NS, half, 0:cols.stop - cols.start], hsum[:, g, :], rab[g][:, cols],
                                   start=(g == 0), stop=(g == 1))
            mm.then_inc(ssum, 1)
            for t in range(48):
                b, h = 2 + t // 8, t % 8
                n = P * (b + 1)
                if t >= 2:
                    pe.wait_ge(dot_relu, t - 1)
                half = slice(64 * (h % 2), 64 * (h % 2) + 64)
                for a in range(0, n, 512):
                    w = min(512, n - a)
                    mm = pe.matmul(PS[:, 2 * (t % 2) + a // 512, 0:w], QI[half, h // 2, b * P:(b + 1) * P],
                                   KI[half, a:a + w], start=True, stop=True)
                mm.then_inc(dot_mm, 1)
            pe.wait_ge(dot_relu, 48)
            pe.wait_ge(qb_set, 8)
            pe.wait_ge(sb_set, 2)
            for s in range(SEQS):
                pe.wait_ge(kv_in[s % 2], 128 * (s // 2 + 1))
                if s >= 2:
                    pe.wait_ge(sexp, s - 1)
                lo, hi_ = PS[0:NS, 2 * (s % 2), :], PS[0:NS, 2 * (s % 2) + 1, 0:NS]
                for o, keys, bias in ((lo, lambda c: KP[s % 2][:, c, :], sbias[:, 0:PAST]),
                                      (hi_, lambda c: K[:, c, NP:NT], sbias[:, PAST:SK])):
                    for c in range(4):
                        pe.matmul(o, QB[:, c, s, :], keys(c), start=(c == 0), stop=False)
                    mm = pe.matmul(o, rep[:, s, :], bias, start=False, stop=True)
                mm.then_inc(slg, 1)
                pe.wait_ge(snorm, s + 1)
                for t in range(5):
                    w = P if t < 4 else NS
                    mm = pe.transpose(PS[0:w, 4, t * NS:(t + 1) * NS], sp_[0:NS, t * P:t * P + w], ident[0:NS, 0:NS])
                mm.then_inc(stp, 1)
                pe.wait_ge(ste, 2 * (s + 1))
                if s >= 1:
                    pe.wait_ge(satt, 2 * s)
                for c in range(4):
                    o = PS[:, 5, 8 * c:8 * c + 8]
                    for t in range(4):
                        pe.matmul(o, VP[s % 2][:, t, c * P:(c + 1) * P], spt[:, t, 8 * c:8 * c + 8],
                                  start=(t == 0), stop=False)
                    mm = pe.matmul(o, VS[:, c * P:(c + 1) * P], spt[0:NS, 4, 8 * c:8 * c + 8], start=False, stop=True)
                mm.then_inc(spv, 1)
            pe.wait_ge(mb_set, 6)
            pe.wait_ge(mb_early, 2)

            def logits(e):
                b, h = e // 8, e % 8
                n = P * (b + 1)
                half = slice(64 * (h % 2), 64 * (h % 2) + 64)
                if e >= 2:
                    pe.wait_ge(aexp, e - 1)
                else:
                    pe.wait_ge(sexp, SEQS)
                for a in range(0, n, 512):
                    w = min(512, n - a)
                    o = PS[:, 2 * (e % 2) + a // 512, 0:w]
                    pe.matmul(o, Q[half, h // 2, b * P:(b + 1) * P], K[half, h // 2, a:a + w], start=True, stop=False)
                    m = mask_cols(b)
                    mm = pe.matmul(o, identb[:, :], MB[:, m.start + a:m.start + a + w], start=False, stop=True)
                mm.then_inc(lg, 1)

            logits(0)
            for e in range(64):
                b, h = e // 8, e % 8
                if e < 63:
                    logits(e + 1)
                pe.wait_ge(anorm, e + 1)
                if e >= 1:
                    pe.wait_ge(ate, e)
                for t in range(b + 1):
                    mm = pe.transpose(PS[:, 4 + t // 4, (t % 4) * P:(t % 4 + 1) * P], PR[e % 2][:, t * P:(t + 1) * P],
                                      ident[:, :])
                mm.then_inc(atp, 1)
                pe.wait_ge(ate, e + 1)
                if e >= 4 and e % 2 == 0:
                    pe.wait_ge(ao_lo, e // 2 - 1)
                o = PS[64 * (h % 2):64 * (h % 2) + 64, 6 + (e // 2) % 2, 0:P]
                for t in range(b + 1):
                    mm = pe.matmul(o, VT[:, t, h * HD:(h + 1) * HD], PT[e % 2][:, t, :], start=(t == 0), stop=(t == b))
                mm.then_inc(apv, 1)
            pe.wait_ge(ao_lo, 32 + 4)
            slabs(OUT1, KD, KD, XH, XL)
            norm_sums(3, UP1)
            pe.wait_ge(x_lo, 4 * KD)
            ffn(UP1, 1)
            norm_sums(4, SLABS)

        @block.scalar
        def _(act):
            act.dma_start(Z[:, :, :], io["xT"]).then_inc(x_in, 16)
            act.dma_start(ident[:, :], io["ident"]).then_inc(consts_in, 16)
            for dst, name in ((lng[:, :], "lng"), (lnb[:, :], "lnb"), (wsT[:, :, :], "wsT"), (bd[:, :, :], "bd"),
                              (bsb[:, :, :], "bsb"), (bw[:, :, :], "bw"), (bh[:, :, :, :], "bh"), (lnp[:, :, :, :], "lnp")):
                act.dma_start(dst, io[name]).then_inc(mix_in, 16)

            def split_high(n, i=None, per=0):
                j = n % 2
                act.wait_ge(loaded[j], val(i, per * 8, 16 * (n // 2 + 1)))
                act.activation(WH[j][:, :, :], RAW[j][:, :, :], ACT.Copy).then_inc(w_hi, 1)

            act.wait_ge(x_in, 16)
            for k in range(KD):
                act.activation(XH[:, k, :], Z[:, k, :], ACT.Copy).then_inc(x_hi, 1)
            split_high(0)
            split_high(1)

            def copied_slabs(first, count, rows, func=ACT.Copy, scale=1.0, free=None):
                with act.Fori(0, count // 2) as i:
                    for j in range(2):
                        act.wait_ge(mm_done, i * 2 + (first + j + 1))
                        if free:
                            act.wait_ge(*free(i, j))
                        act.activation(three(rows(i, j)), bank_set((first + j) % 2), func, scale=scale).then_inc(
                            evac_done[(first + j) % 2], 1)
                        split_high(first + j + 2, i, 2)

            copied_slabs(0, 4, lambda i, j: gv[j][:, :], ACT.Gelu_apprx_tanh)
            act.wait_ge(x_lo, KD)
            copied_slabs(4, 4, lambda i, j: row_of(U, i * 2 + j), ACT.Gelu_apprx_tanh)
            act.wait_ge(vagg, 9)
            act.activation(vrs[:, 0:8], vmv[:, 0:8, 1], ACT.Sqrt, bias=epst[:, :]).then_inc(vsd, 1)
            act.activation(vrs[0:NS, 8:9], vmv[0:NS, 8, 1:2], ACT.Sqrt, bias=epst[0:NS, :]).then_inc(vsd, 1)

            for g in range(4):
                act.wait_ge(gate_f, g + 1)
                act.activation(MH[:, g, :], cf[:, :], ACT.Copy).then_inc(mix_hi, 1)
            act.wait_ge(vnorm, 9)
            act.dma_start(io["o_av"], vtoks[:, :]).then_inc(out_done, 16)
            for jj in range(4):
                n = 8 + 3 * jj
                act.wait_ge(mm_done, n + 1)
                act.wait_ge(mix_lo, 4 + jj)
                act.activation(three(cf[:, :]), bank_set(n % 2), ACT.Copy).then_inc(evac_done[n % 2], 1)
                split_high(n + 2)
                for d in (1, 2):
                    act.wait_ge(mm_done, n + d + 1)
                    split_high(n + d + 2)
                wait_emptied(act, n + 2)
                act.activation(MH[:, 4 + jj, :], cf[:, :], ACT.Copy).then_inc(mix_hi, 1)
            act.wait_ge(bstd, 5)
            act.dma_start(io["o_bst"], bst[:, :, :]).then_inc(out_done, 16)

            def squares(l, first):
                def step(i, m, more=True):
                    act.wait_ge(mm_done, val(i, 2, first + m + 1))
                    if more:
                        split_high(first + m + 2, i, 2)
                    wait_emptied(act, first + m, i, 2)
                    act.wait_ge(zq_done, val(i, 2, 9 * (l - 1) + m + 1))
                    act.activation(sq[:, :], row_of(Z, val(i, 2, m)), ACT.Square).then_inc(sq_done, 1)

                more = first + KD < SLABS
                with act.Fori(0, KD // 2 if more else KD // 2 - 1) as i:
                    for j in range(2):
                        step(i, j)
                if not more:
                    step(None, KD - 2, False)
                    step(None, KD - 1, False)

            def norm(l, last=False):
                act.wait_ge(ln_mean, l)
                act.activation(three(mean[:, :]), bank_set(0), ACT.Copy).then_inc(ln_a, 1)
                act.activation(three(msq[:, :]), bank_set(0), ACT.Square).then_inc(ln_a, 1)
                act.wait_ge(ln_var, 2 * l)
                act.activation(rstd[:, :], msq[:, :], ACT.Sqrt, bias=epst[:, :]).then_inc(ln_sd, 1)
                with act.Fori(0, KD) as m:
                    row = row_of(Z, m)
                    act.wait_ge(ln_d, m + (KD * (l - 1) + 1))
                    act.activation(row, row, ACT.Identity, scale=lnp[:, l - 1, 0, bass.ds(m, 1)],
                                   bias=lnp[:, l - 1, 1, bass.ds(m, 1)]).then_inc(ln_z, 1)
                    if not last:
                        act.wait_ge(ln_z, m + (KD * (l - 1) + 1))
                        act.activation(row_of(XH, m), row, ACT.Copy).then_inc(x_hi, 1)

            def ffn(first, layer):
                act.wait_ge(mm_done, first)
                act.dma_start(fpar[:, :, :], io["fpar"][layer]).then_inc(fpar_in, 16)
                act.dma_start(fhist[:, :, :, :], io["fhist"][layer]).then_inc(fpar_in, 16)
                norm(2 * layer + 1)
                n, u, q = first, layer * 2 * FC, layer * FC
                for bi, nb in enumerate(BLOCKS):
                    with act.Fori(0, nb // 2) as i:
                        for pp in range(2):
                            for j in range(2):
                                s = 2 * pp + j
                                act.wait_ge(mm_done, i * 4 + (n + s + 1))
                                act.wait_ge(conv_done, i * 4 + (u + s + 1))
                                act.wait_ge(st_done, i * 4 + (u + s + 1))
                                for dst, src_ in zip(parts(ext[j], HIST), bank_parts(j)):
                                    ins = act.activation(dst, src_, ACT.Copy)
                                ins.then_inc(evac_done[j], 1)
                                split_high(n + s + 2, i, 4)
                                if j == 0:
                                    act.wait_ge(conv_done, i * 4 + (u + s + 3))
                                    act.activation(sg[:, :], cv[0][:, :], ACT.Silu).then_inc(silu_done, 1)
                                else:
                                    act.wait_ge(hmul, i * 2 + (q + pp + 1))
                                    act.activation(row_of(HH, i * 2 + pp), hf[:, :], ACT.Copy).then_inc(h_hi, 1)
                    n += 2 * nb
                    u += 2 * nb
                    q += nb
                    if bi < len(BLOCKS) - 1:
                        with act.Fori(0, KD // 2) as i:
                            for j in range(2):
                                act.wait_ge(mm_done, i * 2 + (n + j + 1))
                                split_high(n + j + 2, i, 2)
                    else:
                        squares(2 * layer + 2, n)
                    n += KD
                act.wait_ge(st_done, u + 2)
                act.dma_start(io["o_fst"][layer], fst[:, :, :]).then_inc(fst_out, 16)

            def write_y(l):
                act.wait_ge(ln_z, KD * l)
                act.dma_start(io["o_y"], Z[:, :, :]).then_inc(out_done, 16)
                act.wait_ge(out_done, 48)

            squares(1, OUT0)
            ffn(UP0, 0)
            act.wait_ge(fst_out, 16)
            norm(2)
            act.wait_ge(x_lo, 3 * KD)
            act.dma_start(phist[:, :, :, :], io["phist"]).then_inc(phist_in, 16)
            act.dma_start(cw[:, :, :], io["cw"]).then_inc(l1_in, 16)
            act.dma_start(csc[:, :], io["csc"]).then_inc(l1_in, 16)
            act.dma_start(icnt[:, :, :], io["icnt"]).then_inc(l1_in, 16)
            for g in range(4):
                n = IN1 + g
                act.wait_ge(mm_done, n + 1)
                if g == 0:
                    act.wait_ge(pool_zero, 1)
                else:
                    act.wait_ge(pooled, g)
                    act.wait_ge(pst_set, g)
                for dst, src_ in zip(parts(pe0, PH), bank_parts(n % 2)):
                    ins = act.activation(dst, src_, ACT.Copy)
                ins.then_inc(evac_done[n % 2], 1)
                split_high(n + 2)
            act.wait_ge(pst_set, 4)
            act.dma_start(io["o_pst"], pst[:, :, :, :]).then_inc(pst_out, 16)
            act.wait_ge(pooled, 4)
            act.dma_start(RC[:, :], io["rc"]).then_inc(rope_in, 16)
            act.dma_start(RS[:, :], io["rs"]).then_inc(rope_in, 16)
            copied_slabs(IN1 + 4, 4, lambda i, j: qf[j][:, :])

            def roped_slabs(first, count, scale=1.0):
                r = first - IN1 - 8
                copied_slabs(first, count, lambda i, j: qf[j][:, :], scale=scale, free=lambda i, j: (roped, i * 2 + (r + j + 1)))

            roped_slabs(IN1 + 8, 4, HD ** -0.5)
            roped_slabs(IN1 + 12, 8)
            for n in (IN1 + 20, IN1 + 21):
                act.wait_ge(mm_done, n + 1)
                act.wait_ge(roped, n - IN1 - 8 + 1)
                act.activation(three(qf[n % 2][:, :]), bank_set(n % 2), ACT.Copy).then_inc(evac_done[n % 2], 1)
                split_high(n + 2)
            wait_emptied(act, OUT1 - 1)
            act.dma_start(wis.rearrange("s h q -> h s q"), qf[1][0:HEADS, NP:NT].rearrange("p (s q) -> p s q", s=SEQS)).then_inc(wi_out, 16)
            act.wait_ge(roped, 15)
            act.dma_start(io["o_k"], K[:, :, :]).then_inc(kv_out, 16)
            act.dma_start(io["o_ki"], KI[0:IDX, :]).then_inc(kv_out, 16)
            act.dma_start(io["o_v"], VT[:, :, :]).then_inc(kv_out, 16)
            act.dma_start(io["o_vs"], VS[:, :]).then_inc(kv_out, 16)
            for g in range(4):
                act.wait_ge(cmm, g + 1)
                act.wait_ge(z_pre, KD * 2 + g + 1)
                act.activation(three(XH[:, g, :]), bank_set(g % 2), ACT.Copy, scale=csc[:, g:g + 1]).then_inc(c_hi, 1)
            act.wait_ge(z_pre, KD * 3)
            act.dma_start(ptab[:, :], io["ptab"]).then_inc(pt_in, 16)
            for dst, name in ((iota, "iota"), (cmask, "cmask")):
                act.dma_start(dst[:, :], io[name]).then_inc(sconst_in, 16)
            act.dma_start(hsum[:, :, :], io["hsum"]).then_inc(sconst_in, 16)
            act.dma_start(rep[:, :, :], io["rep"]).then_inc(sconst_in, 16)
            act.dma_start(identb[:, :], io["identb"]).then_inc(wt_set, 16)
            act.wait_ge(wi_out, 16)
            for g in range(2):
                act.dma_start(wrow[:, g:g + 1], wis[4 * g:4 * g + 4].rearrange("s h (q a) -> (s h q) a", a=1)).then_inc(wi_in, 16)
            for t in range(48):
                n = P * (3 + t // 8)
                act.wait_ge(dot_mm, t + 1)
                if t >= 2:
                    act.wait_ge(sc_acc, t - 1)
                act.activation(RR[t % 2][:, 0:n], pair(t % 2, n), ACT.Relu).then_inc(dot_relu, 1)
            for s in range(SEQS):
                act.wait_ge(smax, s + 1)
                if s >= 1:
                    act.wait_ge(stp, s)
                act.activation(sp_[0:NS, :], pair(s % 2, SK, NS), ACT.Exp, bias=smx[0:NS, s % 2:s % 2 + 1],
                               accum_out=ssm[0:NS, s % 2:s % 2 + 1]).then_inc(sexp, 1)
            for e in range(65):
                if e < 64:
                    n = P * (e // 8 + 1)
                    act.wait_ge(amax, e + 1)
                    if e >= 2:
                        act.wait_ge(atp, e - 1)
                    elif e == 0:
                        act.wait_ge(spv, SEQS)
                    act.activation(PR[e % 2][:, 0:n], pair(e % 2, n), ACT.Exp, bias=nmx[:, e % 2:e % 2 + 1],
                                   accum_out=psm[:, e % 2:e % 2 + 1]).then_inc(aexp, 1)
                if e >= 1:
                    d = e - 1
                    b = d // 8
                    act.wait_ge(atp, d + 1)
                    if d >= 2:
                        act.wait_ge(apv, d - 1)
                    act.activation(PT[d % 2][:, 0:b + 1, :], pair(2, P * (b + 1)).rearrange("p (t q) -> p t q", q=P),
                                   ACT.Copy).then_inc(ate, 1)
                    if d % 2 == 1:
                        act.wait_ge(apv, d + 1)
                        c = (d % 8) // 2
                        if d == 1:
                            act.wait_ge(satt, 2 * SEQS)
                        act.activation(XH[:, 4 + c, b * P:(b + 1) * P], PS[:, 6 + (d // 2) % 2, 0:P], ACT.Copy).then_inc(ao_hi, 1)
            for c in range(4):
                act.activation(XH[:, 4 + c, NP:NT], atts[:, c, :], ACT.Copy).then_inc(ao_hi, 1)
            squares(3, OUT1)
            act.wait_ge(pst_out, 16)
            act.wait_ge(kv_out, 64)
            ffn(UP1, 1)
            norm(4, True)
            write_y(4)
            act.wait_ge(fst_out, 32)

        @block.gpsimd
        def _(pool):
            def split_rest(n, i=None, per=0):
                j = n % 2
                pool.wait_ge(w_hi, val(i, per, n + 1))
                pool.tensor_tensor(WL[j][:, :, :], RAW[j][:, :, :], WH[j][:, :, :].bitcast(F32),
                                   ALU.subtract).then_inc(w_lo, 1)

            def split_rests(first, count):
                with pool.Fori(0, count // 2) as i:
                    for j in range(2):
                        split_rest(first + j, i, 2)

            pool.memset(onesd[:, :], 1.0 / D)
            pool.memset(epst[:, :], EPS)
            pool.memset(bext[:, 0:HIST], 0.0).then_inc(bstd, 1)
            split_rest(0)
            split_rest(1)
            pool.wait_ge(mix_in, 128)
            pool.affine_select(out=wsT[:, :, :], in_=wsT[:, :, :], pattern=[[0, 4], [1, P]], compare_op=ALU.is_ge,
                               fill=0.0, base=0, channel_multiplier=-1).then_inc(masked, 1)
            pool.affine_select(out=bd[:, :, :], in_=bd[:, :, :], pattern=[[0, 4], [1, NS]], compare_op=ALU.is_ge,
                               fill=0.0, base=0, channel_multiplier=-1).then_inc(masked, 1)
            split_rests(2, 8)
            for jj in range(4):
                n = 8 + 3 * jj
                pool.wait_ge(bconv, jj + 1)
                pool.tensor_copy(sample_cols(bext, HIST, HIST + DEC, HIST + DEC)[:, :, 0:HIST],
                                 bh[:, jj, :, :]).then_inc(bhist, 1)
                for d in (2, 3):
                    split_rest(n + d)
                wait_emptied(pool, n + 1)
                pool.tensor_copy(bst[:, jj, 0:2], bext[:, NP:NP + 2])
                pool.tensor_copy(bst[:, jj, 2:18].rearrange("p (s q) -> p s q", s=SEQS),
                                 sample_cols(bext, HIST, HIST + DEC, 2)).then_inc(bstd, 1)
                split_rest(n + 4)

            def sums(l, first):
                pool.wait_ge(mm_done, first + 1)
                pool.memset(zs[:, :], 0.0).then_inc(zs_done, 1)
                pool.memset(zq[:, :], 0.0).then_inc(zq_done, 1)

                def step(i, m, more=True):
                    if more:
                        split_rest(first + m + 2, i, 2)
                    wait_emptied(pool, first + m, i, 2)
                    pool.wait_ge(zs_done, val(i, 2, 9 * (l - 1) + m + 1))
                    pool.tensor_tensor(zs[:, :], zs[:, :], row_of(Z, val(i, 2, m)), ALU.add).then_inc(zs_done, 1)
                    pool.wait_ge(sq_done, val(i, 2, KD * (l - 1) + m + 1))
                    pool.wait_ge(zq_done, val(i, 2, 9 * (l - 1) + m + 1))
                    pool.tensor_tensor(zq[:, :], zq[:, :], sq[:, :], ALU.add).then_inc(zq_done, 1)

                more = first + KD < SLABS
                with pool.Fori(0, KD // 2 if more else KD // 2 - 1) as i:
                    for j in range(2):
                        step(i, j)
                if not more:
                    step(None, KD - 2, False)
                    step(None, KD - 1, False)

            def ffn(first, layer):
                n, u = first, layer * 2 * FC
                pool.wait_ge(x_lo, KD * (2 + 2 * layer))
                pool.memset(ext[0][:, 0:HIST], 0.0)
                ins = pool.memset(ext[1][:, 0:HIST], 0.0)
                if layer == 0:
                    ins.then_inc(st_done, 2)
                pool.wait_ge(fpar_in, 32 * (layer + 1))
                for bi, nb in enumerate(BLOCKS):
                    with pool.Fori(0, nb // 2) as i:
                        for s in range(4):
                            j = s % 2
                            local = i * 4 + (u - layer * 2 * FC + s)
                            pool.wait_ge(conv_done, i * 4 + (u + s + 1))
                            pool.tensor_copy(sample_cols(ext[j], HIST, HIST + DEC, HIST + DEC)[:, :, 0:HIST],
                                             fhist[:, bass.ds(local, 1), :, :].rearrange("p a s q -> p (a s) q")
                                             ).then_inc(ext_hist, 1)
                            wait_emptied(pool, n + s, i, 4)
                            kept = row_of(fst, local)
                            pool.tensor_copy(kept[:, 0:2], ext[j][:, NP:NP + 2])
                            pool.tensor_copy(kept[:, 2:18].rearrange("p (s q) -> p s q", s=SEQS),
                                             sample_cols(ext[j], HIST, HIST + DEC, 2)).then_inc(st_done, 1)
                            split_rest(n + s + 2, i, 4)
                    n += 2 * nb
                    u += 2 * nb
                    if bi < len(BLOCKS) - 1:
                        split_rests(n + 2, KD)
                    else:
                        sums(2 * layer + 2, n)
                    n += KD

            sums(1, OUT0)
            ffn(UP0, 0)
            pool.wait_ge(x_lo, 3 * KD)
            pool.memset(pe0[:, 0:PH], 0.0).then_inc(pool_zero, 1)
            pool.wait_ge(phist_in, 16)
            for g in range(4):
                n = IN1 + g
                if g >= 1:
                    pool.wait_ge(pooled, g)
                    pool.wait_ge(pst_set, g)
                pool.tensor_copy(sample_cols(pe0, PH, PH + DEC, PH + DEC)[:, :, 0:PH], phist[:, g, :, :]).then_inc(phist_set, 1)
                wait_emptied(pool, n)
                pool.wait_ge(phist_set, g + 1)
                pool.tensor_copy(pst[:, g, 0, :], pe0[:, NP:NP + PH])
                pool.tensor_copy(pst[:, g, 1:9, :], sample_cols(pe0, PH, PH + DEC, PH)).then_inc(pst_set, 1)
                split_rest(n + 2)
            split_rests(IN1 + 6, 18)
            pool.wait_ge(z_pre, KD * 3)
            pool.memset(QIB[:, :, :], 0.0).then_inc(qib_zero, 1)
            pool.wait_ge(pst_out, 16)
            pool.wait_ge(turn_evac, 39)
            pool.memset(MB[:, 0:3 * P], 0.0).then_inc(mb_early, 1)
            pool.wait_ge(mb_early, 1)
            for a in (0, 2 * P):
                ins = pool.affine_select(out=MB[:, a:a + P], in_=MB[:, a:a + P], pattern=[[-1, P]], compare_op=ALU.is_ge,
                                         fill=FAR, base=0, channel_multiplier=1)
            ins.then_inc(mb_early, 1)
            for b in range(2, 8):
                pool.wait_ge(sc_acc, 8 * (b - 1))
                diag = SC[:, b * P:(b + 1) * P]
                pool.affine_select(out=diag, in_=diag, pattern=[[-1, P]], compare_op=ALU.is_ge,
                                   fill=BARRED, base=0, channel_multiplier=1).then_inc(sc_barred, 1)
            pool.wait_ge(mb_set, 6)
            pool.memset(QB[:, :, :, :], 0.0).then_inc(qb_zero, 1)
            sums(3, OUT1)
            ffn(UP1, 1)

        @block.vector
        def _(dve):
            dve.memset(nmx[:, 0:1], 0.0).then_inc(evac_done[0], 1)
            dve.memset(nmx[:, 1:2], 0.0).then_inc(evac_done[1], 1)
            dve.memset(prc[:, 0:1], 0.0).then_inc(conv_done, 2)
            dve.memset(psm[:, 0:1], 0.0).then_inc(bconv, 1)
            dve.memset(psm[:, 1:2], 0.0).then_inc(turn_evac, 2)
            dve.memset(prc[:, 1:2], 0.0).then_inc(roped, 2)
            for k in range(KD):
                dve.wait_ge(x_hi, k + 1)
                dve.tensor_tensor(XL[:, k, :], Z[:, k, :], XH[:, k, :].bitcast(F32), ALU.subtract).then_inc(x_lo, 1)

            def turned_rows(f0, blocks, tail):
                with dve.Fori(0, 2) as i:
                    for j in range(2):
                        for part in range(3):
                            f = f0 + 3 * j + part
                            dve.wait_ge(turned, i * 6 + (f + 1))
                            cols = bass.ds(i * 256 + j * P, P)
                            if part < 2:
                                dve.tensor_copy(blocks[:, 4 * part:4 * part + 4, cols],
                                                turn_bank(f).rearrange("p (b c) -> p b c", b=4)).then_inc(turn_evac, 1)
                            else:
                                dve.tensor_copy(tail[:, cols], turn_bank(f)[0:NS, 0:P]).then_inc(turn_evac, 1)

            turned_rows(0, vtok, vtoks)
            dve.wait_ge(turn_evac, 14)

            def vblock(t):
                return (vtok[:, t, :], P) if t < 8 else (vtoks[:, :], NS)

            for t in range(9):
                a, w = vblock(t)
                dve.bn_stats(vst[0:w, t, :], a).then_inc(vstat, 1)
            for t in range(9):
                w = vblock(t)[1]
                dve.wait_ge(vstat, t + 1)
                dve.bn_aggr(vmv[0:w, t, :], vst[0:w, t, :]).then_inc(vagg, 1)
            dve.wait_ge(vsd, 2)
            dve.reciprocal(vrs[:, 0:8], vrs[:, 0:8]).then_inc(vln, 1)
            dve.reciprocal(vrs[0:NS, 8:9], vrs[0:NS, 8:9]).then_inc(vln, 1)
            dve.wait_ge(vln, 2)
            dve.wait_ge(mix_in, 128)
            for t in range(9):
                a, w = vblock(t)
                dve.tensor_scalar(a, a, vmv[0:w, t, 0:1], vrs[0:w, t:t + 1], ALU.subtract, ALU.mult).then_inc(vln, 1)
            for t in range(9):
                a, w = vblock(t)
                dve.wait_ge(vln, 2 + t + 1)
                dve.tensor_tensor(a, a, lng[0:w, :], ALU.mult).then_inc(vln, 1)
            for t in range(9):
                a, w = vblock(t)
                dve.wait_ge(vln, 11 + t + 1)
                dve.tensor_tensor(a, a, lnb[0:w, :], ALU.add).then_inc(vnorm, 1)

            def mix_rest(k):
                dve.wait_ge(mix_hi, k + 1)
                dve.tensor_tensor(ML[:, k, :], cf[:, :], MH[:, k, :].bitcast(F32), ALU.subtract).then_inc(mix_lo, 1)

            for g in range(4):
                if g >= 1:
                    dve.wait_ge(mix_lo, g)
                for part in range(3):
                    f = 12 + 3 * g + part
                    dve.wait_ge(turned, f + 1)
                    if part < 2:
                        o = cf[:, part * 512:(part + 1) * 512].rearrange("p (b t) -> p b t", b=4)
                        dve.tensor_tensor(o, turn_bank(f).rearrange("p (b t) -> p b t", b=4),
                                          bsb[:, g, None, :].to_broadcast([P, 4, P]), ALU.add).then_inc(turn_evac, 1)
                    else:
                        o = cf[:, NP:NT].rearrange("p (s q) -> p s q", s=SEQS)
                        dve.tensor_tensor(o, turn_bank(f)[:, 0:NS].rearrange("p (s q) -> p s q", s=SEQS),
                                          bsb[:, g, None, 0:DEC].to_broadcast([P, SEQS, DEC]), ALU.add).then_inc(turn_evac, 1)
                dve.wait_ge(turn_evac, 2 + f + 1)
                if g == 0:
                    wait_emptied(dve, 6)
                    wait_emptied(dve, 7)
                dve.tensor_tensor(cf[:, :], cf[:, :], U[:, g, :], ALU.mult).then_inc(gate_f, 1)
                mix_rest(g)

            def taps(row, out, w, tap_sem, value, done):
                if len(w) == 4:
                    dve.tensor_scalar(out, row[:, 2:2 + CW], w[2], w[3], ALU.mult, ALU.add).then_inc(tap_sem, 1)
                else:
                    dve.tensor_scalar(out, row[:, 2:2 + CW], w[2], None, ALU.mult).then_inc(tap_sem, 1)
                dve.wait_ge(tap_sem, value(1))
                dve.scalar_tensor_tensor(out, row[:, 0:CW], w[0], out, ALU.mult, ALU.add).then_inc(tap_sem, 1)
                dve.wait_ge(tap_sem, value(2))
                dve.scalar_tensor_tensor(out, row[:, 1:1 + CW], w[1], out, ALU.mult, ALU.add).then_inc(done, 1)

            for jj in range(4):
                n = 8 + 3 * jj
                dve.wait_ge(mm_done, n + 2)
                wait_emptied(dve, n)
                dve.wait_ge(bstd, jj + 1)
                for dst, src_, c in zip(parts(bext, HIST), bank_parts((n + 1) % 2), parts(cf)):
                    ins = dve.tensor_tensor(dst, src_, c, ALU.mult)
                ins.then_inc(evac_done[(n + 1) % 2], 1)
                wait_emptied(dve, n + 1)
                dve.wait_ge(bhist, jj + 1)
                taps(bext, bcv[:, :], [bw[:, jj, t:t + 1] for t in range(3)], btap, lambda k: 2 * jj + k, bconv)
                dve.wait_ge(bconv, jj + 2)
                dve.wait_ge(mm_done, n + 3)
                conv_parts = [bcv[:, 0:2 * TW].rearrange("p (c t) -> p c t", c=2), bcv[:, 2 * TW:NP],
                              sample_cols(bcv, 0, HIST + DEC, DEC)]
                for dst, src_, c in zip(parts(cf), bank_parts(n % 2), conv_parts):
                    ins = dve.tensor_tensor(dst, src_, c, ALU.mult)
                ins.then_inc(evac_done[n % 2], 1)
                mix_rest(4 + jj)

            def projected(first, pres, before=None):
                with dve.Fori(0, KD // 2) as i:
                    for j in range(2):
                        n = first + j
                        z = row_of(Z, i * 2 + j)
                        if pres is not None:
                            dve.tensor_tensor(z, row_of(XH, i * 2 + j).bitcast(F32), row_of(XL, i * 2 + j).bitcast(F32),
                                              ALU.add).then_inc(z_pre, 1)
                            dve.wait_ge(z_pre, i * 2 + (pres + j + 1))
                        dve.wait_ge(mm_done, i * 2 + (n + 1))
                        if pres is not None or before:
                            dve.scalar_tensor_tensor(three(z), three(z), ALPHA, bank_set(j), ALU.mult,
                                                     ALU.add).then_inc(evac_done[j], 1)
                        else:
                            dve.tensor_tensor(three(z), three(z), bank_set(j), ALU.add).then_inc(evac_done[j], 1)

            def norm(l, last=False):
                dve.wait_ge(ln_a, 2 * l)
                dve.wait_ge(ln_sq, l)
                dve.tensor_tensor(three(msq[:, :]), bank_set(1), three(msq[:, :]), ALU.subtract).then_inc(ln_var, 1)
                dve.wait_ge(ln_var, 2 * l - 1)
                dve.tensor_scalar(msq[:, :], msq[:, :], 0.0, None, ALU.max).then_inc(ln_var, 1)
                dve.wait_ge(ln_sd, l)
                dve.reciprocal(rstd[:, :], rstd[:, :]).then_inc(ln_rstd, 1)
                dve.wait_ge(ln_rstd, l)
                k0 = KD * (l - 1)
                with dve.Fori(0, KD // 2) as i:
                    for j in range(2):
                        z = row_of(Z, i * 2 + j)
                        dve.tensor_tensor(z, z, mean[:, :], ALU.subtract).then_inc(ln_sub, 1)
                    for j in range(2):
                        z = row_of(Z, i * 2 + j)
                        dve.wait_ge(ln_sub, i * 2 + (k0 + j + 1))
                        dve.tensor_tensor(z, z, rstd[:, :], ALU.mult).then_inc(ln_d, 1)
                    if not last:
                        for j in range(2):
                            dve.wait_ge(x_hi, i * 2 + (KD * l + j + 1))
                            dve.tensor_tensor(row_of(XL, i * 2 + j), row_of(Z, i * 2 + j),
                                              row_of(XH, i * 2 + j).bitcast(F32), ALU.subtract).then_inc(x_lo, 1)

            def ffn(first, layer):
                n, u, q = first, layer * 2 * FC, layer * FC
                dve.wait_ge(fpar_in, 32 * (layer + 1))
                for bi, nb in enumerate(BLOCKS):
                    with dve.Fori(0, nb // 2) as i:
                        for pp in range(2):
                            for j in range(2):
                                s = 2 * pp + j
                                wait_emptied(dve, n + s, i, 4)
                                dve.wait_ge(ext_hist, i * 4 + (u + s + 1))
                                w = row_of(fpar, i * 4 + (u - layer * 2 * FC + s))
                                taps(ext[j], cv[j][:, :], [w[:, t:t + 1] for t in range(4)], tap,
                                     lambda k: i * 8 + (2 * (u + s) + k), conv_done)
                            pq = i * 2 + (q + pp + 1)
                            dve.wait_ge(silu_done, pq)
                            dve.wait_ge(conv_done, i * 4 + (u + 2 * pp + 1 + 3))
                            dve.tensor_tensor(hf[:, 0:NP], sg[:, 0:NP], cv[1][:, 0:NP], ALU.mult)
                            dve.tensor_tensor(hf[:, NP:NT].rearrange("p (s q) -> p s q", s=SEQS),
                                              sample_cols(sg, 0, HIST + DEC, DEC), sample_cols(cv[1], 0, HIST + DEC, DEC),
                                              ALU.mult).then_inc(hmul, 1)
                            dve.wait_ge(h_hi, pq)
                            dve.tensor_tensor(row_of(HL, i * 2 + pp), hf[:, :], row_of(HH, i * 2 + pp).bitcast(F32),
                                              ALU.subtract).then_inc(h_lo, 1)
                    n += 2 * nb
                    u += 2 * nb
                    q += nb
                    projected(n, KD * (1 + 2 * layer) if bi == 0 else None)
                    n += KD

            projected(OUT0, 0)
            norm(1)
            ffn(UP0, 0)
            norm(2)
            dve.wait_ge(l1_in, 48)
            step = 0
            for g, w in enumerate((2, 4, 8, 16)):
                wait_emptied(dve, IN1 + g)
                dve.wait_ge(phist_set, g + 1)
                a, bufs, width = pe0, [pe1, pe2], 1
                while width < w:
                    o = bufs[0]
                    lo = 2 * width - 1
                    dve.tensor_tensor(o[:, lo:PEXT], a[:, lo:PEXT], a[:, lo - width:PEXT - width], ALU.add).then_inc(pwin, 1)
                    step += 1
                    dve.wait_ge(pwin, step)
                    a, bufs, width = o, bufs[::-1], 2 * width
                dve.scalar_tensor_tensor(Z[:, g, 16:NP], a[:, PH + 16:PH + NP], 1.0 / w, pe0[:, PH + 16:PH + NP],
                                         ALU.mult, ALU.subtract)
                dve.scalar_tensor_tensor(Z[:, g, NP:NT].rearrange("p (s q) -> p s q", s=SEQS),
                                         sample_cols(a, PH, PH + DEC, DEC), 1.0 / w, sample_cols(pe0, PH, PH + DEC, DEC),
                                         ALU.mult, ALU.subtract)
                dve.tensor_tensor(a[:, PH:PH + 16], a[:, PH:PH + 16], icnt[:, g, :], ALU.mult).then_inc(pwin, 1)
                step += 1
                dve.wait_ge(pwin, step)
                dve.tensor_tensor(Z[:, g, 0:16], a[:, PH:PH + 16], pe0[:, PH:PH + 16], ALU.subtract).then_inc(pooled, 1)
            turned_rows(24, VT, VS)

            def rotate(r, j, dst, i=None):
                dve.wait_ge(rope_in, 32)
                dve.wait_ge(roped, val(i, 2, r + 2))
                wait_emptied(dve, IN1 + 8 + r, i, 2)
                dve.tensor_tensor(dst, qf[j][:, :], RC[:, :], ALU.mult).then_inc(rcos, 1)
                dve.stream_shuffle(sh[:, :], qf[j][:, :], [p ^ 8 if p < 16 else p for p in range(32)]).then_inc(shuf, 1)
                dve.wait_ge(shuf, val(i, 2, r + 1))
                dve.tensor_tensor(sh[:, :], sh[:, :], RS[:, :], ALU.mult).then_inc(shufs, 1)
                dve.wait_ge(shufs, val(i, 2, r + 1))
                dve.wait_ge(rcos, val(i, 2, r + 1))
                dve.tensor_tensor(dst, dst, sh[:, :], ALU.add).then_inc(roped, 1)

            for r0, t in ((0, Q), (4, K), (8, QI)):
                with dve.Fori(0, 2) as i:
                    for j in range(2):
                        rotate(r0 + j, j, row_of(t, i * 2 + j), i)
            rotate(12, 0, KI[:, :])
            dve.wait_ge(turned, 37)
            dve.tensor_copy(wtok[:, 0:8, :], turn_bank(36)[:, 0:8 * HEADS].rearrange("p (t h) -> p t h", t=8)).then_inc(turn_evac, 1)
            for g in range(4):
                dve.wait_ge(cmm, g + 1)
                dve.tensor_tensor(Z[:, g, :], XH[:, g, :].bitcast(F32), XL[:, g, :].bitcast(F32), ALU.add).then_inc(z_pre, 1)
                dve.wait_ge(c_hi, g + 1)
                dve.scalar_tensor_tensor(three(XL[:, g, :]), bank_set(g % 2), csc[:, g:g + 1], three(XH[:, g, :].bitcast(F32)),
                                         ALU.mult, ALU.subtract).then_inc(cevac, 1)
            dve.wait_ge(pst_out, 16)
            for g in range(4, 8):
                dve.tensor_tensor(Z[:, g, :], XH[:, g, :].bitcast(F32), XL[:, g, :].bitcast(F32), ALU.add).then_inc(z_pre, 1)

            def blocked(dst, src, cleared, done):
                dve.wait_ge(cleared, 1)
                for h in range(HEADS):
                    half = slice(64 * (h % 2), 64 * (h % 2) + 64)
                    dve.tensor_copy(dst(half, h), src[half, h // 2, NP:NT].rearrange("p (s q) -> p s q", s=SEQS)).then_inc(done, 1)

            blocked(lambda half, h: QIB[half, :, DEC * h:DEC * h + DEC], QI, qib_zero, qib_set)
            dve.wait_ge(wi_in, 32)
            for g in range(2):
                dve.wait_ge(sdot, 4 * (g + 1))
                dve.tensor_scalar(rab[g][:, :], pair(g, SK), 0.0, wrow[:, g:g + 1], ALU.max, ALU.mult).then_inc(srelu, 1)
            dve.wait_ge(ssum, 1)
            dve.wait_ge(sconst_in, 64)
            dve.tensor_copy(ssc[:, 0:PAST], PS[0:NS, 4, :]).then_inc(ssc_set, 1)
            dve.tensor_tensor(ssc[:, PAST:SK], PS[0:NS, 5, 0:NS], cmask[:, :], ALU.add).then_inc(ssc_set, 1)
            dve.wait_ge(ssc_set, 2)
            with dve.Fori(0, TOPK_S // 8) as i:
                dve.max(s8[:, :], ssc[:, :]).then_inc(stop_, 1)
                dve.wait_ge(stop_, 1)
                dve.match_replace(ssc[:, :], s8[:, :], ssc[:, :], TAKEN).then_inc(stop_, 1)
                dve.wait_ge(stop_, 2)
                dve.sem_clear(stop_)
            dve.max(s8[:, :], ssc[:, :]).then_inc(sidx_set, 1)
            dve.wait_ge(sidx_set, 1)
            dve.max_index(sidx[:, :], s8[:, :], ssc[:, :]).then_inc(sidx_set, 1)
            dve.wait_ge(sidx_set, 2)
            dve.tensor_copy(sidf[:, :], sidx[:, 0:1]).then_inc(sidx_set, 1)
            dve.wait_ge(sidx_set, 3)
            dve.tensor_scalar(sbias[:, :], iota[:, :], sidf[:, 0:1], FAR, ALU.not_equal, ALU.mult).then_inc(sb_set, 1)
            dve.wait_ge(sb_set, 1)
            dve.scalar_tensor_tensor(sbias[:, :], ssc[:, :], TAKEN, sbias[:, :], ALU.is_gt, ALU.mult).then_inc(sb_set, 1)
            for t in range(48):
                b, h = 2 + t // 8, t % 8
                n = P * (b + 1)
                dve.wait_ge(dot_relu, t + 1)
                if h == 0:
                    if b > 2:
                        dve.wait_ge(mb_set, b - 2)
                    dve.tensor_scalar(SC[:, 0:n], RR[t % 2][:, 0:n], wtok[:, b, 0:1], None, ALU.mult).then_inc(sc_acc, 1)
                else:
                    dve.wait_ge(sc_acc, t)
                    dve.scalar_tensor_tensor(SC[:, 0:n], RR[t % 2][:, 0:n], wtok[:, b, h:h + 1], SC[:, 0:n],
                                             ALU.mult, ALU.add).then_inc(sc_acc, 1)
                if h == 7:
                    dve.wait_ge(sc_barred, b - 1)
                    with dve.Fori(0, TOPK_P // 8) as i:
                        dve.max(m8[:, :], SC[:, 0:n]).then_inc(top_, 1)
                        dve.wait_ge(top_, 1)
                        dve.match_replace(SC[:, 0:n], m8[:, :], SC[:, 0:n], TAKEN).then_inc(top_, 1)
                        dve.wait_ge(top_, 2)
                        dve.sem_clear(top_)
                    dve.tensor_scalar(MB[:, mask_cols(b)], SC[:, 0:n], TAKEN, FAR, ALU.is_gt, ALU.mult).then_inc(mb_set, 1)
            blocked(lambda half, h: QB[half, h // 2, :, DEC * h:DEC * h + DEC], Q, qb_zero, qb_set)
            for s in range(SEQS):
                j = s % 2
                dve.wait_ge(slg, s + 1)
                dve.tensor_reduce(smx[0:NS, j:j + 1], pair(j, SK, NS), AXX, ALU.max, negate=True).then_inc(smax, 1)
                dve.wait_ge(sexp, s + 1)
                dve.reciprocal(src[0:NS, j:j + 1], ssm[0:NS, j:j + 1]).then_inc(ssump, 1)
                dve.wait_ge(ssump, s + 1)
                dve.tensor_scalar(sp_[0:NS, :], sp_[0:NS, :], src[0:NS, j:j + 1], None, ALU.mult).then_inc(snorm, 1)
                dve.wait_ge(stp, s + 1)
                dve.tensor_copy(spt[:, 0:4, :], PS[:, 4, 0:4 * NS].rearrange("p (t r) -> p t r", t=4)).then_inc(ste, 1)
                dve.tensor_copy(spt[0:NS, 4, :], PS[0:NS, 4, 4 * NS:5 * NS]).then_inc(ste, 1)
                dve.wait_ge(spv, s + 1)
                for hh in range(2):
                    half = slice(64 * hh, 64 * hh + 64)
                    dve.tensor_copy(atts[half, :, DEC * s:DEC * s + DEC],
                                    PS[half, 5, 0:32].rearrange("p (c r) -> p c r", c=4)[:, :, 4 * hh:4 * hh + 4]).then_inc(satt, 1)

            def att_rest(pr):
                dve.wait_ge(ao_hi, pr + 1)
                b, c = pr // 4, pr % 4
                dve.tensor_tensor(XL[:, 4 + c, b * P:(b + 1) * P], PS[:, 6 + pr % 2, 0:P],
                                  XH[:, 4 + c, b * P:(b + 1) * P].bitcast(F32), ALU.subtract).then_inc(ao_lo, 1)

            for e in range(64):
                b, j = e // 8, e % 2
                n = P * (b + 1)
                dve.wait_ge(lg, e + 1)
                dve.tensor_reduce(nmx[:, j:j + 1], pair(j, n), AXX, ALU.max, negate=True).then_inc(amax, 1)
                if e >= 3 and e % 2 == 1:
                    att_rest((e - 3) // 2)
                dve.wait_ge(aexp, e + 1)
                dve.reciprocal(prc[:, j:j + 1], psm[:, j:j + 1]).then_inc(asum, 1)
                dve.wait_ge(asum, e + 1)
                dve.tensor_scalar(PR[j][:, 0:n], PR[j][:, 0:n], prc[:, j:j + 1], None, ALU.mult).then_inc(anorm, 1)
            att_rest(31)
            for c in range(4):
                dve.wait_ge(ao_hi, 32 + c + 1)
                dve.tensor_tensor(XL[:, 4 + c, NP:NT], atts[:, c, :], XH[:, 4 + c, NP:NT].bitcast(F32),
                                  ALU.subtract).then_inc(ao_lo, 1)
            projected(OUT1, None, before=True)
            norm(3)
            ffn(UP1, 1)
            norm(4, True)


def kernel(**inputs):
    import numpy as np
    import concourse.bacc as bacc
    from concourse import mybir as mb
    from concourse.bass_utils import run_bass_kernel_spmd

    a = {k: np.asarray(v) for k, v in inputs.items()}
    f32 = np.float32

    def rows(w, kc):
        s = w.reshape(kc, P, -1, P).transpose(2, 1, 0, 3)
        if kc == KD:
            return s
        out = np.zeros((s.shape[0], P, KD, P), f32)
        out[:, :, :kc] = s
        return out

    def feature_major(x, lead=0):
        c = x.shape[-1]
        y = np.moveaxis(x.reshape(x.shape[:-1] + (c // P, P)), (-1, -2), (0, 1))
        return np.ascontiguousarray(y)

    we = a["w_in_even"][0]
    cols = lambda w, o, n: w[:, o:o + n]
    even = [cols(we, 512, 512), cols(we, 0, 512)]
    for jj in range(4):
        for base in (1536, 2048, 1024):
            even.append(cols(we, base + jj * P, P))
    wo = a["w_in_odd"][0]
    ki = cols(wo, 2560, 64)
    wi = np.zeros((D, P), f32)
    wi[:, :HEADS] = cols(wo, 2624, HEADS)
    odd = [cols(wo, 0, 512), cols(wo, 1536, 512), cols(wo, 512, 512), cols(wo, 1024, 512), cols(wo, 2048, 512), ki, ki, wi]

    def ffn_slabs(layer):
        up, down = a["ffn_w_up"][layer], a["ffn_w_down"][layer]
        out, c = [], 0
        for nb in BLOCKS:
            both = [cols(up, half * FC * P + (c + q) * P, P) for q in range(nb) for half in (0, 1)]
            out.append(rows(np.concatenate(both, 1), KD))
            out.append(rows(down[c * P:(c + nb) * P], nb))
            c += nb
        return out

    slab_list = [rows(np.concatenate(even, 1), KD), rows(a["w_out_even"][0], KD), *ffn_slabs(0),
                 rows(np.concatenate(odd, 1), KD), rows(a["w_out_odd"][0], KD), *ffn_slabs(1)]
    slab_array = np.concatenate(slab_list, 0)
    assert slab_array.shape == (SLABS, P, KD, P)

    x = np.concatenate([a["x_prompt"].reshape(NP, D), a["x_sample"].reshape(NS, D)], 0)
    ws = a["a_ws"][0]
    bd = np.zeros((NS, 4, NS), f32)
    for s in range(SEQS):
        bd[DEC * s:DEC * s + DEC, :, DEC * s:DEC * s + DEC] = ws[:, :DEC, :DEC].transpose(2, 0, 1)
    spread = lambda v: np.ascontiguousarray(np.broadcast_to(v, (P,) + v.shape))
    pairs = lambda w: np.stack([w[..., FC * 0 * P:FC * P], w[..., FC * P:]], -2)

    def ffn_order(v):
        y = v.reshape(v.shape[:-1] + (2, FC, P))
        y = np.moveaxis(y, (-1, -2, -3), (0, 1, 2))
        return np.ascontiguousarray(y.reshape((P, 2 * FC) + y.shape[3:]))

    fpar = np.stack([np.concatenate([ffn_order(a["ffn_conv_w"][l]), ffn_order(a["ffn_conv_b"][l][None])], 2) for l in range(2)])
    fhist = np.stack([ffn_order(a["state_ffn_conv"][l]) for l in range(2)])
    lnp = np.stack([np.stack([feature_major(a[f"ln_{k}_{p}"][l]) for p in "gb"], 1)
                    for l in range(2) for k in ("mix", "ffn")], 1)

    pos = np.concatenate([np.arange(NP), np.tile(PAST + np.arange(DEC), SEQS)]).astype(f32)
    rot, halfr = HD // 4, HD // 8
    inv = np.power(f32(500000.0), -np.arange(halfr, dtype=f32) * f32(2.0) / f32(rot)).astype(f32)
    ang = (pos[None, :] * inv[:, None]).astype(f32)
    rc, rs = np.ones((P, NT), f32), np.zeros((P, NT), f32)
    for h in (0, HD):
        rc[h:h + halfr] = rc[h + halfr:h + rot] = np.cos(ang)
        rs[h:h + halfr], rs[h + halfr:h + rot] = -np.sin(ang), np.sin(ang)
    icnt = spread(np.stack([1.0 / np.minimum(w, np.arange(16) + 1.0) for w in (2, 4, 8, 16)]).astype(f32))
    rep = np.zeros((NS, SEQS, HEADS, DEC), f32)
    hsum = np.zeros((4, HEADS, DEC, 2, SEQS, DEC), f32)
    cmask = np.full((SEQS, DEC, SEQS, DEC), BARRED, f32)
    for s in range(SEQS):
        for q in range(DEC):
            rep[DEC * s + q, s, :, q] = 1.0
            hsum[s % 4, :, q, s // 4, s, q] = 1.0
            cmask[s, q, s, :q + 1] = 0.0
    import ml_dtypes

    ck = a["cache_k"][0].transpose(0, 2, 3, 1).reshape(POOLED, 4, P, PAGE).transpose(0, 2, 1, 3)
    kidx = a["cache_kidx"][0].transpose(0, 2, 1)
    arrays = dict(
        slabs=slab_array, xT=feature_major(x), ident=np.eye(P, dtype=f32), identb=np.eye(P).astype(ml_dtypes.bfloat16),
        lng=spread(a["a_ln_g"][0]), lnb=spread(a["a_ln_b"][0]), wsT=ws.transpose(2, 0, 1), bd=bd,
        bsb=spread(a["a_bs"][0]), bw=feature_major(a["b_conv_w"][0]), bh=feature_major(a["state_b_conv"][0]),
        lnp=lnp, fpar=fpar, fhist=fhist, phist=feature_major(a["state_c_pool"][0]), cw=a["c_w"][0].transpose(1, 0, 2),
        csc=feature_major(a["c_scale"][0]), icnt=icnt, rc=rc, rs=rs, rep=rep.reshape(NS, SEQS, NS),
        hsum=hsum.reshape(P, 2, NS), cmask=cmask.reshape(NS, NS),
        iota=np.ascontiguousarray(np.broadcast_to(np.arange(SK, dtype=f32), (NS, SK))),
        ptab=a["page_table"].reshape(1, -1), ck=ck, cv=a["cache_v"][0].reshape(POOLED, PAGE, 512),
        kidx=np.concatenate([kidx, kidx], 1),
    )
    outs = dict(o_y=(P, KD, NT), o_av=(NS, 512), o_bst=(P, 4, 18), o_pst=(P, 4, 9, PH), o_k=(P, 4, NT), o_ki=(IDX, NT),
                o_v=(P, 8, 512), o_vs=(NS, 512), o_fst=(2, P, 2 * FC, 18))

    nc = bacc.Bacc("TRN2", target_bir_lowering=False, num_devices=1, dynamic_dma_scratch_size=1024)
    io, feed = {}, {}
    for name, v in arrays.items():
        v = np.ascontiguousarray(v)
        feed["in_" + name] = v
        io[name] = nc.dram_tensor("in_" + name, v.shape, mb.dt.from_np(v.dtype), kind="ExternalInput").ap()
    for name, shape in outs.items():
        io[name] = nc.dram_tensor("out_" + name, shape, mb.dt.float32, kind="ExternalOutput").ap()
    build(nc, io)
    got = run_bass_kernel_spmd(nc, [feed], core_ids=[0]).results[0]
    r = {name: np.asarray(got["out_" + name]) for name in outs}

    def positions(y):
        y = y.transpose(2, 1, 0).reshape(y.shape[2], -1)
        return y[:NP], y[NP:]

    yp, ys = positions(r["o_y"])
    kp, ks = positions(r["o_k"])
    kip, kis = r["o_ki"].T[:NP], r["o_ki"].T[NP:]
    vp = r["o_v"].transpose(1, 0, 2).reshape(NP, 512)
    b = r["o_bst"].transpose(2, 1, 0).reshape(18, 512)
    c = r["o_pst"].transpose(2, 3, 1, 0).reshape(9, PH, 512)
    f = r["o_fst"].reshape(2, P, FC, 2, 18).transpose(0, 4, 3, 2, 1).reshape(2, 18, 2 * FC * P)
    C = np.ascontiguousarray
    return (C(yp.reshape(1, NP, D)), C(ys.reshape(SEQS, DEC, D)), C(r["o_av"].reshape(1, SEQS, DEC, 512)),
            C(b[:2].reshape(1, 1, 2, 512)), C(b[2:].reshape(1, SEQS, 2, 512)),
            C(c[:1].reshape(1, 1, PH, 512)), C(c[1:].reshape(1, SEQS, PH, 512)),
            C(kp.reshape(1, 1, NP, HEADS, HD)), C(vp.reshape(1, 1, NP, HEADS, HD)), C(kip.reshape(1, 1, NP, IDX)),
            C(ks.reshape(1, SEQS, DEC, HEADS, HD)), C(r["o_vs"].reshape(1, SEQS, DEC, HEADS, HD)),
            C(kis.reshape(1, SEQS, DEC, IDX)),
            C(f[:, :2].reshape(2, 1, 2, 2 * FC * P)), C(f[:, 2:].reshape(2, SEQS, 2, 2 * FC * P)))
```

```python
from contextlib import ExitStack

import concourse.bass as bass
from concourse import mybir

ALU = mybir.AluOpType
ACT = mybir.ActivationFunctionType
AXX = mybir.AxisListType.X
F32 = mybir.dt.float32
F32R = mybir.dt.float32r
BF16 = mybir.dt.bfloat16
I32 = mybir.dt.int32
U32 = mybir.dt.uint32

P = 128
NP = 1024
SEQS, DEC = 8, 4
NS = SEQS * DEC
NT = NP + NS
TC, TW = 3, 352
D = 1024
KD = D // P
FC = 22
HEADS, HD = 8, 64
IDX = 64
PAGES, PAGE = 4, 128
PAST = PAGES * PAGE
POOLED = 40
TOPK_P, TOPK_S = 256, 129
HIST = 2
EXTW = HIST + NP + SEQS * (HIST + DEC)
CW = EXTW - HIST
PH = 15
PEXT = PH + NP + SEQS * (PH + DEC)
ALPHA = 4.0 ** 0.25
EPS = 1e-5
BLOCKS = (4, 6, 6, 6)
SK = PAST + NS

IN0, OUT0 = 0, 20
UP0 = OUT0 + KD
FFN_SLABS = 2 * FC + len(BLOCKS) * KD
IN1 = UP0 + FFN_SLABS
OUT1 = IN1 + 22
UP1 = OUT1 + KD
SLABS = UP1 + FFN_SLABS

TAKEN = -3.4e38
BARRED = -3.0e38
FAR = -1.0e30


def build(nc, io):
    with ExitStack() as ctx:
        def sem(name):
            return ctx.enter_context(nc.semaphore(name))

        top = [1152]

        def at(name, shape, dt, offset):
            return nc.alloc_sbuf_tensor_at(name, shape, dt, offset=offset)

        def size(shape, dt):
            n = 2 if dt == BF16 else 4
            for s in shape[1:]:
                n *= s
            return (n + 31) // 32 * 32

        def fixed(name, shape, dt):
            t = at(name, shape, dt, top[0])
            top[0] += size(shape, dt)
            return t

        def region(start, *tensors):
            out = []
            for name, shape, dt in tensors:
                out.append(at(name, shape, dt, start))
                start += size(shape, dt)
            return out, start

        x_off = top[0]
        XH = fixed("XH", [P, KD, NT], F32R)
        xl_off = top[0]
        XL = fixed("XL", [P, KD, NT], F32R)
        z_off = top[0]
        Z = fixed("Z", [P, KD, NT], F32)
        raw_off = top[0]
        RAW = [fixed(f"RAW{j}", [P, KD, P], F32) for j in range(2)]
        wh_off = top[0]
        WH = [fixed(f"WH{j}", [P, KD, P], F32R) for j in range(2)]
        WL = [fixed(f"WL{j}", [P, KD, P], F32R) for j in range(2)]
        ident = fixed("ident", [P, P], F32)
        onesd = fixed("onesd", [P, P], F32)
        lnp = fixed("lnp", [P, 4, 2, KD], F32)
        epst = fixed("epst", [P, 1], F32)
        seed = fixed("seed", [P, 6], F32)
        wtok = fixed("wtok", [P, 9, HEADS], F32)
        G = top[0]
        END = nc.sbuf_usable_end
        ROW = NT * 4
        T6 = G + 16 * ROW
        W6 = (EXTW * 4 + 31) // 32 * 32
        PAREA = T6 + 6 * W6

        MH = at("MH", [P, KD, NT], F32R, G)
        ML = at("ML", [P, KD, NT], F32R, G + 8 * ROW)
        gv = [at(f"gv{j}", [P, NT], F32, G + j * ROW) for j in range(2)]
        (lng, lnb), _ = region(G + 8 * ROW, ("lng", [P, 512], F32), ("lnb", [P, 512], F32))
        U = at("U", [P, 4, NT], F32, z_off)
        vtok = at("vtok", [P, 8, 512], F32, z_off + 4 * ROW)
        cf = at("cf", [P, NT], F32, T6)
        bext = at("bext", [P, EXTW], F32, T6 + W6)
        bcv = at("bcv", [P, CW], F32, T6 + 2 * W6)
        (vst, vmv, vrs, bh), _ = region(T6 + 3 * W6, ("vst", [P, 9, 6], F32), ("vmv", [P, 9, 2], F32),
                                        ("vrs", [P, 9], F32), ("bh", [P, 4, SEQS, 2], F32))
        (vtoks, wsT, bsb, bd, bw, bst), pend = region(
            PAREA, ("vtoks", [NS, 512], F32), ("wsT", [P, 4, P], F32), ("bsb", [P, 4, P], F32),
            ("bd", [NS, 4, NS], F32), ("bw", [P, 4, 3], F32),
            ("bst", [P, 4, 18], F32))
        assert pend <= END, (pend, END)

        NB = max(BLOCKS)
        HH = at("HH", [P, NB, NT], F32R, G)
        HL = at("HL", [P, NB, NT], F32R, G + NB * ROW)
        (fpar, fhist, fst), fend = region(G + 2 * NB * ROW, ("fpar", [P, 2 * FC, 4], F32),
                                          ("fhist", [P, 2 * FC, SEQS, 2], F32), ("fst", [P, 2 * FC, 18], F32))
        assert fend <= T6
        ext = [at(f"ext{j}", [P, EXTW], F32, T6 + j * W6) for j in range(2)]
        cv = [at(f"cv{j}", [P, CW], F32, T6 + (2 + j) * W6) for j in range(2)]
        sg = at("sg", [P, CW], F32, T6 + 4 * W6)
        hf = at("hf", [P, NT], F32, T6 + 5 * W6)

        zs = at("zs", [P, NT], F32, T6 + 2 * W6)
        zq = at("zq", [P, NT], F32, T6 + 3 * W6)
        sq = at("sq", [P, NT], F32, T6 + 4 * W6)
        mean = at("mean", [P, NT], F32, T6)
        msq = at("msq", [P, NT], F32, T6 + W6)
        rstd = at("rstd", [P, NT], F32, T6 + 5 * W6)

        (Q, K, VT, VS, KI), qi_off = region(
            G, ("Q", [P, 4, NT], F32), ("K", [P, 4, NT], F32), ("VT", [P, 8, 512], F32),
            ("VS", [NS, 512], F32), ("KI", [P, NT], F32))
        QI = at("QI", [P, 4, NT], F32, qi_off)
        E0 = qi_off + 4 * ROW
        (RC, RS, qf0, qf1, sh, cw, csc, icnt), eend = region(
            E0, ("RC", [P, NT], F32), ("RS", [P, NT], F32), ("qf0", [P, NT], F32), ("qf1", [P, NT], F32),
            ("sh", [P, NT], F32), ("cw", [P, 4, P], F32), ("csc", [P, 4], F32), ("icnt", [P, 4, 16], F32))
        assert eend <= END, (eend, END)
        qf = [qf0, qf1]
        (pe0, pe1, pe2), pe_end = region(E0, *[(f"pe{j}", [P, PEXT], F32) for j in range(3)])
        assert pe_end <= E0 + 5 * ROW
        (phist, pst), _ = region(z_off + 4 * ROW, ("phist", [P, 4, SEQS, PH], F32),
                                 ("pst", [P, 4, 9, PH], F32))
        (MB, SC0, SC1, R0, R1, m8, identb, nmx, psm, prc, atts), ie = region(
            E0, ("MB", [P, 36 * P], BF16), ("SC0", [P, NP], F32), ("SC1", [P, NP], F32), ("R0", [P, NP], F32),
            ("R1", [P, NP], F32), ("m8", [P, 8], F32), ("identb", [P, P], BF16), ("nmx", [P, 2], F32),
            ("psm", [P, 2], F32), ("prc", [P, 2], F32), ("atts", [P, 4, NS], F32))
        assert ie <= END, (ie, END)
        SC, RR = [SC0, SC1], [R0, R1]
        PR = [at(f"PR{j}", [P, NP], F32, wh_off + j * 4096) for j in range(2)]
        PT = [at(f"PT{j}", [P, 8, P], F32, wh_off + (2 + j) * 4096) for j in range(2)]
        QB = at("QB", [P, 4, SEQS, NS], F32, raw_off)
        (sp_, spt, rep), se = region(raw_off + 4096, ("sp", [P, SK], F32), ("spt", [P, 5, NS], F32),
                                     ("rep", [NS, SEQS, NS], F32))
        assert se <= wh_off
        sbias = at("sbias", [NS, SK], F32, wh_off + 3 * 4096)
        (kix0, kix1, ra, rb, ssc, iota, QIB, hsum, cmask, wrow, sidx, sidf, s8), se = region(
            x_off + 4 * ROW, ("kix0", [P, PAST], F32), ("kix1", [P, PAST], F32), ("ra", [P, SK], F32),
            ("rb", [P, SK], F32), ("ssc", [NS, SK], F32), ("iota", [NS, SK], F32),
            ("QIB", [P, SEQS, NS], F32), ("hsum", [P, 2, NS], F32), ("cmask", [NS, NS], F32),
            ("wrow", [P, 2], F32), ("sidx", [NS, 8], U32), ("sidf", [NS, 1], F32), ("s8", [NS, 8], F32))
        assert se <= x_off + 8 * ROW, se - x_off - 8 * ROW
        kix, rab = [kix0, kix1], [ra, rb]
        KP = [at(f"KP{j}", [P, 4, PAST], F32, o + 4 * ROW) for j, o in enumerate((xl_off, x_off))]
        VP = [at(f"VP{j}", [P, PAGES, 512], F32, o + 4 * ROW + 8192) for j, o in enumerate((xl_off, x_off))]
        ptab = at("ptab", [1, SEQS * PAGES], I32, xl_off + 4 * ROW + 16384)

        PS = ctx.enter_context(nc.psum_tensor("PS", [P, 8, 512], F32))

        def bank_set(j):
            return PS[:, 3 * j:3 * j + 3, 0:TW]

        def turn_bank(f):
            return PS[:, 6 + f % 2, :]

        wis = nc.dram_tensor("wi_rows", (SEQS, HEADS, DEC), F32, kind="Internal").ap()

        loaded = [sem("slab_loaded0"), sem("slab_loaded1")]
        w_hi, w_lo = sem("slab_high_split"), sem("slab_rest_split")
        mm_done = sem("slab_multiplied")
        evac_done = [sem("banks_emptied0"), sem("banks_emptied1")]
        consts_in, mix_in, x_in = sem("consts_in"), sem("mixer_params_in"), sem("x_in")
        x_hi, x_lo = sem("x_high"), sem("x_rest")
        turned, turn_evac = sem("turned"), sem("turned_emptied")
        vstat, vagg, vsd, vln, vnorm = (sem(n) for n in ("v_stats", "v_aggregated", "v_deviation", "v_ln_step", "v_normed"))
        masked = sem("gate_weights_masked")
        gate_f, mix_hi, mix_lo = sem("mix_rows"), sem("mix_high"), sem("mix_rest")
        bhist, btap, bconv, bstd = sem("b_history"), sem("b_tap"), sem("b_conv"), sem("b_state")
        z_pre, sq_done, zs_done, zq_done = (sem(n) for n in ("z_input", "z_squared", "z_summed", "squares_summed"))
        ln_mean, ln_sq, ln_a, ln_var, ln_sd, ln_rstd, ln_sub, ln_d, ln_z = (
            sem("ln_" + n) for n in ("mean", "meansq", "copies", "var", "dev", "rstd", "centred", "scaled", "out"))
        fpar_in, ext_hist, tap, conv_done, st_done, silu_done, hmul, h_hi, h_lo = (
            sem("ffn_" + n) for n in ("params_in", "history", "tap", "conv", "state", "silu", "hidden", "hidden_high", "hidden_rest"))
        out_done = sem("outputs_written")
        fst_out = sem("ffn_state_written")
        rope_in, l1_in, phist_in, phist_set, pwin, pooled, pst_set, pst_out = (
            sem(n) for n in ("rope_tables_in", "l1_params_in", "pool_history_in", "pool_history_set", "pool_window",
                             "pooled", "pool_state_set", "pool_state_written"))
        weighted = sem("i_weighted")
        pool_zero = sem("pool_row_cleared")
        shuf, shufs, rcos, roped = (sem(n) for n in ("rope_partner", "rope_sine", "rope_cosine", "rope_done"))
        cmm, c_hi, cevac = sem("c_multiplied"), sem("c_high"), sem("c_rest")
        wi_out, wi_in, wt_set = sem("wi_rows_out"), sem("wi_rows_in"), sem("wi_turned")
        sconst_in, qib_zero, qib_set, pt_in = (sem(n) for n in ("sample_consts_in", "qib_cleared", "qib_set", "page_table_in"))
        kix_in = [sem("index_pages_in0"), sem("index_pages_in1")]
        sdot, srelu, ssum, ssc_set, stop_, sidx_set, sb_set = (
            sem("s_" + n) for n in ("dots", "relu", "head_sums", "scores", "top", "last", "bias"))
        dot_mm, dot_relu, sc_acc, sc_barred, top_, mb_set, mb_early = (
            sem("i_" + n) for n in ("dots", "relu", "scores", "barred", "top", "bias", "causal_bias"))
        k_in = [sem("key_pages_in0"), sem("key_pages_in1")]
        v_in = [sem("value_pages_in0"), sem("value_pages_in1")]
        qb_zero, qb_set = sem("qb_cleared"), sem("qb_set")
        slg, smax, sexp, ssump, snorm, stp, ste, spv, satt = (
            sem("sa_" + n) for n in ("logits", "max", "exp", "rsum", "probs", "turned", "probs_turned", "values", "out"))
        lg, amax, aexp, asum, anorm, atp, ate, apv, ao_hi, ao_lo = (
            sem("pa_" + n) for n in ("logits", "max", "exp", "rsum", "probs", "turned", "probs_turned", "values", "high", "rest"))
        kv_out = sem("kv_written")

        block = ctx.enter_context(nc.Block())

        def val(i, per, base):
            return base if i is None else i * per + base

        def wait_emptied(eng, n, i=None, per=0):
            eng.wait_ge(evac_done[n % 2], val(i, per // 2, n // 2 + 2))

        def three(ap):
            return ap.rearrange("p (c t) -> p c t", c=TC)

        def row_of(t, index):
            return t[:, bass.ds(index, 1), :].rearrange("p a t -> p (a t)")

        def sample_cols(row, first, width, n):
            a = first + NP
            return row[:, a:a + SEQS * width].rearrange("p (s w) -> p s w", s=SEQS)[:, :, width - n:width]

        def parts(row, hist=0):
            return [row[:, hist:hist + 2 * TW].rearrange("p (c t) -> p c t", c=2),
                    row[:, hist + 2 * TW:hist + NP],
                    sample_cols(row, hist, hist + DEC, DEC)]

        def bank_parts(j):
            bank = bank_set(j)
            return [bank[:, 0:2, :], bank[:, 2, 0:NP - 2 * TW],
                    bank[:, 2, NP - 2 * TW:TW].rearrange("p (s q) -> p s q", s=SEQS)]

        def pair(p, n, rows=P):
            return PS[0:rows, 2 * p:2 * p + 2, :].rearrange("p b t -> p (b t)")[:, 0:n]

        def logit_pair(e):
            return e % 2 if e >= 56 else 0

        def mask_cols(b):
            return slice(P * b * (b + 1) // 2, P * (b + 1) * (b + 2) // 2)

        SLOTS = SEQS + 64
        BEST = TOPK_P // 8
        ROUNDS = 6 * BEST
        per_slot = [3] * 8 + [3] * 8 + [2] * 8 + [3] * 8 + [4] * 24 + [1] * 8 + [0] * 9
        start_round = [sum(per_slot[:k]) for k in range(SLOTS + 1)]
        assert start_round[SLOTS] == ROUNDS
        assert all(start_round[SEQS + 8 * b] >= BEST * (b - 1) for b in range(2, 8))

        def slot_dots(k):
            return [t for t in range(8, 48) if k < SLOTS and start_round[k] <= 4 * (t - 8) < start_round[k + 1]]

        @block.sync
        def _(sp):
            sp.dma_start(RAW[0][:, :, :], io["slabs"][0]).then_inc(loaded[0], 16)
            sp.dma_start(RAW[1][:, :, :], io["slabs"][1]).then_inc(loaded[1], 16)

            def stream(first, last):
                with sp.Fori(0, (last - first) // 2) as i:
                    for j in range(2):
                        sp.wait_ge(w_hi, i * 2 + (first + j - 1))
                        sp.wait_ge(w_lo, i * 2 + (first + j - 1))
                        sp.dma_start(RAW[j][:, :, :],
                                     io["slabs"][bass.ds(i * 2 + (first + j), 1)].rearrange("a p k n -> p (a k) n")
                                     ).then_inc(loaded[j], 16)

            stream(2, OUT1)
            sp.wait_ge(pt_in, 16)

            def page_entry(s, g):
                return bass.ds(s * PAGES + g, 1)

            def page(s, g):
                return sp.value_load(ptab[0:1, page_entry(s, g)], min_val=0, max_val=POOLED - 1)

            def index_pages(i, s):
                for g in range(PAGES):
                    pg = page(val(i, 2, s), g)
                    sp.dma_start(kix[s % 2][:, g * PAGE:(g + 1) * PAGE],
                                 io["kidx"][bass.ds(pg, 1)].rearrange("a p s -> p (a s)")).then_inc(kix_in[s % 2], 16)

            for s in range(2):
                index_pages(None, s)
            with sp.Fori(0, SEQS // 2 - 1) as i:
                for j in range(2):
                    sp.wait_ge(sdot, i * 2 + (j + 1))
                    index_pages(i, 2 + j)

            def key_pages(i, s):
                for g in range(PAGES):
                    pg = page(val(i, 2, s), g)
                    sp.dma_start(KP[s % 2][:, :, g * PAGE:(g + 1) * PAGE],
                                 io["ck"][bass.ds(pg, 1)].rearrange("a p c s -> p (a c) s")).then_inc(k_in[s % 2], 16)

            def value_pages(i, s):
                for g in range(PAGES):
                    pg = page(val(i, 2, s), g)
                    sp.dma_start(VP[s % 2][:, g, :],
                                 io["cv"][bass.ds(pg, 1)].rearrange("a p c -> p (a c)")).then_inc(v_in[s % 2], 16)

            key_pages(None, 0)
            value_pages(None, 0)
            sp.wait_ge(sb_set, 2)
            key_pages(None, 1)
            value_pages(None, 1)
            for s in range(2, SEQS):
                sp.wait_ge(slg, s - 1)
                key_pages(None, s)
                sp.wait_ge(spv, s - 1)
                value_pages(None, s)
            sp.wait_ge(spv, SEQS)
            stream(OUT1, SLABS)

        @block.tensor
        def _(pe):
            def slab(n, kc, hi, lo, i=None, per=0, order=None, wait_k=None):
                j = n % 2
                pe.wait_ge(w_lo, val(i, per, n + 1))
                pe.wait_ge(evac_done[j], val(i, per // 2, n // 2 + 1))
                ks = list(order or range(kc))
                for k in ks:
                    if wait_k and k in wait_k:
                        pe.wait_ge(*wait_k[k])
                    first, last = k == ks[0], k == ks[-1]
                    for c in range(TC):
                        o = bank_set(j)[:, c, :]
                        pe.matmul(o, WH[j][:, k, :], hi[:, k, c * TW:(c + 1) * TW], start=first, stop=False)
                        pe.matmul(o, WH[j][:, k, :], lo[:, k, c * TW:(c + 1) * TW], start=False, stop=False)
                    for c in range(TC):
                        mm = pe.matmul(bank_set(j)[:, c, :], WL[j][:, k, :], hi[:, k, c * TW:(c + 1) * TW],
                                       start=False, stop=last)
                mm.then_inc(mm_done, 1)

            def slabs(first, count, kc, hi, lo, order=None):
                with pe.Fori(0, count // 2) as i:
                    for j in range(2):
                        slab(first + j, kc, hi, lo, i, 2, order)

            def turn(row, f, i=None, per=0):
                for part in range(3):
                    pe.wait_ge(turn_evac, val(i, per, f + part + 1))
                    for b in range(4 if part < 2 else 1):
                        t = part * 4 + b
                        w = P if t < 8 else NS
                        mm = pe.transpose(turn_bank(f + part)[0:w, b * P:(b + 1) * P], row[:, t * P:t * P + w], ident[:, :])
                    mm.then_inc(turned, 1)

            def turned_slabs(first, f, rows):
                with pe.Fori(0, 2) as i:
                    for j in range(2):
                        slab(first + j, KD, XH, XL, i, 2)
                    for j in range(2):
                        wait_emptied(pe, first + j, i, 2)
                        turn(rows[j], f + 3 * j, i, 6)

            def norm_sums(l, n):
                pe.wait_ge(zs_done, 9 * l)
                wait_emptied(pe, n - 2)
                wait_emptied(pe, n - 1)
                for c in range(TC):
                    mm = pe.matmul(bank_set(0)[:, c, :], onesd[:, :], zs[:, c * TW:(c + 1) * TW], start=True, stop=True)
                mm.then_inc(ln_mean, 1)
                pe.wait_ge(zq_done, 9 * l)
                for c in range(TC):
                    mm = pe.matmul(bank_set(1)[:, c, :], onesd[:, :], zq[:, c * TW:(c + 1) * TW], start=True, stop=True)
                mm.then_inc(ln_sq, 1)

            def ffn(first, layer):
                n, chunks = first, layer * FC
                for nb in BLOCKS:
                    slabs(n, 2 * nb, KD, XH, XL)
                    n += 2 * nb
                    chunks += nb
                    slab(n, nb, HH, HL, wait_k={0: (h_lo, chunks - 2), nb - 2: (h_lo, chunks - 1), nb - 1: (h_lo, chunks)})
                    slab(n + 1, nb, HH, HL)
                    slabs(n + 2, KD - 2, nb, HH, HL)
                    n += KD

            pe.wait_ge(x_lo, KD)
            pe.wait_ge(consts_in, 16)
            turned_slabs(0, 0, gv)
            slabs(4, 4, KD, XH, XL)
            pe.wait_ge(vnorm, 9)
            pe.wait_ge(masked, 2)
            for g in range(4):
                for part in range(3):
                    f = 12 + 3 * g + part
                    pe.wait_ge(turn_evac, f + 1)
                    o = turn_bank(f)
                    for b in range(4 if part < 2 else 1):
                        if part < 2:
                            mm = pe.matmul(o[:, b * P:(b + 1) * P], vtok[:, part * 4 + b, g * P:(g + 1) * P],
                                           wsT[:, g, :], start=True, stop=True)
                        else:
                            mm = pe.matmul(o[:, 0:NS], vtoks[:, g * P:(g + 1) * P], bd[:, g, :], start=True, stop=True)
                    mm.then_inc(turned, 1)
            slabs(8, 12, KD, XH, XL)
            pe.wait_ge(mix_lo, KD)
            slabs(OUT0, KD, KD, MH, ML, order=[4, 5, 6, 7, 0, 1, 2, 3])
            norm_sums(1, UP0)
            pe.wait_ge(x_lo, 2 * KD)
            ffn(UP0, 0)
            norm_sums(2, IN1)
            pe.wait_ge(x_lo, 3 * KD)
            slabs(IN1, 4, KD, XH, XL)
            turned_slabs(IN1 + 4, 24, qf)
            slabs(IN1 + 8, 14, KD, XH, XL)
            wait_emptied(pe, OUT1 - 1)
            pe.wait_ge(turn_evac, 37)
            for t in range(8):
                mm = pe.transpose(turn_bank(36)[:, t * HEADS:(t + 1) * HEADS], qf[1][0:HEADS, t * P:(t + 1) * P],
                                  ident[0:HEADS, 0:HEADS])
            mm.then_inc(turned, 1)
            pe.wait_ge(l1_in, 48)
            wait_emptied(pe, OUT1 - 2)
            for g in range(4):
                if g >= 2:
                    pe.wait_ge(cevac, g - 1)
                else:
                    pe.wait_ge(pooled, 4)
                for c in range(TC):
                    mm = pe.matmul(bank_set(g % 2)[:, c, :], cw[:, g, :], Z[:, g, c * TW:(c + 1) * TW], start=True, stop=True)
                mm.then_inc(cmm, 1)
            pe.wait_ge(cevac, 4)
            pe.wait_ge(qib_set, 8)
            pe.wait_ge(sconst_in, 64)
            for s in range(SEQS):
                pe.wait_ge(kix_in[s % 2], 64 * (s // 2 + 1))
                o = PS[32 * (s % 4):32 * (s % 4) + 32, :, :]
                g = 2 * (s // 4)
                pe.matmul(o[:, g, :], QIB[:, s, :], kix[s % 2][:, :], start=True, stop=True)
                pe.matmul(o[:, g + 1, 0:NS], QIB[:, s, :], KI[:, NP:NT], start=True, stop=True).then_inc(sdot, 1)
            pe.wait_ge(srelu, 2)
            for half, cols in ((4, slice(0, PAST)), (5, slice(PAST, SK))):
                for g in range(2):
                    mm = pe.matmul(PS[0:NS, half, 0:cols.stop - cols.start], hsum[:, g, :], rab[g][:, cols],
                                   start=(g == 0), stop=(g == 1))
            mm.then_inc(ssum, 1)
            def dots(t):
                b, h = 2 + t // 8, t % 8
                n = P * (b + 1)
                two = n > 512
                if t >= 1 + (not two):
                    pe.wait_ge(dot_relu, t if two else t - 1)
                half = slice(64 * (h % 2), 64 * (h % 2) + 64)
                for a in range(0, n, 512):
                    w = min(512, n - a)
                    bank = 2 + (a // 512 if two else t % 2)
                    mm = pe.matmul(PS[:, bank, 0:w], QI[half, h // 2, b * P:(b + 1) * P],
                                   KI[half, a:a + w], start=True, stop=True)
                mm.then_inc(dot_mm, 1)

            def sample_logits(s):
                pe.wait_ge(k_in[s % 2], 64 * (s // 2 + 1))
                if s >= 1:
                    pe.wait_ge(sexp, s)
                for o, keys, bias in ((PS[0:NS, 0, :], lambda c: KP[s % 2][:, c, :], sbias[:, 0:PAST]),
                                      (PS[0:NS, 1, 0:NS], lambda c: K[:, c, NP:NT], sbias[:, PAST:SK])):
                    for c in range(4):
                        pe.matmul(o, QB[:, c, s, :], keys(c), start=(c == 0), stop=False)
                    mm = pe.matmul(o, rep[:, s, :], bias, start=False, stop=True)
                mm.then_inc(slg, 1)

            def sample_turn(s):
                pe.wait_ge(snorm, s + 1)
                if s >= 1:
                    pe.wait_ge(ste, 2 * s)
                for t in range(5):
                    w = P if t < 4 else NS
                    mm = pe.transpose(PS[0:w, 4, t * NS:(t + 1) * NS], sp_[0:NS, t * P:t * P + w], ident[0:NS, 0:NS])
                mm.then_inc(stp, 1)

            def sample_values(s):
                pe.wait_ge(ste, 2 * (s + 1))
                pe.wait_ge(v_in[s % 2], 64 * (s // 2 + 1))
                if s >= 1:
                    pe.wait_ge(satt, 2 * s)
                for c in range(4):
                    o = PS[:, 5, 8 * c:8 * c + 8]
                    for t in range(4):
                        pe.matmul(o, VP[s % 2][:, t, c * P:(c + 1) * P], spt[:, t, 8 * c:8 * c + 8],
                                  start=(t == 0), stop=False)
                    mm = pe.matmul(o, VS[:, c * P:(c + 1) * P], spt[0:NS, 4, 8 * c:8 * c + 8], start=False, stop=True)
                mm.then_inc(spv, 1)

            def logits(e):
                b, h = e // 8, e % 8
                n = P * (b + 1)
                half = slice(64 * (h % 2), 64 * (h % 2) + 64)
                if e == 0:
                    pe.wait_ge(sexp, SEQS)
                    pe.wait_ge(mb_early, 2)
                elif e <= 56:
                    pe.wait_ge(aexp, e)
                else:
                    pe.wait_ge(aexp, e - 1)
                if e == 57:
                    pe.wait_ge(dot_relu, 48)
                if b >= 2 and h == 0:
                    pe.wait_ge(mb_set, b - 1)
                for a in range(0, n, 512):
                    w = min(512, n - a)
                    o = PS[:, 2 * logit_pair(e) + a // 512, 0:w]
                    pe.matmul(o, Q[half, h // 2, b * P:(b + 1) * P], K[half, h // 2, a:a + w], start=True, stop=False)
                    m = mask_cols(b)
                    mm = pe.matmul(o, identb[:, :], MB[:, m.start + a:m.start + a + w], start=False, stop=True)
                mm.then_inc(lg, 1)

            def turn_probs(e):
                b = e // 8
                pe.wait_ge(anorm, e + 1)
                if e >= 1:
                    pe.wait_ge(ate, e)
                else:
                    pe.wait_ge(ste, 2 * SEQS)
                for t in range(b + 1):
                    mm = pe.transpose(PS[:, 4 + t // 4, (t % 4) * P:(t % 4 + 1) * P], PR[e % 2][:, t * P:(t + 1) * P],
                                      ident[:, :])
                mm.then_inc(atp, 1)

            def values(e):
                b, h = e // 8, e % 8
                pe.wait_ge(ate, e + 1)
                if e >= 4 and e % 2 == 0:
                    pe.wait_ge(ao_lo, e // 2 - 1)
                o = PS[64 * (h % 2):64 * (h % 2) + 64, 6 + (e // 2) % 2, 0:P]
                for t in range(b + 1):
                    mm = pe.matmul(o, VT[:, t, h * HD:(h + 1) * HD], PT[e % 2][:, t, :], start=(t == 0), stop=(t == b))
                mm.then_inc(apv, 1)

            for t in range(8):
                dots(t)
            pe.wait_ge(qb_set, 8)
            pe.wait_ge(sb_set, 2)
            pe.wait_ge(wt_set, 16)
            for k in range(SLOTS + 1):
                if k < SLOTS:
                    sample_logits(k) if k < SEQS else logits(k - SEQS)
                if k >= 1:
                    sample_turn(k - 1) if k <= SEQS else turn_probs(k - 1 - SEQS)
                for t in slot_dots(k):
                    dots(t)
                if k >= 1:
                    sample_values(k - 1) if k <= SEQS else values(k - 1 - SEQS)
            pe.wait_ge(ao_lo, 32 + 4)
            slabs(OUT1, KD, KD, XH, XL)
            norm_sums(3, UP1)
            pe.wait_ge(x_lo, 4 * KD)
            ffn(UP1, 1)
            norm_sums(4, SLABS)

        @block.scalar
        def _(act):
            act.dma_start(Z[:, :, :], io["xT"]).then_inc(x_in, 16)
            act.dma_start(ident[:, :], io["ident"]).then_inc(consts_in, 16)
            for dst, name in ((lng[:, :], "lng"), (lnb[:, :], "lnb"), (wsT[:, :, :], "wsT"), (bd[:, :, :], "bd"),
                              (bsb[:, :, :], "bsb"), (bw[:, :, :], "bw"), (bh[:, :, :, :], "bh"), (lnp[:, :, :, :], "lnp")):
                act.dma_start(dst, io[name]).then_inc(mix_in, 16)

            def split_high(n, i=None, per=0):
                j = n % 2
                act.wait_ge(loaded[j], val(i, per * 8, 16 * (n // 2 + 1)))
                act.activation(WH[j][:, :, :], RAW[j][:, :, :], ACT.Copy).then_inc(w_hi, 1)

            act.wait_ge(x_in, 16)
            for k in range(KD):
                act.activation(XH[:, k, :], Z[:, k, :], ACT.Copy).then_inc(x_hi, 1)
            split_high(0)
            split_high(1)

            def split_ahead(n):
                if n + 2 < OUT1:
                    split_high(n + 2)

            def copied_slabs(first, count, rows, func=ACT.Copy, scale=1.0, free=None):
                with act.Fori(0, count // 2) as i:
                    for j in range(2):
                        act.wait_ge(mm_done, i * 2 + (first + j + 1))
                        if free:
                            act.wait_ge(*free(i, j))
                        act.activation(three(rows(i, j)), bank_set((first + j) % 2), func, scale=scale).then_inc(
                            evac_done[(first + j) % 2], 1)
                        split_high(first + j + 2, i, 2)

            copied_slabs(0, 4, lambda i, j: gv[j][:, :], ACT.Gelu_apprx_tanh)
            act.wait_ge(x_lo, KD)
            copied_slabs(4, 4, lambda i, j: row_of(U, i * 2 + j), ACT.Gelu_apprx_tanh)
            act.wait_ge(vagg, 9)
            act.activation(vrs[:, 0:8], vmv[:, 0:8, 1], ACT.Sqrt, bias=epst[:, :]).then_inc(vsd, 1)
            act.activation(vrs[0:NS, 8:9], vmv[0:NS, 8, 1:2], ACT.Sqrt, bias=epst[0:NS, :]).then_inc(vsd, 1)

            for g in range(4):
                act.wait_ge(gate_f, g + 1)
                act.activation(MH[:, g, :], cf[:, :], ACT.Copy).then_inc(mix_hi, 1)
            act.wait_ge(vnorm, 9)
            act.dma_start(io["o_av"], vtoks[:, :]).then_inc(out_done, 16)
            for jj in range(4):
                n = 8 + 3 * jj
                act.wait_ge(mm_done, n + 1)
                act.wait_ge(mix_lo, 4 + jj)
                act.activation(three(cf[:, :]), bank_set(n % 2), ACT.Copy).then_inc(evac_done[n % 2], 1)
                split_high(n + 2)
                for d in (1, 2):
                    act.wait_ge(mm_done, n + d + 1)
                    split_high(n + d + 2)
                wait_emptied(act, n + 2)
                act.activation(MH[:, 4 + jj, :], cf[:, :], ACT.Copy).then_inc(mix_hi, 1)
            act.wait_ge(bstd, 5)
            act.dma_start(io["o_bst"], bst[:, :, :]).then_inc(out_done, 16)

            def squares(l, first):
                def step(i, m, more=True):
                    act.wait_ge(mm_done, val(i, 2, first + m + 1))
                    if more:
                        split_high(first + m + 2, i, 2)
                    wait_emptied(act, first + m, i, 2)
                    act.wait_ge(zq_done, val(i, 2, 9 * (l - 1) + m + 1))
                    act.activation(sq[:, :], row_of(Z, val(i, 2, m)), ACT.Square).then_inc(sq_done, 1)

                more = first + KD < SLABS
                with act.Fori(0, KD // 2 if more else KD // 2 - 1) as i:
                    for j in range(2):
                        step(i, j)
                if not more:
                    step(None, KD - 2, False)
                    step(None, KD - 1, False)

            def norm(l, last=False):
                act.wait_ge(ln_mean, l)
                act.activation(three(mean[:, :]), bank_set(0), ACT.Copy).then_inc(ln_a, 1)
                act.activation(three(msq[:, :]), bank_set(0), ACT.Square).then_inc(ln_a, 1)
                act.wait_ge(ln_var, 2 * l)
                act.activation(rstd[:, :], msq[:, :], ACT.Sqrt, bias=epst[:, :]).then_inc(ln_sd, 1)
                with act.Fori(0, KD) as m:
                    row = row_of(Z, m)
                    act.wait_ge(ln_d, m + (KD * (l - 1) + 1))
                    act.activation(row, row, ACT.Identity, scale=lnp[:, l - 1, 0, bass.ds(m, 1)],
                                   bias=lnp[:, l - 1, 1, bass.ds(m, 1)]).then_inc(ln_z, 1)
                    if not last:
                        act.wait_ge(ln_z, m + (KD * (l - 1) + 1))
                        act.activation(row_of(XH, m), row, ACT.Copy).then_inc(x_hi, 1)

            def ffn(first, layer):
                act.wait_ge(mm_done, first)
                act.dma_start(fpar[:, :, :], io["fpar"][layer]).then_inc(fpar_in, 16)
                act.dma_start(fhist[:, :, :, :], io["fhist"][layer]).then_inc(fpar_in, 16)
                norm(2 * layer + 1)
                n, u, q = first, layer * 2 * FC, layer * FC
                for bi, nb in enumerate(BLOCKS):
                    with act.Fori(0, nb // 2) as i:
                        for pp in range(2):
                            for j in range(2):
                                s = 2 * pp + j
                                act.wait_ge(mm_done, i * 4 + (n + s + 1))
                                act.wait_ge(conv_done, i * 4 + (u + s + 1))
                                act.wait_ge(st_done, i * 4 + (u + s + 1))
                                for dst, src_ in zip(parts(ext[j], HIST), bank_parts(j)):
                                    ins = act.activation(dst, src_, ACT.Copy)
                                ins.then_inc(evac_done[j], 1)
                                split_high(n + s + 2, i, 4)
                                if j == 0:
                                    act.wait_ge(conv_done, i * 4 + (u + s + 3))
                                    act.activation(sg[:, :], cv[0][:, :], ACT.Silu).then_inc(silu_done, 1)
                                else:
                                    act.wait_ge(hmul, i * 2 + (q + pp + 1))
                                    act.activation(row_of(HH, i * 2 + pp), hf[:, :], ACT.Copy).then_inc(h_hi, 1)
                    n += 2 * nb
                    u += 2 * nb
                    q += nb
                    if bi < len(BLOCKS) - 1:
                        with act.Fori(0, KD // 2) as i:
                            for j in range(2):
                                act.wait_ge(mm_done, i * 2 + (n + j + 1))
                                split_high(n + j + 2, i, 2)
                    else:
                        squares(2 * layer + 2, n)
                    n += KD
                act.wait_ge(st_done, u + 2)
                act.dma_start(io["o_fst"][layer], fst[:, :, :]).then_inc(fst_out, 16)

            def write_y(l):
                act.wait_ge(ln_z, KD * l)
                act.dma_start(io["o_y"], Z[:, :, :]).then_inc(out_done, 16)
                act.wait_ge(out_done, 48)

            squares(1, OUT0)
            ffn(UP0, 0)
            act.wait_ge(fst_out, 16)
            norm(2)
            act.wait_ge(x_lo, 3 * KD)
            act.dma_start(phist[:, :, :, :], io["phist"]).then_inc(phist_in, 16)
            act.dma_start(cw[:, :, :], io["cw"]).then_inc(l1_in, 16)
            act.dma_start(csc[:, :], io["csc"]).then_inc(l1_in, 16)
            act.dma_start(icnt[:, :, :], io["icnt"]).then_inc(l1_in, 16)
            for g in range(4):
                n = IN1 + g
                act.wait_ge(mm_done, n + 1)
                if g == 0:
                    act.wait_ge(pool_zero, 1)
                else:
                    act.wait_ge(pooled, g)
                    act.wait_ge(pst_set, g)
                for dst, src_ in zip(parts(pe0, PH), bank_parts(n % 2)):
                    ins = act.activation(dst, src_, ACT.Copy)
                ins.then_inc(evac_done[n % 2], 1)
                split_high(n + 2)
            act.wait_ge(pst_set, 4)
            act.dma_start(io["o_pst"], pst[:, :, :, :]).then_inc(pst_out, 16)
            act.wait_ge(pooled, 4)
            act.dma_start(RC[:, :], io["rc"]).then_inc(rope_in, 16)
            act.dma_start(RS[:, :], io["rs"]).then_inc(rope_in, 16)
            copied_slabs(IN1 + 4, 4, lambda i, j: qf[j][:, :])

            def roped_slabs(first, count, scale=1.0):
                r = first - IN1 - 8
                copied_slabs(first, count, lambda i, j: qf[j][:, :], scale=scale, free=lambda i, j: (roped, i * 2 + (r + j + 1)))

            roped_slabs(IN1 + 8, 4, HD ** -0.5)
            roped_slabs(IN1 + 12, 8)
            for n in (IN1 + 20, IN1 + 21):
                act.wait_ge(mm_done, n + 1)
                act.wait_ge(roped, n - IN1 - 8 + 1)
                act.activation(three(qf[n % 2][:, :]), bank_set(n % 2), ACT.Copy).then_inc(evac_done[n % 2], 1)
            wait_emptied(act, OUT1 - 1)
            act.dma_start(wis.rearrange("s h q -> h s q"), qf[1][0:HEADS, NP:NT].rearrange("p (s q) -> p s q", s=SEQS)).then_inc(wi_out, 16)
            act.wait_ge(roped, 15)
            act.dma_start(io["o_k"], K[:, :, :]).then_inc(kv_out, 16)
            act.dma_start(io["o_ki"], KI[0:IDX, :]).then_inc(kv_out, 16)
            act.dma_start(io["o_v"], VT[:, :, :]).then_inc(kv_out, 16)
            act.dma_start(io["o_vs"], VS[:, :]).then_inc(kv_out, 16)
            for g in range(4):
                act.wait_ge(cmm, g + 1)
                act.wait_ge(z_pre, KD * 2 + g + 1)
                act.activation(three(XH[:, g, :]), bank_set(g % 2), ACT.Copy, scale=csc[:, g:g + 1]).then_inc(c_hi, 1)
            act.wait_ge(z_pre, KD * 3)
            act.dma_start(ptab[:, :], io["ptab"]).then_inc(pt_in, 16)
            for dst, name in ((iota, "iota"), (cmask, "cmask")):
                act.dma_start(dst[:, :], io[name]).then_inc(sconst_in, 16)
            act.dma_start(hsum[:, :, :], io["hsum"]).then_inc(sconst_in, 16)
            act.wait_ge(w_lo, OUT1)
            act.dma_start(rep[:, :, :], io["rep"]).then_inc(sconst_in, 16)
            act.dma_start(identb[:, :], io["identb"]).then_inc(wt_set, 16)
            act.wait_ge(wi_out, 16)
            for g in range(2):
                act.dma_start(wrow[:, g:g + 1], wis[4 * g:4 * g + 4].rearrange("s h (q a) -> (s h q) a", a=1)).then_inc(wi_in, 16)
            def rectified(t):
                n = P * (3 + t // 8)
                act.wait_ge(dot_mm, t + 1)
                if t >= 2:
                    act.wait_ge(sc_acc, t - 1)
                src_ = pair(1, n) if n > 512 else PS[:, 2 + t % 2, 0:n]
                act.activation(RR[t % 2][:, 0:n], src_, ACT.Relu).then_inc(dot_relu, 1)

            def sample_exp(s):
                act.wait_ge(smax, s + 1)
                if s >= 1:
                    act.wait_ge(stp, s)
                act.activation(sp_[0:NS, :], pair(0, SK, NS), ACT.Exp, bias=nmx[0:NS, s % 2:s % 2 + 1],
                               accum_out=psm[0:NS, s % 2:s % 2 + 1]).then_inc(sexp, 1)

            def sample_norm(s):
                act.wait_ge(ssump, s + 1)
                act.activation(sp_[0:NS, :], sp_[0:NS, :], ACT.Copy, scale=prc[0:NS, s % 2:s % 2 + 1]).then_inc(snorm, 1)

            def sample_turned(s):
                act.wait_ge(stp, s + 1)
                if s >= 1:
                    act.wait_ge(spv, s)
                act.activation(spt[:, 0:4, :], PS[:, 4, 0:4 * NS].rearrange("p (t r) -> p t r", t=4), ACT.Copy).then_inc(ste, 1)
                act.activation(spt[0:NS, 4, :], PS[0:NS, 4, 4 * NS:5 * NS], ACT.Copy).then_inc(ste, 1)

            def sample_out(s):
                act.wait_ge(spv, s + 1)
                for hh in range(2):
                    half = slice(64 * hh, 64 * hh + 64)
                    act.activation(atts[half, :, DEC * s:DEC * s + DEC],
                                   PS[half, 5, 0:32].rearrange("p (c r) -> p c r", c=4)[:, :, 4 * hh:4 * hh + 4],
                                   ACT.Copy).then_inc(satt, 1)

            def exp(e):
                n = P * (e // 8 + 1)
                act.wait_ge(amax, e + 1)
                if e >= 2:
                    act.wait_ge(atp, e - 1)
                act.activation(PR[e % 2][:, 0:n], pair(logit_pair(e), n), ACT.Exp, bias=nmx[:, e % 2:e % 2 + 1],
                               accum_out=psm[:, e % 2:e % 2 + 1]).then_inc(aexp, 1)

            def norm_probs(e):
                if e < 56:
                    n = P * (e // 8 + 1)
                    act.wait_ge(asum, e + 1)
                    act.activation(PR[e % 2][:, 0:n], PR[e % 2][:, 0:n], ACT.Copy,
                                   scale=prc[:, e % 2:e % 2 + 1]).then_inc(anorm, 1)

            def turned_probs(e):
                b = e // 8
                act.wait_ge(atp, e + 1)
                if e >= 2:
                    act.wait_ge(apv, e - 1)
                else:
                    act.wait_ge(slg, SEQS)
                act.activation(PT[e % 2][:, 0:b + 1, :], pair(2, P * (b + 1)).rearrange("p (t q) -> p t q", q=P),
                               ACT.Copy).then_inc(ate, 1)

            def attended(e):
                if e % 2 == 1:
                    b, c = e // 8, (e % 8) // 2
                    act.wait_ge(apv, e + 1)
                    act.activation(XH[:, 4 + c, b * P:(b + 1) * P], PS[:, 6 + (e // 2) % 2, 0:P], ACT.Copy).then_inc(ao_hi, 1)

            for t in range(8):
                rectified(t)
            for k in range(SLOTS + 1):
                if k >= 1:
                    sample_turned(k - 1) if k <= SEQS else turned_probs(k - 1 - SEQS)
                for t in slot_dots(k):
                    rectified(t)
                if k < SLOTS:
                    sample_exp(k) if k < SEQS else exp(k - SEQS)
                if k >= 1:
                    sample_out(k - 1) if k <= SEQS else attended(k - 1 - SEQS)
                if k < SLOTS:
                    sample_norm(k) if k < SEQS else norm_probs(k - SEQS)
            act.wait_ge(atp, 64)
            split_high(OUT1)
            split_high(OUT1 + 1)
            for c in range(4):
                act.activation(XH[:, 4 + c, NP:NT], atts[:, c, :], ACT.Copy).then_inc(ao_hi, 1)
            squares(3, OUT1)
            act.wait_ge(pst_out, 16)
            act.wait_ge(kv_out, 64)
            ffn(UP1, 1)
            norm(4, True)
            write_y(4)
            act.wait_ge(fst_out, 32)

        @block.gpsimd
        def _(pool):
            def split_rest(n, i=None, per=0):
                j = n % 2
                pool.wait_ge(w_hi, val(i, per, n + 1))
                pool.tensor_tensor(WL[j][:, :, :], RAW[j][:, :, :], WH[j][:, :, :].bitcast(F32),
                                   ALU.subtract).then_inc(w_lo, 1)

            def split_rests(first, count):
                with pool.Fori(0, count // 2) as i:
                    for j in range(2):
                        split_rest(first + j, i, 2)

            pool.memset(onesd[:, :], 1.0 / D)
            pool.memset(epst[:, :], EPS)
            pool.memset(bext[:, 0:HIST], 0.0).then_inc(bstd, 1)
            split_rest(0)
            split_rest(1)
            pool.wait_ge(mix_in, 128)
            pool.affine_select(out=wsT[:, :, :], in_=wsT[:, :, :], pattern=[[0, 4], [1, P]], compare_op=ALU.is_ge,
                               fill=0.0, base=0, channel_multiplier=-1).then_inc(masked, 1)
            pool.affine_select(out=bd[:, :, :], in_=bd[:, :, :], pattern=[[0, 4], [1, NS]], compare_op=ALU.is_ge,
                               fill=0.0, base=0, channel_multiplier=-1).then_inc(masked, 1)
            split_rests(2, 8)
            for jj in range(4):
                n = 8 + 3 * jj
                pool.wait_ge(bconv, jj + 1)
                pool.tensor_copy(sample_cols(bext, HIST, HIST + DEC, HIST + DEC)[:, :, 0:HIST],
                                 bh[:, jj, :, :]).then_inc(bhist, 1)
                for d in (2, 3):
                    split_rest(n + d)
                wait_emptied(pool, n + 1)
                pool.tensor_copy(bst[:, jj, 0:2], bext[:, NP:NP + 2])
                pool.tensor_copy(bst[:, jj, 2:18].rearrange("p (s q) -> p s q", s=SEQS),
                                 sample_cols(bext, HIST, HIST + DEC, 2)).then_inc(bstd, 1)
                split_rest(n + 4)

            def sums(l, first):
                pool.wait_ge(mm_done, first + 1)
                pool.memset(zs[:, :], 0.0).then_inc(zs_done, 1)
                pool.memset(zq[:, :], 0.0).then_inc(zq_done, 1)

                def step(i, m, more=True):
                    if more:
                        split_rest(first + m + 2, i, 2)
                    wait_emptied(pool, first + m, i, 2)
                    pool.wait_ge(zs_done, val(i, 2, 9 * (l - 1) + m + 1))
                    pool.tensor_tensor(zs[:, :], zs[:, :], row_of(Z, val(i, 2, m)), ALU.add).then_inc(zs_done, 1)
                    pool.wait_ge(sq_done, val(i, 2, KD * (l - 1) + m + 1))
                    pool.wait_ge(zq_done, val(i, 2, 9 * (l - 1) + m + 1))
                    pool.tensor_tensor(zq[:, :], zq[:, :], sq[:, :], ALU.add).then_inc(zq_done, 1)

                more = first + KD < SLABS
                with pool.Fori(0, KD // 2 if more else KD // 2 - 1) as i:
                    for j in range(2):
                        step(i, j)
                if not more:
                    step(None, KD - 2, False)
                    step(None, KD - 1, False)

            def ffn(first, layer):
                n, u = first, layer * 2 * FC
                pool.wait_ge(x_lo, KD * (2 + 2 * layer))
                pool.memset(ext[0][:, 0:HIST], 0.0)
                ins = pool.memset(ext[1][:, 0:HIST], 0.0)
                if layer == 0:
                    ins.then_inc(st_done, 2)
                pool.wait_ge(fpar_in, 32 * (layer + 1))
                for bi, nb in enumerate(BLOCKS):
                    with pool.Fori(0, nb // 2) as i:
                        for s in range(4):
                            j = s % 2
                            local = i * 4 + (u - layer * 2 * FC + s)
                            pool.wait_ge(conv_done, i * 4 + (u + s + 1))
                            pool.tensor_copy(sample_cols(ext[j], HIST, HIST + DEC, HIST + DEC)[:, :, 0:HIST],
                                             fhist[:, bass.ds(local, 1), :, :].rearrange("p a s q -> p (a s) q")
                                             ).then_inc(ext_hist, 1)
                            wait_emptied(pool, n + s, i, 4)
                            kept = row_of(fst, local)
                            pool.tensor_copy(kept[:, 0:2], ext[j][:, NP:NP + 2])
                            pool.tensor_copy(kept[:, 2:18].rearrange("p (s q) -> p s q", s=SEQS),
                                             sample_cols(ext[j], HIST, HIST + DEC, 2)).then_inc(st_done, 1)
                            split_rest(n + s + 2, i, 4)
                    n += 2 * nb
                    u += 2 * nb
                    if bi < len(BLOCKS) - 1:
                        split_rests(n + 2, KD)
                    else:
                        sums(2 * layer + 2, n)
                    n += KD

            sums(1, OUT0)
            ffn(UP0, 0)
            pool.wait_ge(x_lo, 3 * KD)
            pool.memset(pe0[:, 0:PH], 0.0).then_inc(pool_zero, 1)
            pool.wait_ge(phist_in, 16)
            for g in range(4):
                n = IN1 + g
                if g >= 1:
                    pool.wait_ge(pooled, g)
                    pool.wait_ge(pst_set, g)
                pool.tensor_copy(sample_cols(pe0, PH, PH + DEC, PH + DEC)[:, :, 0:PH], phist[:, g, :, :]).then_inc(phist_set, 1)
                wait_emptied(pool, n)
                pool.wait_ge(phist_set, g + 1)
                pool.tensor_copy(pst[:, g, 0, :], pe0[:, NP:NP + PH])
                pool.tensor_copy(pst[:, g, 1:9, :], sample_cols(pe0, PH, PH + DEC, PH)).then_inc(pst_set, 1)
                split_rest(n + 2)
            split_rests(IN1 + 6, 16)
            pool.wait_ge(z_pre, KD * 3)
            pool.memset(QIB[:, :, :], 0.0).then_inc(qib_zero, 1)
            pool.wait_ge(pst_out, 16)
            pool.wait_ge(turn_evac, 39)
            pool.memset(MB[:, 0:3 * P], 0.0).then_inc(mb_early, 1)
            pool.wait_ge(mb_early, 1)
            for a in (0, 2 * P):
                ins = pool.affine_select(out=MB[:, a:a + P], in_=MB[:, a:a + P], pattern=[[-1, P]], compare_op=ALU.is_ge,
                                         fill=FAR, base=0, channel_multiplier=1)
            ins.then_inc(mb_early, 1)
            pool.wait_ge(w_lo, OUT1)
            pool.memset(QB[:, :, :, :], 0.0).then_inc(qb_zero, 1)

            def score(t):
                b, h = 2 + t // 8, t % 8
                n = P * (b + 1)
                sc, w = SC[b % 2][:, 0:n], wtok[:, b, h:h + 1]
                pool.wait_ge(dot_relu, t + 1)
                if h == 0:
                    if b >= 4:
                        pool.wait_ge(mb_set, b - 3)
                    pool.tensor_scalar(sc, RR[t % 2][:, 0:n], w, None, ALU.mult).then_inc(sc_acc, 1)
                else:
                    r_ = RR[t % 2][:, 0:n]
                    pool.tensor_scalar(r_, r_, w, None, ALU.mult).then_inc(weighted, 1)
                    pool.wait_ge(sc_acc, t)
                    pool.wait_ge(weighted, t - t // 8)
                    pool.tensor_tensor(sc, sc, r_, ALU.add).then_inc(sc_acc, 1)
                if h == 7:
                    pool.wait_ge(sc_acc, t + 1)
                    diag = SC[b % 2][:, b * P:(b + 1) * P]
                    pool.affine_select(out=diag, in_=diag, pattern=[[-1, P]], compare_op=ALU.is_ge,
                                       fill=BARRED, base=0, channel_multiplier=1).then_inc(sc_barred, 1)

            for t in range(48):
                score(t)
            pool.wait_ge(apv, 64)
            split_rest(OUT1)
            split_rest(OUT1 + 1)
            sums(3, OUT1)
            ffn(UP1, 1)

        @block.vector
        def _(dve):
            dve.memset(seed[:, 0:1], 0.0).then_inc(evac_done[0], 1)
            dve.memset(seed[:, 1:2], 0.0).then_inc(evac_done[1], 1)
            dve.memset(seed[:, 2:3], 0.0).then_inc(conv_done, 2)
            dve.memset(seed[:, 3:4], 0.0).then_inc(bconv, 1)
            dve.memset(seed[:, 4:5], 0.0).then_inc(turn_evac, 2)
            dve.memset(seed[:, 5:6], 0.0).then_inc(roped, 2)
            for k in range(KD):
                dve.wait_ge(x_hi, k + 1)
                dve.tensor_tensor(XL[:, k, :], Z[:, k, :], XH[:, k, :].bitcast(F32), ALU.subtract).then_inc(x_lo, 1)

            def turned_rows(f0, blocks, tail):
                with dve.Fori(0, 2) as i:
                    for j in range(2):
                        for part in range(3):
                            f = f0 + 3 * j + part
                            dve.wait_ge(turned, i * 6 + (f + 1))
                            cols = bass.ds(i * 256 + j * P, P)
                            if part < 2:
                                dve.tensor_copy(blocks[:, 4 * part:4 * part + 4, cols],
                                                turn_bank(f).rearrange("p (b c) -> p b c", b=4)).then_inc(turn_evac, 1)
                            else:
                                dve.tensor_copy(tail[:, cols], turn_bank(f)[0:NS, 0:P]).then_inc(turn_evac, 1)

            turned_rows(0, vtok, vtoks)
            dve.wait_ge(turn_evac, 14)

            def vblock(t):
                return (vtok[:, t, :], P) if t < 8 else (vtoks[:, :], NS)

            for t in range(9):
                a, w = vblock(t)
                dve.bn_stats(vst[0:w, t, :], a).then_inc(vstat, 1)
            for t in range(9):
                w = vblock(t)[1]
                dve.wait_ge(vstat, t + 1)
                dve.bn_aggr(vmv[0:w, t, :], vst[0:w, t, :]).then_inc(vagg, 1)
            dve.wait_ge(vsd, 2)
            dve.reciprocal(vrs[:, 0:8], vrs[:, 0:8]).then_inc(vln, 1)
            dve.reciprocal(vrs[0:NS, 8:9], vrs[0:NS, 8:9]).then_inc(vln, 1)
            dve.wait_ge(vln, 2)
            dve.wait_ge(mix_in, 128)
            for t in range(9):
                a, w = vblock(t)
                dve.tensor_scalar(a, a, vmv[0:w, t, 0:1], vrs[0:w, t:t + 1], ALU.subtract, ALU.mult).then_inc(vln, 1)
            for t in range(9):
                a, w = vblock(t)
                dve.wait_ge(vln, 2 + t + 1)
                dve.tensor_tensor(a, a, lng[0:w, :], ALU.mult).then_inc(vln, 1)
            for t in range(9):
                a, w = vblock(t)
                dve.wait_ge(vln, 11 + t + 1)
                dve.tensor_tensor(a, a, lnb[0:w, :], ALU.add).then_inc(vnorm, 1)

            def mix_rest(k):
                dve.wait_ge(mix_hi, k + 1)
                dve.tensor_tensor(ML[:, k, :], cf[:, :], MH[:, k, :].bitcast(F32), ALU.subtract).then_inc(mix_lo, 1)

            for g in range(4):
                if g >= 1:
                    dve.wait_ge(mix_lo, g)
                for part in range(3):
                    f = 12 + 3 * g + part
                    dve.wait_ge(turned, f + 1)
                    if part < 2:
                        o = cf[:, part * 512:(part + 1) * 512].rearrange("p (b t) -> p b t", b=4)
                        dve.tensor_tensor(o, turn_bank(f).rearrange("p (b t) -> p b t", b=4),
                                          bsb[:, g, None, :].to_broadcast([P, 4, P]), ALU.add).then_inc(turn_evac, 1)
                    else:
                        o = cf[:, NP:NT].rearrange("p (s q) -> p s q", s=SEQS)
                        dve.tensor_tensor(o, turn_bank(f)[:, 0:NS].rearrange("p (s q) -> p s q", s=SEQS),
                                          bsb[:, g, None, 0:DEC].to_broadcast([P, SEQS, DEC]), ALU.add).then_inc(turn_evac, 1)
                dve.wait_ge(turn_evac, 2 + f + 1)
                if g == 0:
                    wait_emptied(dve, 6)
                    wait_emptied(dve, 7)
                dve.tensor_tensor(cf[:, :], cf[:, :], U[:, g, :], ALU.mult).then_inc(gate_f, 1)
                mix_rest(g)

            def taps(row, out, w, tap_sem, value, done):
                if len(w) == 4:
                    dve.tensor_scalar(out, row[:, 2:2 + CW], w[2], w[3], ALU.mult, ALU.add).then_inc(tap_sem, 1)
                else:
                    dve.tensor_scalar(out, row[:, 2:2 + CW], w[2], None, ALU.mult).then_inc(tap_sem, 1)
                dve.wait_ge(tap_sem, value(1))
                dve.scalar_tensor_tensor(out, row[:, 0:CW], w[0], out, ALU.mult, ALU.add).then_inc(tap_sem, 1)
                dve.wait_ge(tap_sem, value(2))
                dve.scalar_tensor_tensor(out, row[:, 1:1 + CW], w[1], out, ALU.mult, ALU.add).then_inc(done, 1)

            for jj in range(4):
                n = 8 + 3 * jj
                dve.wait_ge(mm_done, n + 2)
                wait_emptied(dve, n)
                dve.wait_ge(bstd, jj + 1)
                for dst, src_, c in zip(parts(bext, HIST), bank_parts((n + 1) % 2), parts(cf)):
                    ins = dve.tensor_tensor(dst, src_, c, ALU.mult)
                ins.then_inc(evac_done[(n + 1) % 2], 1)
                wait_emptied(dve, n + 1)
                dve.wait_ge(bhist, jj + 1)
                taps(bext, bcv[:, :], [bw[:, jj, t:t + 1] for t in range(3)], btap, lambda k: 2 * jj + k, bconv)
                dve.wait_ge(bconv, jj + 2)
                dve.wait_ge(mm_done, n + 3)
                conv_parts = [bcv[:, 0:2 * TW].rearrange("p (c t) -> p c t", c=2), bcv[:, 2 * TW:NP],
                              sample_cols(bcv, 0, HIST + DEC, DEC)]
                for dst, src_, c in zip(parts(cf), bank_parts(n % 2), conv_parts):
                    ins = dve.tensor_tensor(dst, src_, c, ALU.mult)
                ins.then_inc(evac_done[n % 2], 1)
                mix_rest(4 + jj)

            def projected(first, pres, before=None):
                with dve.Fori(0, KD // 2) as i:
                    for j in range(2):
                        n = first + j
                        z = row_of(Z, i * 2 + j)
                        if pres is not None:
                            dve.tensor_tensor(z, row_of(XH, i * 2 + j).bitcast(F32), row_of(XL, i * 2 + j).bitcast(F32),
                                              ALU.add).then_inc(z_pre, 1)
                            dve.wait_ge(z_pre, i * 2 + (pres + j + 1))
                        dve.wait_ge(mm_done, i * 2 + (n + 1))
                        if pres is not None or before:
                            dve.scalar_tensor_tensor(three(z), three(z), ALPHA, bank_set(j), ALU.mult,
                                                     ALU.add).then_inc(evac_done[j], 1)
                        else:
                            dve.tensor_tensor(three(z), three(z), bank_set(j), ALU.add).then_inc(evac_done[j], 1)

            def norm(l, last=False):
                dve.wait_ge(ln_a, 2 * l)
                dve.wait_ge(ln_sq, l)
                dve.tensor_tensor(three(msq[:, :]), bank_set(1), three(msq[:, :]), ALU.subtract).then_inc(ln_var, 1)
                dve.wait_ge(ln_var, 2 * l - 1)
                dve.tensor_scalar(msq[:, :], msq[:, :], 0.0, None, ALU.max).then_inc(ln_var, 1)
                dve.wait_ge(ln_sd, l)
                dve.reciprocal(rstd[:, :], rstd[:, :]).then_inc(ln_rstd, 1)
                dve.wait_ge(ln_rstd, l)
                k0 = KD * (l - 1)
                with dve.Fori(0, KD // 2) as i:
                    for j in range(2):
                        z = row_of(Z, i * 2 + j)
                        dve.tensor_tensor(z, z, mean[:, :], ALU.subtract).then_inc(ln_sub, 1)
                    for j in range(2):
                        z = row_of(Z, i * 2 + j)
                        dve.wait_ge(ln_sub, i * 2 + (k0 + j + 1))
                        dve.tensor_tensor(z, z, rstd[:, :], ALU.mult).then_inc(ln_d, 1)
                    if not last:
                        for j in range(2):
                            dve.wait_ge(x_hi, i * 2 + (KD * l + j + 1))
                            dve.tensor_tensor(row_of(XL, i * 2 + j), row_of(Z, i * 2 + j),
                                              row_of(XH, i * 2 + j).bitcast(F32), ALU.subtract).then_inc(x_lo, 1)

            def ffn(first, layer):
                n, u, q = first, layer * 2 * FC, layer * FC
                dve.wait_ge(fpar_in, 32 * (layer + 1))
                for bi, nb in enumerate(BLOCKS):
                    with dve.Fori(0, nb // 2) as i:
                        for pp in range(2):
                            for j in range(2):
                                s = 2 * pp + j
                                wait_emptied(dve, n + s, i, 4)
                                dve.wait_ge(ext_hist, i * 4 + (u + s + 1))
                                w = row_of(fpar, i * 4 + (u - layer * 2 * FC + s))
                                taps(ext[j], cv[j][:, :], [w[:, t:t + 1] for t in range(4)], tap,
                                     lambda k: i * 8 + (2 * (u + s) + k), conv_done)
                            pq = i * 2 + (q + pp + 1)
                            dve.wait_ge(silu_done, pq)
                            dve.wait_ge(conv_done, i * 4 + (u + 2 * pp + 1 + 3))
                            dve.tensor_tensor(hf[:, 0:NP], sg[:, 0:NP], cv[1][:, 0:NP], ALU.mult)
                            dve.tensor_tensor(hf[:, NP:NT].rearrange("p (s q) -> p s q", s=SEQS),
                                              sample_cols(sg, 0, HIST + DEC, DEC), sample_cols(cv[1], 0, HIST + DEC, DEC),
                                              ALU.mult).then_inc(hmul, 1)
                            dve.wait_ge(h_hi, pq)
                            dve.tensor_tensor(row_of(HL, i * 2 + pp), hf[:, :], row_of(HH, i * 2 + pp).bitcast(F32),
                                              ALU.subtract).then_inc(h_lo, 1)
                    n += 2 * nb
                    u += 2 * nb
                    q += nb
                    projected(n, KD * (1 + 2 * layer) if bi == 0 else None)
                    n += KD

            projected(OUT0, 0)
            norm(1)
            ffn(UP0, 0)
            norm(2)
            dve.wait_ge(l1_in, 48)
            step = 0
            for g, w in enumerate((2, 4, 8, 16)):
                wait_emptied(dve, IN1 + g)
                dve.wait_ge(phist_set, g + 1)
                a, bufs, width = pe0, [pe1, pe2], 1
                while width < w:
                    o = bufs[0]
                    lo = 2 * width - 1
                    dve.tensor_tensor(o[:, lo:PEXT], a[:, lo:PEXT], a[:, lo - width:PEXT - width], ALU.add).then_inc(pwin, 1)
                    step += 1
                    dve.wait_ge(pwin, step)
                    a, bufs, width = o, bufs[::-1], 2 * width
                dve.scalar_tensor_tensor(Z[:, g, 16:NP], a[:, PH + 16:PH + NP], 1.0 / w, pe0[:, PH + 16:PH + NP],
                                         ALU.mult, ALU.subtract)
                dve.scalar_tensor_tensor(Z[:, g, NP:NT].rearrange("p (s q) -> p s q", s=SEQS),
                                         sample_cols(a, PH, PH + DEC, DEC), 1.0 / w, sample_cols(pe0, PH, PH + DEC, DEC),
                                         ALU.mult, ALU.subtract)
                dve.tensor_tensor(a[:, PH:PH + 16], a[:, PH:PH + 16], icnt[:, g, :], ALU.mult).then_inc(pwin, 1)
                step += 1
                dve.wait_ge(pwin, step)
                dve.tensor_tensor(Z[:, g, 0:16], a[:, PH:PH + 16], pe0[:, PH:PH + 16], ALU.subtract).then_inc(pooled, 1)
            turned_rows(24, VT, VS)

            def rotate(r, j, dst, i=None):
                dve.wait_ge(rope_in, 32)
                dve.wait_ge(roped, val(i, 2, r + 2))
                wait_emptied(dve, IN1 + 8 + r, i, 2)
                dve.tensor_tensor(dst, qf[j][:, :], RC[:, :], ALU.mult).then_inc(rcos, 1)
                dve.stream_shuffle(sh[:, :], qf[j][:, :], [p ^ 8 if p < 16 else p for p in range(32)]).then_inc(shuf, 1)
                dve.wait_ge(shuf, val(i, 2, r + 1))
                dve.tensor_tensor(sh[:, :], sh[:, :], RS[:, :], ALU.mult).then_inc(shufs, 1)
                dve.wait_ge(shufs, val(i, 2, r + 1))
                dve.wait_ge(rcos, val(i, 2, r + 1))
                dve.tensor_tensor(dst, dst, sh[:, :], ALU.add).then_inc(roped, 1)

            for r0, t in ((0, Q), (4, K), (8, QI)):
                with dve.Fori(0, 2) as i:
                    for j in range(2):
                        rotate(r0 + j, j, row_of(t, i * 2 + j), i)
            rotate(12, 0, KI[:, :])
            dve.wait_ge(turned, 37)
            dve.tensor_copy(wtok[:, 0:8, :], turn_bank(36)[:, 0:8 * HEADS].rearrange("p (t h) -> p t h", t=8)).then_inc(turn_evac, 1)
            for g in range(4):
                dve.wait_ge(cmm, g + 1)
                dve.tensor_tensor(Z[:, g, :], XH[:, g, :].bitcast(F32), XL[:, g, :].bitcast(F32), ALU.add).then_inc(z_pre, 1)
                dve.wait_ge(c_hi, g + 1)
                dve.scalar_tensor_tensor(three(XL[:, g, :]), bank_set(g % 2), csc[:, g:g + 1], three(XH[:, g, :].bitcast(F32)),
                                         ALU.mult, ALU.subtract).then_inc(cevac, 1)
            dve.wait_ge(pst_out, 16)
            for g in range(4, 8):
                dve.tensor_tensor(Z[:, g, :], XH[:, g, :].bitcast(F32), XL[:, g, :].bitcast(F32), ALU.add).then_inc(z_pre, 1)

            def blocked(dst, src, cleared, done):
                dve.wait_ge(cleared, 1)
                for h in range(HEADS):
                    half = slice(64 * (h % 2), 64 * (h % 2) + 64)
                    dve.tensor_copy(dst(half, h), src[half, h // 2, NP:NT].rearrange("p (s q) -> p s q", s=SEQS)).then_inc(done, 1)

            blocked(lambda half, h: QIB[half, :, DEC * h:DEC * h + DEC], QI, qib_zero, qib_set)
            dve.wait_ge(wi_in, 32)
            for g in range(2):
                dve.wait_ge(sdot, 4 * (g + 1))
                dve.tensor_scalar(rab[g][:, :], pair(g, SK), 0.0, wrow[:, g:g + 1], ALU.max, ALU.mult).then_inc(srelu, 1)
            dve.wait_ge(ssum, 1)
            dve.wait_ge(sconst_in, 64)
            dve.tensor_copy(ssc[:, 0:PAST], PS[0:NS, 4, :]).then_inc(ssc_set, 1)
            dve.tensor_tensor(ssc[:, PAST:SK], PS[0:NS, 5, 0:NS], cmask[:, :], ALU.add).then_inc(ssc_set, 1)
            dve.wait_ge(ssc_set, 2)
            for r in range(TOPK_S // 8):
                dve.max(s8[:, :], ssc[:, :]).then_inc(stop_, 1)
                dve.wait_ge(stop_, 2 * r + 1)
                dve.match_replace(ssc[:, :], s8[:, :], ssc[:, :], TAKEN).then_inc(stop_, 1)
                dve.wait_ge(stop_, 2 * r + 2)
            dve.max(s8[:, :], ssc[:, :]).then_inc(sidx_set, 1)
            dve.wait_ge(sidx_set, 1)
            dve.max_index(sidx[:, :], s8[:, :], ssc[:, :]).then_inc(sidx_set, 1)
            dve.wait_ge(sidx_set, 2)
            dve.tensor_copy(sidf[:, :], sidx[:, 0:1]).then_inc(sidx_set, 1)
            dve.wait_ge(sidx_set, 3)
            dve.tensor_scalar(sbias[:, :], iota[:, :], sidf[:, 0:1], FAR, ALU.not_equal, ALU.mult).then_inc(sb_set, 1)
            dve.wait_ge(sb_set, 1)
            dve.scalar_tensor_tensor(sbias[:, :], ssc[:, :], TAKEN, sbias[:, :], ALU.is_gt, ALU.mult).then_inc(sb_set, 1)
            blocked(lambda half, h: QB[half, h // 2, :, DEC * h:DEC * h + DEC], Q, qb_zero, qb_set)

            def best(r):
                b = 2 + r // BEST
                n = P * (b + 1)
                sc = SC[b % 2][:, 0:n]
                if r % BEST == 0:
                    dve.wait_ge(sc_barred, b - 1)
                dve.max(m8[:, :], sc).then_inc(top_, 1)
                dve.wait_ge(top_, 2 * r + 1)
                dve.match_replace(sc, m8[:, :], sc, TAKEN).then_inc(top_, 1)
                dve.wait_ge(top_, 2 * r + 2)
                if r % BEST == BEST - 1:
                    dve.tensor_scalar(MB[:, mask_cols(b)], sc, TAKEN, FAR, ALU.is_gt, ALU.mult).then_inc(mb_set, 1)

            def rounds(k, part):
                a, z = start_round[k], start_round[k + 1]
                mid = (a + z) // 2
                for r in range(a, mid) if part == 0 else range(mid, z):
                    best(r)

            def sample_max(s):
                j = s % 2
                dve.wait_ge(slg, s + 1)
                dve.tensor_reduce(nmx[0:NS, j:j + 1], pair(0, SK, NS), AXX, ALU.max, negate=True).then_inc(smax, 1)

            def sample_recip(s):
                j = s % 2
                dve.wait_ge(sexp, s + 1)
                dve.reciprocal(prc[0:NS, j:j + 1], psm[0:NS, j:j + 1]).then_inc(ssump, 1)

            def row_max(e):
                n, j = P * (e // 8 + 1), e % 2
                dve.wait_ge(lg, e + 1)
                dve.tensor_reduce(nmx[:, j:j + 1], pair(logit_pair(e), n), AXX, ALU.max, negate=True).then_inc(amax, 1)

            def row_recip(e):
                n, j = P * (e // 8 + 1), e % 2
                dve.wait_ge(aexp, e + 1)
                dve.reciprocal(prc[:, j:j + 1], psm[:, j:j + 1]).then_inc(asum, 1)
                if e >= 56:
                    dve.wait_ge(asum, e + 1)
                    dve.tensor_scalar(PR[j][:, 0:n], PR[j][:, 0:n], prc[:, j:j + 1], None, ALU.mult).then_inc(anorm, 1)

            def att_rest(pr):
                dve.wait_ge(ao_hi, pr + 1)
                b, c = pr // 4, pr % 4
                dve.tensor_tensor(XL[:, 4 + c, b * P:(b + 1) * P], PS[:, 6 + pr % 2, 0:P],
                                  XH[:, 4 + c, b * P:(b + 1) * P].bitcast(F32), ALU.subtract).then_inc(ao_lo, 1)

            for k in range(SLOTS):
                e = k - SEQS
                if e >= 3 and e % 2 == 1:
                    att_rest((e - 3) // 2)
                rounds(k, 0)
                sample_max(k) if k < SEQS else row_max(e)
                rounds(k, 1)
                sample_recip(k) if k < SEQS else row_recip(e)
            att_rest(31)
            for c in range(4):
                dve.wait_ge(ao_hi, 32 + c + 1)
                dve.tensor_tensor(XL[:, 4 + c, NP:NT], atts[:, c, :], XH[:, 4 + c, NP:NT].bitcast(F32),
                                  ALU.subtract).then_inc(ao_lo, 1)
            projected(OUT1, None, before=True)
            norm(3)
            ffn(UP1, 1)
            norm(4, True)


def kernel(**inputs):
    import numpy as np
    import concourse.bacc as bacc
    from concourse import mybir as mb
    from concourse.bass_utils import run_bass_kernel_spmd

    a = {k: np.asarray(v) for k, v in inputs.items()}
    f32 = np.float32

    def rows(w, kc):
        s = w.reshape(kc, P, -1, P).transpose(2, 1, 0, 3)
        if kc == KD:
            return s
        out = np.zeros((s.shape[0], P, KD, P), f32)
        out[:, :, :kc] = s
        return out

    def feature_major(x, lead=0):
        c = x.shape[-1]
        y = np.moveaxis(x.reshape(x.shape[:-1] + (c // P, P)), (-1, -2), (0, 1))
        return np.ascontiguousarray(y)

    we = a["w_in_even"][0]
    cols = lambda w, o, n: w[:, o:o + n]
    even = [cols(we, 512, 512), cols(we, 0, 512)]
    for jj in range(4):
        for base in (1536, 2048, 1024):
            even.append(cols(we, base + jj * P, P))
    wo = a["w_in_odd"][0]
    ki = cols(wo, 2560, 64)
    wi = np.zeros((D, P), f32)
    wi[:, :HEADS] = cols(wo, 2624, HEADS)
    odd = [cols(wo, 0, 512), cols(wo, 1536, 512), cols(wo, 512, 512), cols(wo, 1024, 512), cols(wo, 2048, 512), ki, ki, wi]

    def ffn_slabs(layer):
        up, down = a["ffn_w_up"][layer], a["ffn_w_down"][layer]
        out, c = [], 0
        for nb in BLOCKS:
            both = [cols(up, half * FC * P + (c + q) * P, P) for q in range(nb) for half in (0, 1)]
            out.append(rows(np.concatenate(both, 1), KD))
            out.append(rows(down[c * P:(c + nb) * P], nb))
            c += nb
        return out

    slab_list = [rows(np.concatenate(even, 1), KD), rows(a["w_out_even"][0], KD), *ffn_slabs(0),
                 rows(np.concatenate(odd, 1), KD), rows(a["w_out_odd"][0], KD), *ffn_slabs(1)]
    slab_array = np.concatenate(slab_list, 0)
    assert slab_array.shape == (SLABS, P, KD, P)

    x = np.concatenate([a["x_prompt"].reshape(NP, D), a["x_sample"].reshape(NS, D)], 0)
    ws = a["a_ws"][0]
    bd = np.zeros((NS, 4, NS), f32)
    for s in range(SEQS):
        bd[DEC * s:DEC * s + DEC, :, DEC * s:DEC * s + DEC] = ws[:, :DEC, :DEC].transpose(2, 0, 1)
    spread = lambda v: np.ascontiguousarray(np.broadcast_to(v, (P,) + v.shape))
    pairs = lambda w: np.stack([w[..., FC * 0 * P:FC * P], w[..., FC * P:]], -2)

    def ffn_order(v):
        y = v.reshape(v.shape[:-1] + (2, FC, P))
        y = np.moveaxis(y, (-1, -2, -3), (0, 1, 2))
        return np.ascontiguousarray(y.reshape((P, 2 * FC) + y.shape[3:]))

    fpar = np.stack([np.concatenate([ffn_order(a["ffn_conv_w"][l]), ffn_order(a["ffn_conv_b"][l][None])], 2) for l in range(2)])
    fhist = np.stack([ffn_order(a["state_ffn_conv"][l]) for l in range(2)])
    lnp = np.stack([np.stack([feature_major(a[f"ln_{k}_{p}"][l]) for p in "gb"], 1)
                    for l in range(2) for k in ("mix", "ffn")], 1)

    pos = np.concatenate([np.arange(NP), np.tile(PAST + np.arange(DEC), SEQS)]).astype(f32)
    rot, halfr = HD // 4, HD // 8
    inv = np.power(f32(500000.0), -np.arange(halfr, dtype=f32) * f32(2.0) / f32(rot)).astype(f32)
    ang = (pos[None, :] * inv[:, None]).astype(f32)
    rc, rs = np.ones((P, NT), f32), np.zeros((P, NT), f32)
    for h in (0, HD):
        rc[h:h + halfr] = rc[h + halfr:h + rot] = np.cos(ang)
        rs[h:h + halfr], rs[h + halfr:h + rot] = -np.sin(ang), np.sin(ang)
    icnt = spread(np.stack([1.0 / np.minimum(w, np.arange(16) + 1.0) for w in (2, 4, 8, 16)]).astype(f32))
    rep = np.zeros((NS, SEQS, HEADS, DEC), f32)
    hsum = np.zeros((4, HEADS, DEC, 2, SEQS, DEC), f32)
    cmask = np.full((SEQS, DEC, SEQS, DEC), BARRED, f32)
    for s in range(SEQS):
        for q in range(DEC):
            rep[DEC * s + q, s, :, q] = 1.0
            hsum[s % 4, :, q, s // 4, s, q] = 1.0
            cmask[s, q, s, :q + 1] = 0.0
    import ml_dtypes

    ck = a["cache_k"][0].transpose(0, 2, 3, 1).reshape(POOLED, 4, P, PAGE).transpose(0, 2, 1, 3)
    kidx = a["cache_kidx"][0].transpose(0, 2, 1)
    arrays = dict(
        slabs=slab_array, xT=feature_major(x), ident=np.eye(P, dtype=f32), identb=np.eye(P).astype(ml_dtypes.bfloat16),
        lng=spread(a["a_ln_g"][0]), lnb=spread(a["a_ln_b"][0]), wsT=ws.transpose(2, 0, 1), bd=bd,
        bsb=spread(a["a_bs"][0]), bw=feature_major(a["b_conv_w"][0]), bh=feature_major(a["state_b_conv"][0]),
        lnp=lnp, fpar=fpar, fhist=fhist, phist=feature_major(a["state_c_pool"][0]), cw=a["c_w"][0].transpose(1, 0, 2),
        csc=feature_major(a["c_scale"][0]), icnt=icnt, rc=rc, rs=rs, rep=rep.reshape(NS, SEQS, NS),
        hsum=hsum.reshape(P, 2, NS), cmask=cmask.reshape(NS, NS),
        iota=np.ascontiguousarray(np.broadcast_to(np.arange(SK, dtype=f32), (NS, SK))),
        ptab=a["page_table"].reshape(1, -1), ck=ck, cv=a["cache_v"][0].reshape(POOLED, PAGE, 512),
        kidx=np.concatenate([kidx, kidx], 1),
    )
    outs = dict(o_y=(P, KD, NT), o_av=(NS, 512), o_bst=(P, 4, 18), o_pst=(P, 4, 9, PH), o_k=(P, 4, NT), o_ki=(IDX, NT),
                o_v=(P, 8, 512), o_vs=(NS, 512), o_fst=(2, P, 2 * FC, 18))

    nc = bacc.Bacc("TRN2", target_bir_lowering=False, num_devices=1, dynamic_dma_scratch_size=1024)
    io, feed = {}, {}
    for name, v in arrays.items():
        v = np.ascontiguousarray(v)
        feed["in_" + name] = v
        io[name] = nc.dram_tensor("in_" + name, v.shape, mb.dt.from_np(v.dtype), kind="ExternalInput").ap()
    for name, shape in outs.items():
        io[name] = nc.dram_tensor("out_" + name, shape, mb.dt.float32, kind="ExternalOutput").ap()
    build(nc, io)
    got = run_bass_kernel_spmd(nc, [feed], core_ids=[0]).results[0]
    r = {name: np.asarray(got["out_" + name]) for name in outs}

    def positions(y):
        y = y.transpose(2, 1, 0).reshape(y.shape[2], -1)
        return y[:NP], y[NP:]

    yp, ys = positions(r["o_y"])
    kp, ks = positions(r["o_k"])
    kip, kis = r["o_ki"].T[:NP], r["o_ki"].T[NP:]
    vp = r["o_v"].transpose(1, 0, 2).reshape(NP, 512)
    b = r["o_bst"].transpose(2, 1, 0).reshape(18, 512)
    c = r["o_pst"].transpose(2, 3, 1, 0).reshape(9, PH, 512)
    f = r["o_fst"].reshape(2, P, FC, 2, 18).transpose(0, 4, 3, 2, 1).reshape(2, 18, 2 * FC * P)
    C = np.ascontiguousarray
    return (C(yp.reshape(1, NP, D)), C(ys.reshape(SEQS, DEC, D)), C(r["o_av"].reshape(1, SEQS, DEC, 512)),
            C(b[:2].reshape(1, 1, 2, 512)), C(b[2:].reshape(1, SEQS, 2, 512)),
            C(c[:1].reshape(1, 1, PH, 512)), C(c[1:].reshape(1, SEQS, PH, 512)),
            C(kp.reshape(1, 1, NP, HEADS, HD)), C(vp.reshape(1, 1, NP, HEADS, HD)), C(kip.reshape(1, 1, NP, IDX)),
            C(ks.reshape(1, SEQS, DEC, HEADS, HD)), C(r["o_vs"].reshape(1, SEQS, DEC, HEADS, HD)),
            C(kis.reshape(1, SEQS, DEC, IDX)),
            C(f[:, :2].reshape(2, 1, 2, 2 * FC * P)), C(f[:, 2:].reshape(2, SEQS, 2, 2 * FC * P)))
```

```python
from contextlib import ExitStack

import concourse.bass as bass
from concourse import mybir

ALU = mybir.AluOpType
ACT = mybir.ActivationFunctionType
AXX = mybir.AxisListType.X
F32 = mybir.dt.float32
F32R = mybir.dt.float32r
BF16 = mybir.dt.bfloat16
I32 = mybir.dt.int32
U32 = mybir.dt.uint32

P = 128
NP = 1024
SEQS, DEC = 8, 4
NS = SEQS * DEC
NT = NP + NS
SB = 96
TC, TW = 3, 352
D = 1024
KD = D // P
FC = 22
HEADS, HD = 8, 64
IDX = 64
PAGES, PAGE = 4, 128
PAST = PAGES * PAGE
POOLED = 40
TOPK_P, TOPK_S = 256, 129
HIST = 2
EXTW = HIST + NP + SEQS * (HIST + DEC)
CW = EXTW - HIST
PH = 15
PEXT = PH + NP + SEQS * (PH + DEC)
ALPHA = 4.0 ** 0.25
EPS = 1e-5
NB3 = KD * TC
BLOCKS = (4, 6, 6, 6)
KIX_EARLY = 5
SK = PAST + NS

IN0, OUT0 = 0, 20
UP0 = OUT0 + KD
FFN_SLABS = 2 * FC + len(BLOCKS) * KD
IN1 = UP0 + FFN_SLABS
OUT1 = IN1 + 22
UP1 = OUT1 + KD
SLABS = UP1 + FFN_SLABS

TAKEN = -3.4e38
BARRED = -3.0e38
FAR = -1.0e30


def build(nc, io):
    with ExitStack() as ctx:
        def sem(name):
            return ctx.enter_context(nc.semaphore(name))

        top = [1152]

        def at(name, shape, dt, offset):
            return nc.alloc_sbuf_tensor_at(name, shape, dt, offset=offset)

        def size(shape, dt):
            n = 2 if dt == BF16 else 4
            for s in shape[1:]:
                n *= s
            return (n + 31) // 32 * 32

        def fixed(name, shape, dt):
            t = at(name, shape, dt, top[0])
            top[0] += size(shape, dt)
            return t

        def region(start, *tensors):
            out = []
            for name, shape, dt in tensors:
                out.append(at(name, shape, dt, start))
                start += size(shape, dt)
            return out, start

        x_off = top[0]
        XH = fixed("XH", [P, KD, NT], F32R)
        xl_off = top[0]
        XL = fixed("XL", [P, KD, NT], F32R)
        z_off = top[0]
        Z = fixed("Z", [P, KD, NT], F32)
        raw_off = top[0]
        RAW = [fixed(f"RAW{j}", [P, KD, P], F32) for j in range(2)]
        wh_off = top[0]
        WH = [fixed(f"WH{j}", [P, KD, P], F32R) for j in range(2)]
        WL = [fixed(f"WL{j}", [P, KD, P], F32R) for j in range(2)]
        ident = fixed("ident", [P, P], F32)
        onesd = fixed("onesd", [P, P], F32)
        lnp = fixed("lnp", [P, 4, 2, KD], F32)
        epst = fixed("epst", [P, 1], F32)
        seed = fixed("seed", [P, 7], F32)
        ptab = fixed("ptab", [1, SEQS * PAGES], I32)
        stats = fixed("stats", [SB, 3, NT // SB], F32)
        wtok = fixed("wtok", [P, 9, HEADS], F32)
        G = top[0]
        END = nc.sbuf_usable_end
        ROW = NT * 4
        T6 = G + 16 * ROW
        W6 = (EXTW * 4 + 31) // 32 * 32
        PAREA = T6 + 6 * W6

        MH = at("MH", [P, KD, NT], F32R, G)
        ML = at("ML", [P, KD, NT], F32R, G + 8 * ROW)
        gv = [at(f"gv{j}", [P, NT], F32, G + j * ROW) for j in range(2)]
        (lng, lnb), _ = region(G + 8 * ROW, ("lng", [P, 512], F32), ("lnb", [P, 512], F32))
        U = at("U", [P, 4, NT], F32, z_off)
        vtok = at("vtok", [P, 8, 512], F32, z_off + 4 * ROW)
        cf = at("cf", [P, NT], F32, T6)
        bext = at("bext", [P, EXTW], F32, T6 + W6)
        bcv = at("bcv", [P, CW], F32, T6 + 2 * W6)
        (vst, vmv, vrs, bh, bd), _ = region(T6 + 3 * W6, ("vst", [P, 9, 6], F32), ("vmv", [P, 9, 2], F32),
                                        ("vrs", [P, 9], F32), ("bh", [P, 4, SEQS, 2], F32), ("bd", [NS, 4, NS], F32))
        (vtoks, wsT, bsb, bw, bst), pend = region(
            PAREA, ("vtoks", [NS, 512], F32), ("wsT", [P, 4, P], F32), ("bsb", [P, 4, P], F32),
            ("bw", [P, 4, 3], F32),
            ("bst", [P, 4, 18], F32))
        assert pend <= END, (pend, END)

        NB = max(BLOCKS)
        HH = at("HH", [P, NB, NT], F32R, G)
        HL = at("HL", [P, NB, NT], F32R, G + NB * ROW)
        (fpar, fhist, fst), fend = region(G + 2 * NB * ROW, ("fpar", [P, 2 * FC, 4], F32),
                                          ("fhist", [P, 2 * FC, SEQS, 2], F32), ("fst", [P, 2 * FC, 18], F32))
        assert fend <= T6
        ext = [at(f"ext{j}", [P, EXTW], F32, T6 + j * W6) for j in range(2)]
        cv = [at(f"cv{j}", [P, CW], F32, T6 + (2 + j) * W6) for j in range(2)]
        sg = at("sg", [P, CW], F32, T6 + 4 * W6)
        hf = at("hf", [P, NT], F32, T6 + 5 * W6)

        zs = at("zs", [P, NT], F32, T6 + 2 * W6)
        zq = at("zq", [P, NT], F32, T6 + 3 * W6)
        sq = at("sq", [P, NT], F32, T6 + 4 * W6)
        mean = at("mean", [P, NT], F32, T6)
        rstd = at("rstd", [P, NT], F32, T6 + W6)
        drstd = at("drstd", [SB, NT // SB, SB], F32, T6 + 5 * W6)

        (Q, K, VT, VS, KI), qi_off = region(
            G, ("Q", [P, 4, NT], F32), ("K", [P, 4, NT], F32), ("VT", [P, 8, 512], F32),
            ("VS", [NS, 512], F32), ("KI", [P, NT], F32))
        QI = at("QI", [P, 4, NT], F32, qi_off)
        E0 = qi_off + 4 * ROW
        (RC, RS, qf0, qf1, sh, cw, csc, icnt), eend = region(
            E0, ("RC", [P, NT], F32), ("RS", [P, NT], F32), ("qf0", [P, NT], F32), ("qf1", [P, NT], F32),
            ("sh", [P, NT], F32), ("cw", [P, 4, P], F32), ("csc", [P, 4], F32), ("icnt", [P, 4, 16], F32))
        assert eend <= END, (eend, END)
        qf = [qf0, qf1]
        (pe0, pe1, pe2), pe_end = region(E0, *[(f"pe{j}", [P, PEXT], F32) for j in range(3)])
        assert pe_end <= E0 + 5 * ROW
        (phist, pst), _ = region(z_off + 4 * ROW, ("phist", [P, 4, SEQS, PH], F32),
                                 ("pst", [P, 4, 9, PH], F32))
        MB = at("MB", [P, 36 * P], BF16, E0)
        r0_off = E0 + 21 * P * 2
        (R0, SC45), sc67_off = region(r0_off, ("R0", [P, NP], F32), ("SC45", [P, 11 * P], F32))
        (SC23, R1), _ = region(sc67_off, ("SC23", [P, 7 * P], F32), ("R1", [P, 6 * P], F32))
        SC67 = at("SC67", [P, 15 * P], F32, sc67_off)
        (m8a, m8b, identb, nmx, psm, prc, atts), ie = region(
            E0 + 36 * P * 2 + 4 * 4096, ("m8a", [P, 8], F32), ("m8b", [P, 8], F32), ("identb", [P, P], BF16), ("nmx", [P, 2], F32),
            ("psm", [P, 2], F32), ("prc", [P, 2], F32), ("atts", [P, 4, NS], F32))
        assert ie <= END, (ie, END)
        SC = {2: SC23[:, 0:3 * P], 3: SC23[:, 3 * P:7 * P], 4: SC45[:, 0:5 * P], 5: SC45[:, 5 * P:11 * P],
              6: SC67[:, 0:7 * P], 7: SC67[:, 7 * P:15 * P]}
        m8 = [m8a, m8b]

        def products(t):
            return (R0 if t >= 32 else (R0, R1)[t % 2])[:, 0:P * (3 + t // 8)]

        PR = [at(f"PR{j}", [P, NP], F32, wh_off + j * 4096) for j in range(2)]
        PT = [at(f"PT{j}", [P, 8, P], F32, wh_off + (2 + j) * 4096) for j in range(2)]
        QB = at("QB", [P, 4, SEQS, NS], F32, raw_off)
        (sp_, spt, rep), se = region(raw_off + 4096, ("sp", [P, SK], F32), ("spt", [P, 5, NS], F32),
                                     ("rep", [NS, SEQS, NS], BF16))
        assert se <= wh_off
        sbias = at("sbias", [NS, SK], BF16, wh_off + 3 * 4096)
        (kix_a, ), zu_end = region(z_off + 4 * ROW + 1920 + 2176, ("kix_a", [P, KIX_EARLY, PAST], F32))
        assert zu_end <= z_off + 8 * ROW
        (QIB, ), _ = region(E0 + ROW, ("QIB", [P, SEQS, NS], F32))
        (ra, rb, ssc, iota, kix_b, hsum, cmask, wrow, sidx, sidf, s8), se = region(
            wh_off, ("ra", [P, SK], F32), ("rb", [P, SK], F32), ("ssc", [NS, SK], F32), ("iota", [NS, SK], F32),
            ("kix_b", [P, SEQS - KIX_EARLY, PAST], F32), ("hsum", [P, 2, NS], F32), ("cmask", [NS, NS], F32),
            ("wrow", [P, 2], F32), ("sidx", [NS, 8], U32), ("sidf", [NS, 1], F32), ("s8", [NS, 8], F32))
        assert se <= wh_off + 4 * 4096, se - wh_off
        kix = [kix_a[:, s, :] for s in range(KIX_EARLY)] + [kix_b[:, s, :] for s in range(SEQS - KIX_EARLY)]
        rab = [ra, rb]
        KP = [at(f"KP{j}", [P, 4, PAST], F32, o + 4 * ROW) for j, o in enumerate((xl_off, x_off))]
        VP = [at(f"VP{j}", [P, PAGES, 512], F32, o + 4 * ROW + 8192) for j, o in enumerate((xl_off, x_off))]

        PS = ctx.enter_context(nc.psum_tensor("PS", [P, 8, 512], F32))

        def bank_set(j):
            return PS[:, 3 * j:3 * j + 3, 0:TW]

        def turn_bank(f):
            return PS[:, 6 + f % 2, :]

        wis = nc.dram_tensor("wi_rows", (SEQS, HEADS, DEC), F32, kind="Internal").ap()

        loaded = [sem("slab_loaded0"), sem("slab_loaded1")]
        w_hi, w_lo = sem("slab_high_split"), sem("slab_rest_split")
        mm_done = sem("slab_multiplied")
        evac_done = [sem("banks_emptied0"), sem("banks_emptied1")]
        consts_in, mix_in = sem("consts_in"), sem("mixer_params_in")
        x_in = [sem(f"x_in{k}") for k in range(KD)]
        x_hi, x_lo = sem("x_high"), sem("x_rest")
        turned, turn_evac = sem("turned"), sem("turned_emptied")
        vstat, vagg, vsd, vln, vnorm = (sem(n) for n in ("v_stats", "v_aggregated", "v_deviation", "v_ln_step", "v_normed"))
        masked = sem("gate_weights_masked")
        gate_f, mix_hi, mix_lo = sem("mix_rows"), sem("mix_high"), sem("mix_rest")
        bhist, btap, bconv, bstd = sem("b_history"), sem("b_tap"), sem("b_conv"), sem("b_state")
        z_pre, sq_done, zs_done, zq_done = (sem(n) for n in ("z_input", "z_squared", "z_summed", "squares_summed"))
        ln_mean, ln_sq, ln_m, ln_var, ln_sd, ln_rstd, ln_diag, ln_mb, ln_rb, ln_a, ln_sub, ln_d, ln_z = (
            sem("ln_" + n) for n in ("mean", "meansq", "mean_kept", "var", "dev", "rstd", "diagonals", "mean_spread",
                                     "rstd_spread", "copies", "centred", "scaled", "out"))
        fpar_in, ext_hist, tap, conv_done, st_done, silu_done, hmul, h_hi, h_lo = (
            sem("ffn_" + n) for n in ("params_in", "history", "tap", "conv", "state", "silu", "hidden", "hidden_high", "hidden_rest"))
        out_done = sem("outputs_written")
        fst_out = sem("ffn_state_written")
        rope_in, l1_in, phist_in, phist_set, pwin, pooled, pst_set, pst_out = (
            sem(n) for n in ("rope_tables_in", "l1_params_in", "pool_history_in", "pool_history_set", "pool_window",
                             "pooled", "pool_state_set", "pool_state_written"))
        ln_own = sem("ln_centred_by_dve")
        z_up = sem("z_upper_input")
        sv_kept, sv_turned = sem("sa_values_kept"), sem("sa_values_turned")
        weighted = sem("i_weighted")
        pool_zero = sem("pool_row_cleared")
        shuf, shufs, rcos, roped = (sem(n) for n in ("rope_partner", "rope_sine", "rope_cosine", "rope_done"))
        cmm, c_hi, cevac = sem("c_multiplied"), sem("c_high"), sem("c_rest")
        wi_out, wi_in, identb_in = sem("wi_rows_out"), sem("wi_rows_in"), sem("bf16_identity_in")
        sconst_in, qib_zero, qib_set, pt_in = (sem(n) for n in ("sample_consts_in", "qib_cleared", "qib_set", "page_table_in"))
        kix_in = [sem("index_pages_early"), sem("index_pages_late")]
        sdot, srelu, ssum, ssc_set, stop_, sidx_set, sb_set = (
            sem("s_" + n) for n in ("dots", "relu", "head_sums", "scores", "top", "last", "bias"))
        dot_mm, dot_relu, sc_acc, sc_barred, top_, mb_set, mb_early = (
            sem("i_" + n) for n in ("dots", "relu", "scores", "barred", "top", "bias", "causal_bias"))
        k_in = [sem("key_pages_in0"), sem("key_pages_in1")]
        v_in = [sem("value_pages_in0"), sem("value_pages_in1")]
        qb_zero, qb_set = sem("qb_cleared"), sem("qb_set")
        slg, smax, sexp, ssump, snorm, stp, ste, spv, satt = (
            sem("sa_" + n) for n in ("logits", "max", "exp", "rsum", "probs", "turned", "probs_turned", "values", "out"))
        lg, amax, aexp, asum, anorm, atp, ate, apv, ao_hi, ao_lo = (
            sem("pa_" + n) for n in ("logits", "max", "exp", "rsum", "probs", "turned", "probs_turned", "values", "high", "rest"))
        kv_out = sem("kv_written")

        block = ctx.enter_context(nc.Block())

        def val(i, per, base):
            return base if i is None else i * per + base

        def wait_emptied(eng, n, i=None, per=0):
            eng.wait_ge(evac_done[n % 2], val(i, per // 2, n // 2 + 2))

        def three(ap):
            return ap.rearrange("p (c t) -> p c t", c=TC)

        def row_of(t, index):
            return t[:, bass.ds(index, 1), :].rearrange("p a t -> p (a t)")

        def third(t, index, c):
            return t[:, bass.ds(index, 1), c * TW:(c + 1) * TW].rearrange("p a t -> p (a t)")

        def sample_cols(row, first, width, n):
            a = first + NP
            return row[:, a:a + SEQS * width].rearrange("p (s w) -> p s w", s=SEQS)[:, :, width - n:width]

        def parts(row, hist=0):
            return [row[:, hist:hist + 2 * TW].rearrange("p (c t) -> p c t", c=2),
                    row[:, hist + 2 * TW:hist + NP],
                    sample_cols(row, hist, hist + DEC, DEC)]

        def bank_parts(j):
            bank = bank_set(j)
            return [bank[:, 0:2, :], bank[:, 2, 0:NP - 2 * TW],
                    bank[:, 2, NP - 2 * TW:TW].rearrange("p (s q) -> p s q", s=SEQS)]

        def pair(p, n, rows=P):
            return PS[0:rows, 2 * p:2 * p + 2, :].rearrange("p b t -> p (b t)")[:, 0:n]

        def logits_of(e):
            n = P * (e // 8 + 1)
            if n <= 512:
                return PS[:, e % 2, 0:n]
            return pair(e % 2 if e >= TWO_PAIRS else 0, n)

        def sample_logits_of(s):
            return pair(3 * (s % 2), SK, NS)

        def mask_cols(b):
            return slice(P * b * (b + 1) // 2, P * (b + 1) * (b + 2) // 2)

        SLOTS = SEQS + 64
        BEST = TOPK_P // 8
        GROUPS = ((2, 3), (4, 5), (6, 7))
        ROUNDS = len(GROUPS) * 2 * BEST
        per_slot = [3] + [13] * 7 + [2] * 16 + [2] * 16 + [2] * 14 + [3] * 2 + [0] * 17
        start_round = [sum(per_slot[:k]) for k in range(SLOTS + 1)]
        assert start_round[SLOTS] == ROUNDS
        assert all(start_round[SEQS + 8 * blocks[0]] >= 2 * BEST * (g + 1) for g, blocks in enumerate(GROUPS))

        def dot_round(t):
            return 4 * (t - 16)

        def slot_dots(k):
            return [t for t in range(16, 48) if k < SLOTS and start_round[k] <= dot_round(t) < start_round[k + 1]]

        TWO_PAIRS = min(e for e in range(32, 64, 8) if not any(slot_dots(k) for k in range(SEQS + e, SLOTS)))

        @block.sync
        def _(sp):
            sp.dma_start(RAW[0][:, :, :], io["slabs"][0]).then_inc(loaded[0], 16)
            for k in range(1, KD, 2):
                sp.dma_start(Z[:, k, :], io["xT"][:, k, :]).then_inc(x_in[k], 16)
            sp.dma_start(RAW[1][:, :, :], io["slabs"][1]).then_inc(loaded[1], 16)
            for dst, name in ((lng[:, :], "lng"), (lnb[:, :], "lnb"), (wsT[:, :, :], "wsT"), (bd[:, :, :], "bd"),
                              (bsb[:, :, :], "bsb"), (bw[:, :, :], "bw"), (bh[:, :, :, :], "bh"), (lnp[:, :, :, :], "lnp")):
                sp.dma_start(dst, io[name]).then_inc(mix_in, 16)

            def stream(first, last):
                with sp.Fori(0, (last - first) // 2) as i:
                    for j in range(2):
                        sp.wait_ge(w_hi, i * 2 + (first + j - 1))
                        sp.wait_ge(w_lo, i * 2 + (first + j - 1))
                        sp.dma_start(RAW[j][:, :, :],
                                     io["slabs"][bass.ds(i * 2 + (first + j), 1)].rearrange("a p k n -> p (a k) n")
                                     ).then_inc(loaded[j], 16)

            stream(2, OUT1)
            sp.wait_ge(pt_in, 16)

            def page_entry(s, g):
                return bass.ds(s * PAGES + g, 1)

            def page(s, g):
                return sp.value_load(ptab[0:1, page_entry(s, g)], min_val=0, max_val=POOLED - 1)

            def index_pages(late, s):
                for g in range(PAGES):
                    pg = page(s, g)
                    sp.dma_start(kix[s][:, g * PAGE:(g + 1) * PAGE],
                                 io["kidx"][bass.ds(pg, 1)].rearrange("a p s -> p (a s)")).then_inc(kix_in[late], 16)

            for s in range(KIX_EARLY):
                index_pages(0, s)
            sp.wait_ge(mm_done, OUT1)
            for s in range(KIX_EARLY, SEQS):
                index_pages(1, s)
            sp.wait_ge(z_up, 4)

            def key_pages(i, s):
                for g in range(PAGES):
                    pg = page(val(i, 2, s), g)
                    sp.dma_start(KP[s % 2][:, :, g * PAGE:(g + 1) * PAGE],
                                 io["ck"][bass.ds(pg, 1)].rearrange("a p c s -> p (a c) s")).then_inc(k_in[s % 2], 16)

            def value_pages(i, s):
                for g in range(PAGES):
                    pg = page(val(i, 2, s), g)
                    sp.dma_start(VP[s % 2][:, g, :],
                                 io["cv"][bass.ds(pg, 1)].rearrange("a p c -> p (a c)")).then_inc(v_in[s % 2], 16)

            key_pages(None, 0)
            value_pages(None, 0)
            key_pages(None, 1)
            value_pages(None, 1)
            for s in range(2, SEQS):
                sp.wait_ge(slg, s - 1)
                key_pages(None, s)
                sp.wait_ge(spv, s - 1)
                value_pages(None, s)
            sp.wait_ge(spv, SEQS)
            stream(OUT1, SLABS)

        @block.tensor
        def _(pe):
            def slab_chunk(j, k, hi, lo, first, last):
                for c in range(TC):
                    o = bank_set(j)[:, c, :]
                    pe.matmul(o, WH[j][:, k, :], hi[:, k, c * TW:(c + 1) * TW], start=first, stop=False)
                    pe.matmul(o, WH[j][:, k, :], lo[:, k, c * TW:(c + 1) * TW], start=False, stop=False)
                for c in range(TC):
                    mm = pe.matmul(bank_set(j)[:, c, :], WL[j][:, k, :], hi[:, k, c * TW:(c + 1) * TW],
                                   start=False, stop=last)
                return mm

            def slab(n, kc, hi, lo, i=None, per=0, order=None, wait_k=None):
                j = n % 2
                pe.wait_ge(w_lo, val(i, per, n + 1))
                pe.wait_ge(evac_done[j], val(i, per // 2, n // 2 + 1))
                ks = list(order or range(kc))
                for k in ks:
                    if wait_k and k in wait_k:
                        pe.wait_ge(*wait_k[k])
                    mm = slab_chunk(j, k, hi, lo, k == ks[0], k == ks[-1])
                mm.then_inc(mm_done, 1)

            def slabs(first, count, kc, hi, lo, order=None):
                with pe.Fori(0, count // 2) as i:
                    for j in range(2):
                        slab(first + j, kc, hi, lo, i, 2, order)

            def turn(row, f, i=None, per=0):
                pe.wait_ge(consts_in, 16)
                for part in range(3):
                    pe.wait_ge(turn_evac, val(i, per, f + part + 1))
                    for b in range(4 if part < 2 else 1):
                        t = part * 4 + b
                        w = P if t < 8 else NS
                        mm = pe.transpose(turn_bank(f + part)[0:w, b * P:(b + 1) * P], row[:, t * P:t * P + w], ident[:, :])
                    mm.then_inc(turned, 1)

            def turned_slabs(first, f, rows):
                with pe.Fori(0, 2) as i:
                    for j in range(2):
                        slab(first + j, KD, XH, XL, i, 2, wait_k=None if first or j else {k: (x_lo, k + 1) for k in range(KD)})
                    for j in range(2):
                        wait_emptied(pe, first + j, i, 2)
                        turn(rows[j], f + 3 * j, i, 6)

            def lead_slabs(n, l):
                for j in range(2):
                    pe.wait_ge(w_lo, n + j + 1)
                    pe.wait_ge(evac_done[j], n // 2 + 1)
                for c in range(TC):
                    cols = slice(c * TW, (c + 1) * TW)
                    for j in range(2):
                        pe.wait_ge(ln_a, 4 * (l - 1) + (4 if j else 1))
                        o = bank_set(j)[:, c, :]
                        for k in range(KD):
                            if j == 0:
                                pe.wait_ge(x_lo, KD + NB3 * (l - 1) + KD * c + k + 1)
                            pe.matmul(o, WH[j][:, k, :], XH[:, k, cols], start=(k == 0), stop=False)
                            pe.matmul(o, WH[j][:, k, :], XL[:, k, cols], start=False, stop=False)
                            mm = pe.matmul(o, WL[j][:, k, :], XH[:, k, cols], start=False, stop=(k == KD - 1))
                        if c == TC - 1:
                            mm.then_inc(mm_done, 1)

            def norm_sums(l, n):
                def sums(bank, total, done):
                    for t in range(NT // SB):
                        mm = pe.matmul(PS[0:SB, bank, t:t + 1], total[:, t * SB:(t + 1) * SB], onesd[:, 0:1],
                                       start=True, stop=True)
                    mm.then_inc(done, 1)

                pe.wait_ge(zs_done, 9 * l)
                wait_emptied(pe, n - 2)
                for c in range(TC):
                    mm = pe.matmul(bank_set(0)[:, c, :], onesd[:, :], zs[:, c * TW:(c + 1) * TW], start=True, stop=True)
                mm.then_inc(ln_mb, 1)
                sums(6, zs, ln_mean)
                pe.wait_ge(zq_done, 9 * l)
                sums(7, zq, ln_sq)
                wait_emptied(pe, n - 1)
                pe.wait_ge(ln_diag, l)
                for c in range(TC):
                    pe.matmul(bank_set(1)[:, c, :], onesd[0:SB, :],
                              drstd[:, :, :].rearrange("p t s -> p (t s)")[:, c * TW:(c + 1) * TW],
                              start=True, stop=True).then_inc(ln_rb, 1)

            def ffn(first, layer):
                n, chunks = first, layer * FC
                for bi, nb in enumerate(BLOCKS):
                    if bi == 0:
                        lead_slabs(n, 2 * layer + 1)
                        slabs(n + 2, 2 * nb - 2, KD, XH, XL)
                    else:
                        slabs(n, 2 * nb, KD, XH, XL)
                    n += 2 * nb
                    chunks += nb
                    for ks in (range(nb - 2), range(nb - 2, nb)):
                        for j in range(2):
                            if ks[0] == 0:
                                pe.wait_ge(w_lo, n + j + 1)
                                pe.wait_ge(evac_done[j], n // 2 + 1)
                                pe.wait_ge(h_lo, chunks - 2)
                            for k in ks:
                                if ks[0] and j == 0:
                                    pe.wait_ge(h_lo, chunks - nb + k + 1)
                                mm = slab_chunk(j, k, HH, HL, k == 0, k == nb - 1)
                            if ks[0]:
                                mm.then_inc(mm_done, 1)
                    slabs(n + 2, KD - 2, nb, HH, HL)
                    n += KD

            turned_slabs(0, 0, gv)
            slabs(4, 4, KD, XH, XL)
            pe.wait_ge(vnorm, 9)
            pe.wait_ge(masked, 2)
            for g in range(4):
                for part in range(3):
                    f = 12 + 3 * g + part
                    pe.wait_ge(turn_evac, f + 1)
                    o = turn_bank(f)
                    for b in range(4 if part < 2 else 1):
                        if part < 2:
                            mm = pe.matmul(o[:, b * P:(b + 1) * P], vtok[:, part * 4 + b, g * P:(g + 1) * P],
                                           wsT[:, g, :], start=True, stop=True)
                        else:
                            mm = pe.matmul(o[:, 0:NS], vtoks[:, g * P:(g + 1) * P], bd[:, g, :], start=True, stop=True)
                    mm.then_inc(turned, 1)
            slabs(8, 12, KD, XH, XL)
            pe.wait_ge(mix_lo, KD)
            slabs(OUT0, KD, KD, MH, ML, order=[4, 5, 6, 7, 0, 1, 2, 3])
            norm_sums(1, UP0)
            ffn(UP0, 0)
            norm_sums(2, IN1)
            lead_slabs(IN1, 2)
            slabs(IN1 + 2, 2, KD, XH, XL)
            turned_slabs(IN1 + 4, 24, qf)
            slabs(IN1 + 8, 14, KD, XH, XL)
            wait_emptied(pe, OUT1 - 1)
            pe.wait_ge(turn_evac, 37)
            for t in range(8):
                mm = pe.transpose(turn_bank(36)[:, t * HEADS:(t + 1) * HEADS], qf[1][0:HEADS, t * P:(t + 1) * P],
                                  ident[0:HEADS, 0:HEADS])
            mm.then_inc(turned, 1)
            def sample_dots(s):
                o = PS[32 * (s % 4):32 * (s % 4) + 32, :, :]
                pe.matmul(o[:, 6, :], QIB[:, s, :], kix[s], start=True, stop=True)
                pe.matmul(o[:, 7, 0:NS], QIB[:, s, :], KI[:, NP:NT], start=True, stop=True).then_inc(sdot, 1)

            pe.wait_ge(turn_evac, 39)
            pe.wait_ge(qib_set, 8)
            pe.wait_ge(kix_in[0], 64 * KIX_EARLY)
            for s in range(4):
                sample_dots(s)
            pe.wait_ge(l1_in, 48)
            wait_emptied(pe, OUT1 - 2)
            for g in range(4):
                if g >= 2:
                    pe.wait_ge(cevac, g - 1)
                else:
                    pe.wait_ge(pooled, 4)
                for c in range(TC):
                    mm = pe.matmul(bank_set(g % 2)[:, c, :], cw[:, g, :], Z[:, g, c * TW:(c + 1) * TW], start=True, stop=True)
                mm.then_inc(cmm, 1)
            pe.wait_ge(srelu, 1)
            sample_dots(4)
            pe.wait_ge(kix_in[1], 64 * (SEQS - KIX_EARLY))
            for s in range(5, SEQS):
                sample_dots(s)
            pe.wait_ge(sconst_in, 64)
            pe.wait_ge(srelu, 2)
            for half, cols in ((6, slice(0, PAST)), (7, slice(PAST, SK))):
                for g in range(2):
                    mm = pe.matmul(PS[0:NS, half, 0:cols.stop - cols.start], hsum[:, g, :], rab[g][:, cols],
                                   start=(g == 0), stop=(g == 1))
            mm.then_inc(ssum, 1)
            def dots(t):
                b, h = 2 + t // 8, t % 8
                n = P * (b + 1)
                two = n > 512
                if t >= 1 + (not two):
                    pe.wait_ge(dot_relu, t if two else t - 1)
                half = slice(64 * (h % 2), 64 * (h % 2) + 64)
                for a in range(0, n, 512):
                    w = min(512, n - a)
                    bank = 2 + (a // 512 if two else t % 2)
                    mm = pe.matmul(PS[:, bank, 0:w], QI[half, h // 2, b * P:(b + 1) * P],
                                   KI[half, a:a + w], start=True, stop=True)
                mm.then_inc(dot_mm, 1)

            def sample_logits(s):
                pe.wait_ge(k_in[s % 2], 64 * (s // 2 + 1))
                if s >= 2:
                    pe.wait_ge(sexp, s - 1)
                both = sample_logits_of(s)
                for o, keys, bias in ((both[:, 0:PAST], lambda c: KP[s % 2][:, c, :], sbias[:, 0:PAST]),
                                      (both[:, PAST:SK], lambda c: K[:, c, NP:NT], sbias[:, PAST:SK])):
                    for c in range(4):
                        pe.matmul(o, QB[:, c, s, :], keys(c), start=(c == 0), stop=False)
                    mm = pe.matmul(o, rep[:, s, :], bias, start=False, stop=True)
                mm.then_inc(slg, 1)

            def sample_turn(s):
                pe.wait_ge(snorm, s + 1)
                if s >= 1:
                    pe.wait_ge(ste, 2 * s)
                for t in range(5):
                    w = P if t < 4 else NS
                    mm = pe.transpose(PS[0:w, 4, t * NS:(t + 1) * NS], sp_[0:NS, t * P:t * P + w], ident[0:NS, 0:NS])
                mm.then_inc(stp, 1)

            def sample_values(s):
                pe.wait_ge(ste, 2 * (s + 1))
                pe.wait_ge(v_in[s % 2], 64 * (s // 2 + 1))
                if s == 4:
                    pe.wait_ge(satt, 8)
                o = PS[32 * (s % 4):32 * (s % 4) + 32, 5, :]
                for t in range(4):
                    pe.matmul(o, spt[:, t, :], VP[s % 2][:, t, :], start=(t == 0), stop=False)
                pe.matmul(o, spt[0:NS, 4, :], VS[:, :], start=False, stop=True).then_inc(spv, 1)

            def sample_values_turn(g):
                pe.wait_ge(sv_kept, g + 1)
                for c in range(4):
                    mm = pe.transpose(PS[:, 5, c * P:(c + 1) * P], PR[1][:, c * P:(c + 1) * P], ident[:, :])
                mm.then_inc(sv_turned, 1)

            def logits(e):
                b, h = e // 8, e % 8
                n = P * (b + 1)
                half = slice(64 * (h % 2), 64 * (h % 2) + 64)
                if e == 0:
                    pe.wait_ge(sexp, SEQS - 1)
                    pe.wait_ge(mb_early, 2)
                elif P * (b + 1) > 512 and e <= TWO_PAIRS:
                    pe.wait_ge(aexp, e)
                elif e >= 2:
                    pe.wait_ge(aexp, e - 1)
                if e == TWO_PAIRS + 1:
                    pe.wait_ge(dot_relu, 48)
                if b >= 2 and h == 0:
                    pe.wait_ge(mb_set, b - 1)
                for a in range(0, n, 512):
                    w = min(512, n - a)
                    o = logits_of(e)[:, a:a + w]
                    pe.matmul(o, Q[half, h // 2, b * P:(b + 1) * P], K[half, h // 2, a:a + w], start=True, stop=False)
                    m = mask_cols(b)
                    mm = pe.matmul(o, identb[:, :], MB[:, m.start + a:m.start + a + w], start=False, stop=True)
                mm.then_inc(lg, 1)

            def turn_probs(e):
                b = e // 8
                pe.wait_ge(anorm, e + 1)
                if e >= 1:
                    pe.wait_ge(ate, e)
                else:
                    pe.wait_ge(ste, 2 * SEQS)
                for t in range(b + 1):
                    mm = pe.transpose(PS[:, 4 + t // 4, (t % 4) * P:(t % 4 + 1) * P], PR[e % 2][:, t * P:(t + 1) * P],
                                      ident[:, :])
                mm.then_inc(atp, 1)

            def values(e):
                b, h = e // 8, e % 8
                pe.wait_ge(ate, e + 1)
                if e >= 4 and e % 2 == 0:
                    pe.wait_ge(ao_lo, e // 2 - 1)
                o = PS[64 * (h % 2):64 * (h % 2) + 64, 6 + (e // 2) % 2, 0:P]
                for t in range(b + 1):
                    mm = pe.matmul(o, VT[:, t, h * HD:(h + 1) * HD], PT[e % 2][:, t, :], start=(t == 0), stop=(t == b))
                mm.then_inc(apv, 1)

            for t in range(16):
                dots(t)
            pe.wait_ge(qb_set, 8)
            pe.wait_ge(sb_set, 2)
            pe.wait_ge(identb_in, 16)
            def early(k):
                return SEQS + TWO_PAIRS + 1 < k < SLOTS

            for k in range(SLOTS + 1):
                if k < SLOTS and not early(k):
                    sample_logits(k) if k < SEQS else logits(k - SEQS)
                if k >= 1:
                    sample_turn(k - 1) if k <= SEQS else turn_probs(k - 1 - SEQS)
                if early(k + 1):
                    logits(k + 1 - SEQS)
                for t in slot_dots(k):
                    dots(t)
                if k in (5, 9):
                    sample_values_turn(k // 4 - 1)
                if k >= 1:
                    sample_values(k - 1) if k <= SEQS else values(k - 1 - SEQS)
            pe.wait_ge(ao_lo, 32 + 4)
            slabs(OUT1, KD, KD, XH, XL)
            norm_sums(3, UP1)
            ffn(UP1, 1)
            norm_sums(4, SLABS)

        @block.scalar
        def _(act):
            for k in range(0, KD, 2):
                act.dma_start(Z[:, k, :], io["xT"][:, k, :]).then_inc(x_in[k], 16)
            act.dma_start(ident[:, :], io["ident"]).then_inc(consts_in, 16)

            def split_high(n, i=None, per=0):
                j = n % 2
                act.wait_ge(loaded[j], val(i, per * 8, 16 * (n // 2 + 1)))
                act.activation(WH[j][:, :, :], RAW[j][:, :, :], ACT.Copy).then_inc(w_hi, 1)

            split_high(0)
            for k in range(KD):
                if k == 4:
                    split_high(1)
                act.wait_ge(x_in[k], 16)
                act.activation(XH[:, k, :], Z[:, k, :], ACT.Copy).then_inc(x_hi, 1)

            def split_ahead(n):
                if n + 2 < OUT1:
                    split_high(n + 2)

            def copied_slabs(first, count, rows, func=ACT.Copy, scale=1.0, free=None):
                with act.Fori(0, count // 2) as i:
                    for j in range(2):
                        act.wait_ge(mm_done, i * 2 + (first + j + 1))
                        if free:
                            act.wait_ge(*free(i, j))
                        act.activation(three(rows(i, j)), bank_set((first + j) % 2), func, scale=scale).then_inc(
                            evac_done[(first + j) % 2], 1)
                        split_high(first + j + 2, i, 2)

            copied_slabs(0, 4, lambda i, j: gv[j][:, :], ACT.Gelu_apprx_tanh)
            act.wait_ge(x_lo, KD)
            copied_slabs(4, 2, lambda i, j: row_of(U, i * 2 + j), ACT.Gelu_apprx_tanh)
            act.wait_ge(vagg, 9)
            act.activation(vrs[:, 0:8], vmv[:, 0:8, 1], ACT.Sqrt, bias=epst[:, :]).then_inc(vsd, 1)
            act.activation(vrs[0:NS, 8:9], vmv[0:NS, 8, 1:2], ACT.Sqrt, bias=epst[0:NS, :]).then_inc(vsd, 1)
            copied_slabs(6, 2, lambda i, j: row_of(U, i * 2 + (2 + j)), ACT.Gelu_apprx_tanh)

            for g in range(4):
                act.wait_ge(gate_f, g + 1)
                act.activation(MH[:, g, :], cf[:, :], ACT.Copy).then_inc(mix_hi, 1)
            act.wait_ge(vnorm, 9)
            act.dma_start(io["o_av"], vtoks[:, :]).then_inc(out_done, 16)
            for jj in range(4):
                n = 8 + 3 * jj
                act.wait_ge(mm_done, n + 1)
                act.wait_ge(mix_lo, 4 + jj)
                act.activation(three(cf[:, :]), bank_set(n % 2), ACT.Copy).then_inc(evac_done[n % 2], 1)
                split_high(n + 2)
                for d in (1, 2):
                    act.wait_ge(mm_done, n + d + 1)
                    split_high(n + d + 2)
                wait_emptied(act, n + 2)
                act.activation(MH[:, 4 + jj, :], cf[:, :], ACT.Copy).then_inc(mix_hi, 1)
            act.wait_ge(bstd, 5)
            act.dma_start(io["o_bst"], bst[:, :, :]).then_inc(out_done, 16)

            def squares(l, first):
                def step(i, m, more=True):
                    act.wait_ge(mm_done, val(i, 2, first + m + 1))
                    if more:
                        split_high(first + m + 2, i, 2)
                    wait_emptied(act, first + m, i, 2)
                    act.wait_ge(zq_done, val(i, 2, 9 * (l - 1) + m + 1))
                    act.activation(sq[:, :], row_of(Z, val(i, 2, m)), ACT.Square).then_inc(sq_done, 1)

                more = first + KD < SLABS
                with act.Fori(0, KD // 2 - 1) as i:
                    for j in range(2):
                        step(i, j)
                step(None, KD - 2, more)
                step(None, KD - 1, more)
                act.activation(seed[:, 6:7], epst[:, :], ACT.Sqrt)

            def norm(l, last=False):
                act.wait_ge(ln_mb, l)
                act.activation(three(mean[:, :]), bank_set(0), ACT.Copy).then_inc(ln_a, 1)
                act.wait_ge(ln_var, 3 * l)
                act.activation(stats[:, 2, :], stats[:, 2, :], ACT.Sqrt, bias=epst[0:SB, :]).then_inc(ln_sd, 1)
                for c in range(TC):
                    act.wait_ge(ln_rb, TC * (l - 1) + c + 1)
                    act.activation(rstd[:, c * TW:(c + 1) * TW], bank_set(1)[:, c, :], ACT.Copy,
                                   scale=float(D)).then_inc(ln_a, 1)
                for c in range(TC):
                    at0 = NB3 * (l - 1) + KD * c
                    for half in range(2):
                        with act.Fori(0, KD // 4) as i:
                            for j in range(2):
                                m = i * 2 + (4 * half + j)
                                z = third(Z, m, c)
                                act.wait_ge(ln_d, i * 2 + (at0 + 4 * half + j + 1))
                                gain, shift = (lnp[:, l - 1, x, bass.ds(m, 1)] for x in range(2))
                                if last:
                                    act.activation(z, z, ACT.Identity, scale=gain, bias=shift).then_inc(ln_z, 1)
                                else:
                                    act.activation(third(XL, m, c).bitcast(F32), z, ACT.Identity, scale=gain, bias=shift)
                                    act.activation(third(XH, m, c), z, ACT.Identity, scale=gain, bias=shift).then_inc(x_hi, 1)
                        if last:
                            act.wait_ge(ln_z, KD * c + 4 * half + 4)
                            rows, cols = slice(4 * half, 4 * half + 4), slice(c * TW, (c + 1) * TW)
                            act.dma_start(io["o_y"][:, rows, cols], Z[:, rows, cols]).then_inc(out_done, 16)

            def ffn(first, layer):
                act.wait_ge(mm_done, first)
                act.dma_start(fpar[:, :, :], io["fpar"][layer]).then_inc(fpar_in, 16)
                act.dma_start(fhist[:, :, :, :], io["fhist"][layer]).then_inc(fpar_in, 16)
                norm(2 * layer + 1)
                n, u, q = first, layer * 2 * FC, layer * FC
                for bi, nb in enumerate(BLOCKS):
                    with act.Fori(0, nb // 2) as i:
                        for pp in range(2):
                            for j in range(2):
                                s = 2 * pp + j
                                act.wait_ge(mm_done, i * 4 + (n + s + 1))
                                act.wait_ge(conv_done, i * 4 + (u + s + 1))
                                act.wait_ge(st_done, i * 4 + (u + s + 1))
                                for dst, src_ in zip(parts(ext[j], HIST), bank_parts(j)):
                                    ins = act.activation(dst, src_, ACT.Copy)
                                ins.then_inc(evac_done[j], 1)
                                split_high(n + s + 2, i, 4)
                                if j == 0:
                                    act.wait_ge(conv_done, i * 4 + (u + s + 3))
                                    act.activation(sg[:, :], cv[0][:, :], ACT.Silu).then_inc(silu_done, 1)
                                else:
                                    act.wait_ge(hmul, i * 2 + (q + pp + 1))
                                    act.activation(row_of(HH, i * 2 + pp), hf[:, :], ACT.Copy).then_inc(h_hi, 1)
                    n += 2 * nb
                    u += 2 * nb
                    q += nb
                    if bi < len(BLOCKS) - 1:
                        with act.Fori(0, KD // 2) as i:
                            for j in range(2):
                                act.wait_ge(mm_done, i * 2 + (n + j + 1))
                                split_high(n + j + 2, i, 2)
                    else:
                        squares(2 * layer + 2, n)
                    n += KD
                act.wait_ge(st_done, u + 2)
                act.dma_start(io["o_fst"][layer], fst[:, :, :]).then_inc(fst_out, 16)

            squares(1, OUT0)
            ffn(UP0, 0)
            act.wait_ge(fst_out, 16)
            norm(2)
            act.wait_ge(x_lo, KD + 2 * NB3)
            act.dma_start(ptab[:, :], io["ptab"]).then_inc(pt_in, 16)
            act.dma_start(phist[:, :, :, :], io["phist"]).then_inc(phist_in, 16)
            act.dma_start(cw[:, :, :], io["cw"]).then_inc(l1_in, 16)
            act.dma_start(csc[:, :], io["csc"]).then_inc(l1_in, 16)
            act.dma_start(icnt[:, :, :], io["icnt"]).then_inc(l1_in, 16)
            for g in range(4):
                n = IN1 + g
                act.wait_ge(mm_done, n + 1)
                if g == 0:
                    act.wait_ge(pool_zero, 1)
                else:
                    act.wait_ge(pooled, g)
                    act.wait_ge(pst_set, g)
                for dst, src_ in zip(parts(pe0, PH), bank_parts(n % 2)):
                    ins = act.activation(dst, src_, ACT.Copy)
                ins.then_inc(evac_done[n % 2], 1)
                split_high(n + 2)
            act.wait_ge(pst_set, 4)
            act.dma_start(io["o_pst"], pst[:, :, :, :]).then_inc(pst_out, 16)
            act.wait_ge(pooled, 4)
            act.dma_start(RC[:, :], io["rc"]).then_inc(rope_in, 16)
            act.dma_start(RS[:, :], io["rs"]).then_inc(rope_in, 16)
            copied_slabs(IN1 + 4, 4, lambda i, j: qf[j][:, :])

            def roped_slabs(first, count, scale=1.0):
                r = first - IN1 - 8
                copied_slabs(first, count, lambda i, j: qf[j][:, :], scale=scale, free=lambda i, j: (roped, i * 2 + (r + j + 1)))

            roped_slabs(IN1 + 8, 4, HD ** -0.5)
            roped_slabs(IN1 + 12, 8)
            for n in (IN1 + 20, IN1 + 21):
                act.wait_ge(mm_done, n + 1)
                act.wait_ge(roped, n - IN1 - 8 + 1)
                act.activation(three(qf[n % 2][:, :]), bank_set(n % 2), ACT.Copy).then_inc(evac_done[n % 2], 1)
            wait_emptied(act, OUT1 - 1)
            act.wait_ge(w_lo, OUT1)
            act.wait_ge(mm_done, OUT1)
            act.dma_start(wis.rearrange("s h q -> h s q"), qf[1][0:HEADS, NP:NT].rearrange("p (s q) -> p s q", s=SEQS)).then_inc(wi_out, 16)
            for dst, name in ((iota, "iota"), (cmask, "cmask")):
                act.dma_start(dst[:, :], io[name]).then_inc(sconst_in, 16)
            act.dma_start(hsum[:, :, :], io["hsum"]).then_inc(sconst_in, 16)
            act.dma_start(rep[:, :, :], io["rep"]).then_inc(sconst_in, 16)
            act.wait_ge(wi_out, 16)
            for g in range(2):
                act.dma_start(wrow[:, g:g + 1], wis[4 * g:4 * g + 4].rearrange("s h (q a) -> (s h q) a", a=1)).then_inc(wi_in, 16)
            act.wait_ge(roped, 15)
            act.dma_start(io["o_k"], K[:, :, :]).then_inc(kv_out, 16)
            act.dma_start(io["o_ki"], KI[0:IDX, :]).then_inc(kv_out, 16)
            act.dma_start(io["o_v"], VT[:, :, :]).then_inc(kv_out, 16)
            act.dma_start(io["o_vs"], VS[:, :]).then_inc(kv_out, 16)
            for g in range(4):
                act.wait_ge(cmm, g + 1)
                act.wait_ge(z_pre, KD * 2 + g + 1)
                act.activation(three(XH[:, g, :]), bank_set(g % 2), ACT.Copy, scale=csc[:, g:g + 1]).then_inc(c_hi, 1)
            act.dma_start(identb[:, :], io["identb"]).then_inc(identb_in, 16)
            def rectified(t):
                n = P * (3 + t // 8)
                act.wait_ge(dot_mm, t + 1)
                if t >= 2:
                    act.wait_ge(sc_acc, t if t >= 32 else t - 1)
                src_ = pair(1, n) if n > 512 else PS[:, 2 + t % 2, 0:n]
                act.activation(products(t), src_, ACT.Relu).then_inc(dot_relu, 1)
                act.wait_ge(dot_relu, t + 1)
                act.activation(products(t), products(t), ACT.Copy,
                               scale=wtok[:, 2 + t // 8, t % 8:t % 8 + 1]).then_inc(weighted, 1)

            def sample_exp(s):
                act.wait_ge(smax, s + 1)
                if s >= 1:
                    act.wait_ge(stp, s)
                act.activation(sp_[0:NS, :], sample_logits_of(s), ACT.Exp, bias=nmx[0:NS, s % 2:s % 2 + 1],
                               accum_out=psm[0:NS, s % 2:s % 2 + 1]).then_inc(sexp, 1)

            def sample_norm(s):
                act.wait_ge(ssump, s + 1)
                act.activation(sp_[0:NS, :], sp_[0:NS, :], ACT.Copy, scale=prc[0:NS, s % 2:s % 2 + 1]).then_inc(snorm, 1)

            def sample_turned(s):
                act.wait_ge(stp, s + 1)
                if s >= 1:
                    act.wait_ge(spv, s)
                act.activation(spt[:, 0:4, :], PS[:, 4, 0:4 * NS].rearrange("p (t r) -> p t r", t=4), ACT.Copy).then_inc(ste, 1)
                act.activation(spt[0:NS, 4, :], PS[0:NS, 4, 4 * NS:5 * NS], ACT.Copy).then_inc(ste, 1)

            def sample_kept(g):
                act.wait_ge(spv, 4 * g + 4)
                act.activation(PR[1][:, 0:512], PS[:, 5, :], ACT.Copy).then_inc(sv_kept, 1)

            def sample_out(g):
                act.wait_ge(sv_turned, g + 1)
                for h in range(HEADS):
                    half, c = slice(64 * (h % 2), 64 * (h % 2) + 64), h // 2
                    act.activation(atts[half, c, 16 * g:16 * g + 16].rearrange("p (s q) -> p s q", s=4),
                                   PS[half, 5, c * P:(c + 1) * P].rearrange("p (s r) -> p s r", s=4)[:, :, DEC * h:DEC * h + DEC],
                                   ACT.Copy).then_inc(satt, 1)

            def exp(e):
                n = P * (e // 8 + 1)
                act.wait_ge(amax, e + 1)
                if e >= 2:
                    act.wait_ge(atp, e - 1)
                elif e == 1:
                    act.wait_ge(sv_turned, 2)
                act.activation(PR[e % 2][:, 0:n], logits_of(e), ACT.Exp, bias=nmx[:, e % 2:e % 2 + 1],
                               accum_out=psm[:, e % 2:e % 2 + 1]).then_inc(aexp, 1)

            def norm_probs(e):
                if e < 56:
                    n = P * (e // 8 + 1)
                    act.wait_ge(asum, e + 1)
                    act.activation(PR[e % 2][:, 0:n], PR[e % 2][:, 0:n], ACT.Copy,
                                   scale=prc[:, e % 2:e % 2 + 1]).then_inc(anorm, 1)

            def turned_probs(e):
                b = e // 8
                act.wait_ge(atp, e + 1)
                if e >= 2:
                    act.wait_ge(apv, e - 1)
                else:
                    act.wait_ge(slg, SEQS)
                act.activation(PT[e % 2][:, 0:b + 1, :], pair(2, P * (b + 1)).rearrange("p (t q) -> p t q", q=P),
                               ACT.Copy).then_inc(ate, 1)

            def attended(e):
                if e % 2 == 1:
                    b, c = e // 8, (e % 8) // 2
                    act.wait_ge(apv, e + 1)
                    act.activation(XH[:, 4 + c, b * P:(b + 1) * P], PS[:, 6 + (e // 2) % 2, 0:P], ACT.Copy).then_inc(ao_hi, 1)

            for t in range(16):
                rectified(t)
            for k in range(SLOTS + 1):
                if k >= 1:
                    sample_turned(k - 1) if k <= SEQS else turned_probs(k - 1 - SEQS)
                if k < SLOTS:
                    sample_exp(k) if k < SEQS else exp(k - SEQS)
                for t in slot_dots(k):
                    rectified(t)
                if k in (4, 8):
                    sample_kept(k // 4 - 1)
                if k in (5, 9):
                    sample_out(k // 4 - 1)
                if k > SEQS:
                    attended(k - 1 - SEQS)
                if k < SLOTS:
                    sample_norm(k) if k < SEQS else norm_probs(k - SEQS)
            act.wait_ge(atp, 64)
            split_high(OUT1)
            split_high(OUT1 + 1)
            for c in range(4):
                act.activation(XH[:, 4 + c, NP:NT], atts[:, c, :], ACT.Copy).then_inc(ao_hi, 1)
            squares(3, OUT1)
            act.wait_ge(pst_out, 16)
            act.wait_ge(kv_out, 64)
            ffn(UP1, 1)
            norm(4, True)
            act.wait_ge(out_done, 16 * (2 + 2 * TC))
            act.wait_ge(fst_out, 32)

        @block.gpsimd
        def _(pool):
            def split_rest(n, i=None, per=0):
                j = n % 2
                pool.wait_ge(w_hi, val(i, per, n + 1))
                pool.tensor_tensor(WL[j][:, :, :], RAW[j][:, :, :], WH[j][:, :, :].bitcast(F32),
                                   ALU.subtract).then_inc(w_lo, 1)

            def split_rests(first, count):
                with pool.Fori(0, count // 2) as i:
                    for j in range(2):
                        split_rest(first + j, i, 2)

            pool.memset(onesd[:, :], 1.0 / D)
            pool.memset(epst[:, :], EPS)
            pool.memset(bext[:, 0:HIST], 0.0).then_inc(bstd, 1)
            split_rest(0)
            split_rest(1)
            pool.wait_ge(mix_in, 128)
            pool.affine_select(out=wsT[:, :, :], in_=wsT[:, :, :], pattern=[[0, 4], [1, P]], compare_op=ALU.is_ge,
                               fill=0.0, base=0, channel_multiplier=-1).then_inc(masked, 1)
            pool.affine_select(out=bd[:, :, :], in_=bd[:, :, :], pattern=[[0, 4], [1, NS]], compare_op=ALU.is_ge,
                               fill=0.0, base=0, channel_multiplier=-1).then_inc(masked, 1)
            split_rests(2, 8)
            for jj in range(4):
                n = 8 + 3 * jj
                pool.wait_ge(bconv, jj + 1)
                pool.tensor_copy(sample_cols(bext, HIST, HIST + DEC, HIST + DEC)[:, :, 0:HIST],
                                 bh[:, jj, :, :]).then_inc(bhist, 1)
                for d in (2, 3):
                    split_rest(n + d)
                wait_emptied(pool, n + 1)
                pool.tensor_copy(bst[:, jj, 0:2], bext[:, NP:NP + 2])
                pool.tensor_copy(bst[:, jj, 2:18].rearrange("p (s q) -> p s q", s=SEQS),
                                 sample_cols(bext, HIST, HIST + DEC, 2)).then_inc(bstd, 1)
                split_rest(n + 4)

            def sums(l, first):
                pool.wait_ge(mm_done, first + 1)
                pool.memset(zs[:, :], 0.0).then_inc(zs_done, 1)
                pool.memset(zq[:, :], 0.0).then_inc(zq_done, 1)

                def step(i, m, more=True):
                    if more:
                        split_rest(first + m + 2, i, 2)
                    if m == KD - 1:
                        return
                    wait_emptied(pool, first + m, i, 2)
                    pool.wait_ge(zs_done, val(i, 2, 9 * (l - 1) + m + 1))
                    pool.tensor_tensor(zs[:, :], zs[:, :], row_of(Z, val(i, 2, m)), ALU.add).then_inc(zs_done, 1)
                    pool.wait_ge(sq_done, val(i, 2, KD * (l - 1) + m + 1))
                    pool.wait_ge(zq_done, val(i, 2, 9 * (l - 1) + m + 1))
                    pool.tensor_tensor(zq[:, :], zq[:, :], sq[:, :], ALU.add).then_inc(zq_done, 1)

                more = first + KD < SLABS
                with pool.Fori(0, KD // 2 - 1) as i:
                    for j in range(2):
                        step(i, j)
                step(None, KD - 2, more)
                step(None, KD - 1, more)
                pool.wait_ge(ln_a, 4 * (l - 1) + 1)
                wait_emptied(pool, first + KD - 1)
                for c in range(TC) if more else (0, 2):
                    with pool.Fori(0, KD) as m:
                        z = third(Z, m, c)
                        pool.tensor_tensor(z, z, mean[:, c * TW:(c + 1) * TW], ALU.subtract).then_inc(ln_sub, 1)

            def ffn(first, layer):
                n, u = first, layer * 2 * FC
                pool.wait_ge(x_lo, KD + NB3 * (2 * layer + 1))
                pool.memset(ext[0][:, 0:HIST], 0.0)
                ins = pool.memset(ext[1][:, 0:HIST], 0.0)
                if layer == 0:
                    ins.then_inc(st_done, 2)
                pool.wait_ge(fpar_in, 32 * (layer + 1))
                for bi, nb in enumerate(BLOCKS):
                    with pool.Fori(0, nb // 2) as i:
                        for s in range(4):
                            j = s % 2
                            local = i * 4 + (u - layer * 2 * FC + s)
                            pool.wait_ge(conv_done, i * 4 + (u + s + 1))
                            pool.tensor_copy(sample_cols(ext[j], HIST, HIST + DEC, HIST + DEC)[:, :, 0:HIST],
                                             fhist[:, bass.ds(local, 1), :, :].rearrange("p a s q -> p (a s) q")
                                             ).then_inc(ext_hist, 1)
                            wait_emptied(pool, n + s, i, 4)
                            kept = row_of(fst, local)
                            pool.tensor_copy(kept[:, 0:2], ext[j][:, NP:NP + 2])
                            pool.tensor_copy(kept[:, 2:18].rearrange("p (s q) -> p s q", s=SEQS),
                                             sample_cols(ext[j], HIST, HIST + DEC, 2)).then_inc(st_done, 1)
                            split_rest(n + s + 2, i, 4)
                    n += 2 * nb
                    u += 2 * nb
                    if bi < len(BLOCKS) - 1:
                        split_rests(n + 2, KD)
                    else:
                        sums(2 * layer + 2, n)
                    n += KD

            sums(1, OUT0)
            ffn(UP0, 0)
            pool.wait_ge(x_lo, KD + 2 * NB3)
            pool.memset(pe0[:, 0:PH], 0.0).then_inc(pool_zero, 1)
            pool.wait_ge(phist_in, 16)
            for g in range(4):
                n = IN1 + g
                if g >= 1:
                    pool.wait_ge(pooled, g)
                    pool.wait_ge(pst_set, g)
                pool.tensor_copy(sample_cols(pe0, PH, PH + DEC, PH + DEC)[:, :, 0:PH], phist[:, g, :, :]).then_inc(phist_set, 1)
                wait_emptied(pool, n)
                pool.wait_ge(phist_set, g + 1)
                pool.tensor_copy(pst[:, g, 0, :], pe0[:, NP:NP + PH])
                pool.tensor_copy(pst[:, g, 1:9, :], sample_cols(pe0, PH, PH + DEC, PH)).then_inc(pst_set, 1)
                split_rest(n + 2)
            split_rests(IN1 + 6, 16)
            pool.wait_ge(roped, 15)
            pool.memset(QIB[:, :, :], 0.0).then_inc(qib_zero, 1)
            pool.wait_ge(pst_out, 16)
            pool.wait_ge(sdot, KIX_EARLY)
            pool.wait_ge(mm_done, OUT1)
            for g in range(4, 8):
                pool.tensor_tensor(Z[:, g, :], XH[:, g, :].bitcast(F32), XL[:, g, :].bitcast(F32), ALU.add).then_inc(z_up, 1)
            pool.wait_ge(turn_evac, 39)
            pool.memset(MB[:, 0:3 * P], 0.0).then_inc(mb_early, 1)
            pool.wait_ge(mb_early, 1)
            for a in (0, 2 * P):
                ins = pool.affine_select(out=MB[:, a:a + P], in_=MB[:, a:a + P], pattern=[[-1, P]], compare_op=ALU.is_ge,
                                         fill=FAR, base=0, channel_multiplier=1)
            ins.then_inc(mb_early, 1)
            pool.wait_ge(w_lo, OUT1)
            pool.memset(QB[:, :, :, :], 0.0).then_inc(qb_zero, 1)

            def score(t):
                b, h = 2 + t // 8, t % 8
                n = P * (b + 1)
                sc, r_ = SC[b], products(t)
                pool.wait_ge(weighted, t + 1)
                if h == 0:
                    if b >= 6:
                        pool.wait_ge(mb_set, 2)
                    pool.tensor_copy(sc, r_).then_inc(sc_acc, 1)
                else:
                    pool.wait_ge(sc_acc, t)
                    pool.tensor_tensor(sc, sc, r_, ALU.add).then_inc(sc_acc, 1)
                if h == 7:
                    pool.wait_ge(sc_acc, t + 1)
                    diag = sc[:, b * P:(b + 1) * P]
                    pool.affine_select(out=diag, in_=diag, pattern=[[-1, P]], compare_op=ALU.is_ge,
                                       fill=BARRED, base=0, channel_multiplier=1).then_inc(sc_barred, 1)

            for t in range(48):
                score(t)
            pool.wait_ge(apv, 64)
            split_rest(OUT1)
            split_rest(OUT1 + 1)
            sums(3, OUT1)
            ffn(UP1, 1)

        @block.vector
        def _(dve):
            dve.memset(seed[:, 0:1], 0.0).then_inc(evac_done[0], 1)
            dve.memset(seed[:, 1:2], 0.0).then_inc(evac_done[1], 1)
            dve.memset(seed[:, 2:3], 0.0).then_inc(conv_done, 2)
            dve.memset(seed[:, 3:4], 0.0).then_inc(bconv, 1)
            dve.memset(seed[:, 4:5], 0.0).then_inc(turn_evac, 2)
            dve.memset(seed[:, 5:6], 0.0).then_inc(roped, 2)
            for k in range(KD):
                dve.wait_ge(x_hi, k + 1)
                dve.tensor_tensor(XL[:, k, :], Z[:, k, :], XH[:, k, :].bitcast(F32), ALU.subtract).then_inc(x_lo, 1)

            def turned_rows(f0, blocks, tail):
                with dve.Fori(0, 2) as i:
                    for j in range(2):
                        for part in range(3):
                            f = f0 + 3 * j + part
                            dve.wait_ge(turned, i * 6 + (f + 1))
                            cols = bass.ds(i * 256 + j * P, P)
                            if part < 2:
                                dve.tensor_copy(blocks[:, 4 * part:4 * part + 4, cols],
                                                turn_bank(f).rearrange("p (b c) -> p b c", b=4)).then_inc(turn_evac, 1)
                            else:
                                dve.tensor_copy(tail[:, cols], turn_bank(f)[0:NS, 0:P]).then_inc(turn_evac, 1)

            turned_rows(0, vtok, vtoks)
            dve.wait_ge(turn_evac, 14)

            def vblock(t):
                return (vtok[:, t, :], P) if t < 8 else (vtoks[:, :], NS)

            for t in range(9):
                a, w = vblock(t)
                dve.bn_stats(vst[0:w, t, :], a).then_inc(vstat, 1)
            for t in range(9):
                w = vblock(t)[1]
                dve.wait_ge(vstat, t + 1)
                dve.bn_aggr(vmv[0:w, t, :], vst[0:w, t, :]).then_inc(vagg, 1)
            dve.wait_ge(vsd, 2)
            dve.reciprocal(vrs[:, 0:8], vrs[:, 0:8]).then_inc(vln, 1)
            dve.reciprocal(vrs[0:NS, 8:9], vrs[0:NS, 8:9]).then_inc(vln, 1)
            dve.wait_ge(vln, 2)
            dve.wait_ge(mix_in, 128)
            for t in range(9):
                a, w = vblock(t)
                dve.tensor_scalar(a, a, vmv[0:w, t, 0:1], vrs[0:w, t:t + 1], ALU.subtract, ALU.mult).then_inc(vln, 1)
            for t in range(9):
                a, w = vblock(t)
                dve.wait_ge(vln, 2 + t + 1)
                dve.tensor_tensor(a, a, lng[0:w, :], ALU.mult).then_inc(vln, 1)
            for t in range(9):
                a, w = vblock(t)
                dve.wait_ge(vln, 11 + t + 1)
                dve.tensor_tensor(a, a, lnb[0:w, :], ALU.add).then_inc(vnorm, 1)

            def mix_rest(k):
                dve.wait_ge(mix_hi, k + 1)
                dve.tensor_tensor(ML[:, k, :], cf[:, :], MH[:, k, :].bitcast(F32), ALU.subtract).then_inc(mix_lo, 1)

            for g in range(4):
                if g >= 1:
                    dve.wait_ge(mix_lo, g)
                for part in range(3):
                    f = 12 + 3 * g + part
                    dve.wait_ge(turned, f + 1)
                    if part < 2:
                        o = cf[:, part * 512:(part + 1) * 512].rearrange("p (b t) -> p b t", b=4)
                        dve.tensor_tensor(o, turn_bank(f).rearrange("p (b t) -> p b t", b=4),
                                          bsb[:, g, None, :].to_broadcast([P, 4, P]), ALU.add).then_inc(turn_evac, 1)
                    else:
                        o = cf[:, NP:NT].rearrange("p (s q) -> p s q", s=SEQS)
                        dve.tensor_tensor(o, turn_bank(f)[:, 0:NS].rearrange("p (s q) -> p s q", s=SEQS),
                                          bsb[:, g, None, 0:DEC].to_broadcast([P, SEQS, DEC]), ALU.add).then_inc(turn_evac, 1)
                dve.wait_ge(turn_evac, 2 + f + 1)
                if g == 0:
                    wait_emptied(dve, 6)
                    wait_emptied(dve, 7)
                dve.tensor_tensor(cf[:, :], cf[:, :], U[:, g, :], ALU.mult).then_inc(gate_f, 1)
                mix_rest(g)

            def taps(row, out, w, tap_sem, value, done):
                if len(w) == 4:
                    dve.tensor_scalar(out, row[:, 2:2 + CW], w[2], w[3], ALU.mult, ALU.add).then_inc(tap_sem, 1)
                else:
                    dve.tensor_scalar(out, row[:, 2:2 + CW], w[2], None, ALU.mult).then_inc(tap_sem, 1)
                dve.wait_ge(tap_sem, value(1))
                dve.scalar_tensor_tensor(out, row[:, 0:CW], w[0], out, ALU.mult, ALU.add).then_inc(tap_sem, 1)
                dve.wait_ge(tap_sem, value(2))
                dve.scalar_tensor_tensor(out, row[:, 1:1 + CW], w[1], out, ALU.mult, ALU.add).then_inc(done, 1)

            for jj in range(4):
                n = 8 + 3 * jj
                dve.wait_ge(mm_done, n + 2)
                wait_emptied(dve, n)
                dve.wait_ge(bstd, jj + 1)
                for dst, src_, c in zip(parts(bext, HIST), bank_parts((n + 1) % 2), parts(cf)):
                    ins = dve.tensor_tensor(dst, src_, c, ALU.mult)
                ins.then_inc(evac_done[(n + 1) % 2], 1)
                wait_emptied(dve, n + 1)
                dve.wait_ge(bhist, jj + 1)
                taps(bext, bcv[:, :], [bw[:, jj, t:t + 1] for t in range(3)], btap, lambda k: 2 * jj + k, bconv)
                dve.wait_ge(bconv, jj + 2)
                dve.wait_ge(mm_done, n + 3)
                conv_parts = [bcv[:, 0:2 * TW].rearrange("p (c t) -> p c t", c=2), bcv[:, 2 * TW:NP],
                              sample_cols(bcv, 0, HIST + DEC, DEC)]
                for dst, src_, c in zip(parts(cf), bank_parts(n % 2), conv_parts):
                    ins = dve.tensor_tensor(dst, src_, c, ALU.mult)
                ins.then_inc(evac_done[n % 2], 1)
                mix_rest(4 + jj)

            def projected(first, pres, before=None):
                with dve.Fori(0, KD // 2) as i:
                    for j in range(2):
                        n = first + j
                        z = row_of(Z, i * 2 + j)
                        if pres is not None:
                            dve.tensor_tensor(z, row_of(XH, i * 2 + j).bitcast(F32), row_of(XL, i * 2 + j).bitcast(F32),
                                              ALU.add).then_inc(z_pre, 1)
                            dve.wait_ge(z_pre, i * 2 + (pres + j + 1))
                        dve.wait_ge(mm_done, i * 2 + (n + 1))
                        if pres is not None or before:
                            dve.scalar_tensor_tensor(three(z), three(z), ALPHA, bank_set(j), ALU.mult,
                                                     ALU.add).then_inc(evac_done[j], 1)
                        else:
                            dve.tensor_tensor(three(z), three(z), bank_set(j), ALU.add).then_inc(evac_done[j], 1)

            def norm(l, last=False):
                last_slab = (OUT0, IN1 - KD, OUT1, SLABS - KD)[l - 1] + KD - 1
                m, sqr, dev = (stats[:, x, :] for x in range(3))
                blocks = NT // SB

                def diagonal(out, v):
                    return dve.tensor_tensor(out[:, :, :], ident[0:SB, None, 0:SB].to_broadcast([SB, blocks, SB]),
                                             v[:, :, None].to_broadcast([SB, blocks, SB]), ALU.mult)

                dve.wait_ge(zs_done, 9 * l - 1)
                wait_emptied(dve, last_slab)
                dve.tensor_tensor(zs[:, :], zs[:, :], Z[:, KD - 1, :], ALU.add).then_inc(zs_done, 1)
                dve.wait_ge(zq_done, 9 * l - 1)
                dve.wait_ge(sq_done, KD * l)
                dve.tensor_tensor(zq[:, :], zq[:, :], sq[:, :], ALU.add).then_inc(zq_done, 1)
                dve.wait_ge(ln_mean, l)
                dve.tensor_copy(m, PS[0:SB, 6, 0:blocks]).then_inc(ln_m, 1)
                dve.wait_ge(ln_m, l)
                dve.tensor_tensor(sqr, m, m, ALU.mult).then_inc(ln_var, 1)
                dve.wait_ge(ln_sq, l)
                dve.wait_ge(ln_var, 3 * l - 2)
                dve.tensor_tensor(dev, PS[0:SB, 7, 0:blocks], sqr, ALU.subtract).then_inc(ln_var, 1)
                dve.wait_ge(ln_var, 3 * l - 1)
                dve.tensor_scalar(dev, dev, 0.0, None, ALU.max).then_inc(ln_var, 1)
                dve.wait_ge(ln_sd, l)
                dve.reciprocal(dev, dev).then_inc(ln_rstd, 1)
                dve.wait_ge(ln_rstd, l)
                diagonal(drstd, dev).then_inc(ln_diag, 1)

                def scaled(c, m0, i=None):
                    for j in range(2):
                        x = val(i, 2, m0 + j)
                        z = third(Z, x, c)
                        if last and c == 1:
                            if j == 0:
                                for y in range(2):
                                    zy = third(Z, val(i, 2, m0 + y), c)
                                    dve.tensor_tensor(zy, zy, mean[:, c * TW:(c + 1) * TW], ALU.subtract).then_inc(ln_own, 1)
                            dve.wait_ge(ln_own, val(i, 2, m0 + j + 1))
                        else:
                            before = KD if last and c == 2 else KD * c
                            dve.wait_ge(ln_sub, val(i, 2, NB3 * (l - 1) + before + m0 + j + 1))
                        if m0 == 0 and i is None and j == 0:
                            dve.wait_ge(ln_a, 4 * (l - 1) + c + 2)
                        dve.tensor_tensor(z, z, rstd[:, c * TW:(c + 1) * TW], ALU.mult).then_inc(ln_d, 1)

                def rests(c, m0, i=None):
                    if last:
                        return
                    for j in range(2):
                        x = val(i, 2, m0 + j)
                        dve.wait_ge(x_hi, val(i, 2, KD + NB3 * (l - 1) + KD * c + m0 + j + 1))
                        xl = third(XL, x, c)
                        dve.tensor_tensor(xl, xl.bitcast(F32), third(XH, x, c).bitcast(F32), ALU.subtract).then_inc(x_lo, 1)

                scaled(0, 0)
                for c in range(TC):
                    with dve.Fori(0, KD // 2 - 1) as i:
                        scaled(c, 2, i)
                        rests(c, 0, i)
                    if c < TC - 1:
                        scaled(c + 1, 0)
                    rests(c, KD - 2)

            def ffn(first, layer):
                n, u, q = first, layer * 2 * FC, layer * FC
                dve.wait_ge(fpar_in, 32 * (layer + 1))
                for bi, nb in enumerate(BLOCKS):
                    with dve.Fori(0, nb // 2) as i:
                        for pp in range(2):
                            for j in range(2):
                                s = 2 * pp + j
                                wait_emptied(dve, n + s, i, 4)
                                dve.wait_ge(ext_hist, i * 4 + (u + s + 1))
                                w = row_of(fpar, i * 4 + (u - layer * 2 * FC + s))
                                taps(ext[j], cv[j][:, :], [w[:, t:t + 1] for t in range(4)], tap,
                                     lambda k: i * 8 + (2 * (u + s) + k), conv_done)
                            pq = i * 2 + (q + pp + 1)
                            dve.wait_ge(silu_done, pq)
                            dve.wait_ge(conv_done, i * 4 + (u + 2 * pp + 1 + 3))
                            dve.tensor_tensor(hf[:, 0:NP], sg[:, 0:NP], cv[1][:, 0:NP], ALU.mult)
                            dve.tensor_tensor(hf[:, NP:NT].rearrange("p (s q) -> p s q", s=SEQS),
                                              sample_cols(sg, 0, HIST + DEC, DEC), sample_cols(cv[1], 0, HIST + DEC, DEC),
                                              ALU.mult).then_inc(hmul, 1)
                            dve.wait_ge(h_hi, pq)
                            dve.tensor_tensor(row_of(HL, i * 2 + pp), hf[:, :], row_of(HH, i * 2 + pp).bitcast(F32),
                                              ALU.subtract).then_inc(h_lo, 1)
                    n += 2 * nb
                    u += 2 * nb
                    q += nb
                    projected(n, KD + (KD + 4) * layer if bi == 0 else None)
                    n += KD

            projected(OUT0, 0)
            norm(1)
            ffn(UP0, 0)
            norm(2)
            dve.wait_ge(l1_in, 48)
            step = 0
            for g, w in enumerate((2, 4, 8, 16)):
                wait_emptied(dve, IN1 + g)
                dve.wait_ge(phist_set, g + 1)
                a, bufs, width = pe0, [pe1, pe2], 1
                while width < w:
                    o = bufs[0]
                    lo = 2 * width - 1
                    dve.tensor_tensor(o[:, lo:PEXT], a[:, lo:PEXT], a[:, lo - width:PEXT - width], ALU.add).then_inc(pwin, 1)
                    step += 1
                    dve.wait_ge(pwin, step)
                    a, bufs, width = o, bufs[::-1], 2 * width
                dve.scalar_tensor_tensor(Z[:, g, 16:NP], a[:, PH + 16:PH + NP], 1.0 / w, pe0[:, PH + 16:PH + NP],
                                         ALU.mult, ALU.subtract)
                dve.scalar_tensor_tensor(Z[:, g, NP:NT].rearrange("p (s q) -> p s q", s=SEQS),
                                         sample_cols(a, PH, PH + DEC, DEC), 1.0 / w, sample_cols(pe0, PH, PH + DEC, DEC),
                                         ALU.mult, ALU.subtract)
                dve.tensor_tensor(a[:, PH:PH + 16], a[:, PH:PH + 16], icnt[:, g, :], ALU.mult).then_inc(pwin, 1)
                step += 1
                dve.wait_ge(pwin, step)
                dve.tensor_tensor(Z[:, g, 0:16], a[:, PH:PH + 16], pe0[:, PH:PH + 16], ALU.subtract).then_inc(pooled, 1)
            turned_rows(24, VT, VS)

            def rotate(r, j, dst, i=None):
                dve.wait_ge(rope_in, 32)
                dve.wait_ge(roped, val(i, 2, r + 2))
                wait_emptied(dve, IN1 + 8 + r, i, 2)
                dve.tensor_tensor(dst, qf[j][:, :], RC[:, :], ALU.mult).then_inc(rcos, 1)
                dve.stream_shuffle(sh[:, :], qf[j][:, :], [p ^ 8 if p < 16 else p for p in range(32)]).then_inc(shuf, 1)
                dve.wait_ge(shuf, val(i, 2, r + 1))
                dve.tensor_tensor(sh[:, :], sh[:, :], RS[:, :], ALU.mult).then_inc(shufs, 1)
                dve.wait_ge(shufs, val(i, 2, r + 1))
                dve.wait_ge(rcos, val(i, 2, r + 1))
                dve.tensor_tensor(dst, dst, sh[:, :], ALU.add).then_inc(roped, 1)

            for r0, t in ((0, Q), (4, K), (8, QI)):
                with dve.Fori(0, 2) as i:
                    for j in range(2):
                        rotate(r0 + j, j, row_of(t, i * 2 + j), i)
            rotate(12, 0, KI[:, :])
            dve.wait_ge(turned, 37)
            dve.tensor_copy(wtok[:, 0:8, :], turn_bank(36)[:, 0:8 * HEADS].rearrange("p (t h) -> p t h", t=8)).then_inc(turn_evac, 1)
            def blocked(dst, src, cleared, done):
                dve.wait_ge(cleared, 1)
                for h in range(HEADS):
                    half = slice(64 * (h % 2), 64 * (h % 2) + 64)
                    dve.tensor_copy(dst(half, h), src[half, h // 2, NP:NT].rearrange("p (s q) -> p s q", s=SEQS)).then_inc(done, 1)

            def sample_relu(g):
                dve.wait_ge(wi_in, 32)
                dve.wait_ge(sdot, 4 * (g + 1))
                dve.tensor_scalar(rab[g][:, :], pair(3, SK), 0.0, wrow[:, g:g + 1], ALU.max, ALU.mult).then_inc(srelu, 1)

            blocked(lambda half, h: QIB[half, :, DEC * h:DEC * h + DEC], QI, qib_zero, qib_set)
            for g in range(4):
                dve.wait_ge(cmm, g + 1)
                dve.tensor_tensor(Z[:, g, :], XH[:, g, :].bitcast(F32), XL[:, g, :].bitcast(F32), ALU.add).then_inc(z_pre, 1)
                dve.wait_ge(c_hi, g + 1)
                dve.scalar_tensor_tensor(three(XL[:, g, :]), bank_set(g % 2), csc[:, g:g + 1], three(XH[:, g, :].bitcast(F32)),
                                         ALU.mult, ALU.subtract).then_inc(cevac, 1)
                if g == 1:
                    sample_relu(0)
            sample_relu(1)
            dve.wait_ge(ssum, 1)
            dve.wait_ge(sconst_in, 64)
            dve.tensor_copy(ssc[:, 0:PAST], PS[0:NS, 6, :]).then_inc(ssc_set, 1)
            dve.tensor_tensor(ssc[:, PAST:SK], PS[0:NS, 7, 0:NS], cmask[:, :], ALU.add).then_inc(ssc_set, 1)
            dve.wait_ge(ssc_set, 2)
            for r in range(TOPK_S // 8):
                dve.max(s8[:, :], ssc[:, :]).then_inc(stop_, 1)
                dve.wait_ge(stop_, 2 * r + 1)
                dve.match_replace(ssc[:, :], s8[:, :], ssc[:, :], TAKEN).then_inc(stop_, 1)
                dve.wait_ge(stop_, 2 * r + 2)
            dve.max(s8[:, :], ssc[:, :]).then_inc(sidx_set, 1)
            dve.wait_ge(sidx_set, 1)
            dve.max_index(sidx[:, :], s8[:, :], ssc[:, :]).then_inc(sidx_set, 1)
            dve.wait_ge(sidx_set, 2)
            dve.tensor_copy(sidf[:, :], sidx[:, 0:1]).then_inc(sidx_set, 1)
            dve.wait_ge(sidx_set, 3)
            dve.tensor_scalar(sbias[:, :], iota[:, :], sidf[:, 0:1], FAR, ALU.not_equal, ALU.mult).then_inc(sb_set, 1)
            dve.wait_ge(sb_set, 1)
            dve.scalar_tensor_tensor(sbias[:, :], ssc[:, :], TAKEN, sbias[:, :], ALU.is_gt, ALU.mult).then_inc(sb_set, 1)
            blocked(lambda half, h: QB[half, h // 2, :, DEC * h:DEC * h + DEC], Q, qb_zero, qb_set)

            def best(u):
                r, second = u // 2, u % 2
                blocks = GROUPS[r // BEST]
                if r % BEST == 0 and not second:
                    dve.wait_ge(sc_barred, blocks[-1] - 1)
                for x, b in enumerate(blocks):
                    if u % (2 * BEST):
                        dve.wait_ge(top_, 2 * u - 1 + x)
                    if second:
                        dve.match_replace(SC[b], m8[x][:, :], SC[b], TAKEN).then_inc(top_, 1)
                    else:
                        dve.max(m8[x][:, :], SC[b]).then_inc(top_, 1)
                if u % (2 * BEST) == 2 * BEST - 1:
                    for x, b in enumerate(blocks):
                        dve.wait_ge(top_, 2 * u + 1 + x)
                        dve.tensor_scalar(MB[:, mask_cols(b)], SC[b], TAKEN, FAR, ALU.is_gt, ALU.mult).then_inc(mb_set, 1)

            def rounds(k, part):
                a, z = start_round[k], start_round[k + 1]
                mid = min(a + 1, z)
                for r in range(a, mid) if part == 0 else range(mid, z):
                    best(r)

            def sample_max(s):
                j = s % 2
                dve.wait_ge(slg, s + 1)
                dve.tensor_reduce(nmx[0:NS, j:j + 1], sample_logits_of(s), AXX, ALU.max, negate=True).then_inc(smax, 1)

            def sample_recip(s):
                j = s % 2
                dve.wait_ge(sexp, s + 1)
                dve.reciprocal(prc[0:NS, j:j + 1], psm[0:NS, j:j + 1]).then_inc(ssump, 1)

            def row_max(e):
                n, j = P * (e // 8 + 1), e % 2
                dve.wait_ge(lg, e + 1)
                dve.tensor_reduce(nmx[:, j:j + 1], logits_of(e), AXX, ALU.max, negate=True).then_inc(amax, 1)

            def row_recip(e):
                n, j = P * (e // 8 + 1), e % 2
                dve.wait_ge(aexp, e + 1)
                dve.reciprocal(prc[:, j:j + 1], psm[:, j:j + 1]).then_inc(asum, 1)
                if e >= 56:
                    dve.wait_ge(asum, e + 1)
                    dve.tensor_scalar(PR[j][:, 0:n], PR[j][:, 0:n], prc[:, j:j + 1], None, ALU.mult).then_inc(anorm, 1)

            def att_rest(pr):
                dve.wait_ge(ao_hi, pr + 1)
                b, c = pr // 4, pr % 4
                dve.tensor_tensor(XL[:, 4 + c, b * P:(b + 1) * P], PS[:, 6 + pr % 2, 0:P],
                                  XH[:, 4 + c, b * P:(b + 1) * P].bitcast(F32), ALU.subtract).then_inc(ao_lo, 1)

            for k in range(SLOTS):
                e = k - SEQS
                sample_max(k) if k < SEQS else row_max(e)
                rounds(k, 0)
                sample_recip(k) if k < SEQS else row_recip(e)
                if e >= 3 and e % 2 == 1:
                    att_rest((e - 3) // 2)
                rounds(k, 1)
            att_rest(31)
            for c in range(4):
                dve.wait_ge(ao_hi, 32 + c + 1)
                dve.tensor_tensor(XL[:, 4 + c, NP:NT], atts[:, c, :], XH[:, 4 + c, NP:NT].bitcast(F32),
                                  ALU.subtract).then_inc(ao_lo, 1)
            projected(OUT1, None, before=True)
            norm(3)
            ffn(UP1, 1)
            norm(4, True)


def kernel(**inputs):
    import numpy as np
    import concourse.bacc as bacc
    from concourse import mybir as mb
    from concourse.bass_utils import run_bass_kernel_spmd

    a = {k: np.asarray(v) for k, v in inputs.items()}
    f32 = np.float32

    def rows(w, kc):
        s = w.reshape(kc, P, -1, P).transpose(2, 1, 0, 3)
        if kc == KD:
            return s
        out = np.zeros((s.shape[0], P, KD, P), f32)
        out[:, :, :kc] = s
        return out

    def feature_major(x):
        c = x.shape[-1]
        y = np.moveaxis(x.reshape(x.shape[:-1] + (c // P, P)), (-1, -2), (0, 1))
        return np.ascontiguousarray(y)

    we = a["w_in_even"][0]
    cols = lambda w, o, n: w[:, o:o + n]
    even = [cols(we, 512, 512), cols(we, 0, 512)]
    for jj in range(4):
        for base in (1536, 2048, 1024):
            even.append(cols(we, base + jj * P, P))
    wo = a["w_in_odd"][0]
    ki = cols(wo, 2560, 64)
    wi = np.zeros((D, P), f32)
    wi[:, :HEADS] = cols(wo, 2624, HEADS)
    odd = [cols(wo, 0, 512), cols(wo, 1536, 512), cols(wo, 512, 512), cols(wo, 1024, 512), cols(wo, 2048, 512), ki, ki, wi]

    def ffn_slabs(layer):
        up, down = a["ffn_w_up"][layer], a["ffn_w_down"][layer]
        out, c = [], 0
        for nb in BLOCKS:
            both = [cols(up, half * FC * P + (c + q) * P, P) for q in range(nb) for half in (0, 1)]
            out.append(rows(np.concatenate(both, 1), KD))
            out.append(rows(down[c * P:(c + nb) * P], nb))
            c += nb
        return out

    slab_list = [rows(np.concatenate(even, 1), KD), rows(a["w_out_even"][0], KD), *ffn_slabs(0),
                 rows(np.concatenate(odd, 1), KD), rows(a["w_out_odd"][0], KD), *ffn_slabs(1)]
    slab_array = np.concatenate(slab_list, 0)
    assert slab_array.shape == (SLABS, P, KD, P)

    x = np.concatenate([a["x_prompt"].reshape(NP, D), a["x_sample"].reshape(NS, D)], 0)
    ws = a["a_ws"][0]
    bd = np.zeros((NS, 4, NS), f32)
    for s in range(SEQS):
        bd[DEC * s:DEC * s + DEC, :, DEC * s:DEC * s + DEC] = ws[:, :DEC, :DEC].transpose(2, 0, 1)
    spread = lambda v: np.ascontiguousarray(np.broadcast_to(v, (P,) + v.shape))

    def ffn_order(v):
        y = v.reshape(v.shape[:-1] + (2, FC, P))
        y = np.moveaxis(y, (-1, -2, -3), (0, 1, 2))
        return np.ascontiguousarray(y.reshape((P, 2 * FC) + y.shape[3:]))

    fpar = np.stack([np.concatenate([ffn_order(a["ffn_conv_w"][l]), ffn_order(a["ffn_conv_b"][l][None])], 2) for l in range(2)])
    fhist = np.stack([ffn_order(a["state_ffn_conv"][l]) for l in range(2)])
    lnp = np.stack([np.stack([feature_major(a[f"ln_{k}_{p}"][l]) for p in "gb"], 1)
                    for l in range(2) for k in ("mix", "ffn")], 1)

    pos = np.concatenate([np.arange(NP), np.tile(PAST + np.arange(DEC), SEQS)]).astype(f32)
    rot, halfr = HD // 4, HD // 8
    inv = np.power(f32(500000.0), -np.arange(halfr, dtype=f32) * f32(2.0) / f32(rot)).astype(f32)
    ang = (pos[None, :] * inv[:, None]).astype(f32)
    rc, rs = np.ones((P, NT), f32), np.zeros((P, NT), f32)
    for h in (0, HD):
        rc[h:h + halfr] = rc[h + halfr:h + rot] = np.cos(ang)
        rs[h:h + halfr], rs[h + halfr:h + rot] = -np.sin(ang), np.sin(ang)
    icnt = spread(np.stack([1.0 / np.minimum(w, np.arange(16) + 1.0) for w in (2, 4, 8, 16)]).astype(f32))
    rep = np.zeros((NS, SEQS, HEADS, DEC), f32)
    hsum = np.zeros((4, HEADS, DEC, 2, SEQS, DEC), f32)
    cmask = np.full((SEQS, DEC, SEQS, DEC), BARRED, f32)
    for s in range(SEQS):
        for q in range(DEC):
            rep[DEC * s + q, s, :, q] = 1.0
            hsum[s % 4, :, q, s // 4, s, q] = 1.0
            cmask[s, q, s, :q + 1] = 0.0
    import ml_dtypes

    ck = a["cache_k"][0].transpose(0, 2, 3, 1).reshape(POOLED, 4, P, PAGE).transpose(0, 2, 1, 3)
    kidx = a["cache_kidx"][0].transpose(0, 2, 1)
    arrays = dict(
        slabs=slab_array, xT=feature_major(x), ident=np.eye(P, dtype=f32), identb=np.eye(P).astype(ml_dtypes.bfloat16),
        lng=spread(a["a_ln_g"][0]), lnb=spread(a["a_ln_b"][0]), wsT=ws.transpose(2, 0, 1), bd=bd,
        bsb=spread(a["a_bs"][0]), bw=feature_major(a["b_conv_w"][0]), bh=feature_major(a["state_b_conv"][0]),
        lnp=lnp, fpar=fpar, fhist=fhist, phist=feature_major(a["state_c_pool"][0]), cw=a["c_w"][0].transpose(1, 0, 2),
        csc=feature_major(a["c_scale"][0]), icnt=icnt, rc=rc, rs=rs, rep=rep.reshape(NS, SEQS, NS).astype(ml_dtypes.bfloat16),
        hsum=hsum.reshape(P, 2, NS), cmask=cmask.reshape(NS, NS),
        iota=np.ascontiguousarray(np.broadcast_to(np.arange(SK, dtype=f32), (NS, SK))),
        ptab=a["page_table"].reshape(1, -1), ck=ck, cv=a["cache_v"][0].reshape(POOLED, PAGE, 512),
        kidx=np.concatenate([kidx, kidx], 1),
    )
    outs = dict(o_y=(P, KD, NT), o_av=(NS, 512), o_bst=(P, 4, 18), o_pst=(P, 4, 9, PH), o_k=(P, 4, NT), o_ki=(IDX, NT),
                o_v=(P, 8, 512), o_vs=(NS, 512), o_fst=(2, P, 2 * FC, 18))

    nc = bacc.Bacc("TRN2", target_bir_lowering=False, num_devices=1, dynamic_dma_scratch_size=1024)
    io, feed = {}, {}
    for name, v in arrays.items():
        v = np.ascontiguousarray(v)
        feed["in_" + name] = v
        io[name] = nc.dram_tensor("in_" + name, v.shape, mb.dt.from_np(v.dtype), kind="ExternalInput").ap()
    for name, shape in outs.items():
        io[name] = nc.dram_tensor("out_" + name, shape, mb.dt.float32, kind="ExternalOutput").ap()
    build(nc, io)
    got = run_bass_kernel_spmd(nc, [feed], core_ids=[0]).results[0]
    r = {name: np.asarray(got["out_" + name]) for name in outs}

    def positions(y):
        y = y.transpose(2, 1, 0).reshape(y.shape[2], -1)
        return y[:NP], y[NP:]

    yp, ys = positions(r["o_y"])
    kp, ks = positions(r["o_k"])
    kip, kis = r["o_ki"].T[:NP], r["o_ki"].T[NP:]
    vp = r["o_v"].transpose(1, 0, 2).reshape(NP, 512)
    b = r["o_bst"].transpose(2, 1, 0).reshape(18, 512)
    c = r["o_pst"].transpose(2, 3, 1, 0).reshape(9, PH, 512)
    f = r["o_fst"].reshape(2, P, FC, 2, 18).transpose(0, 4, 3, 2, 1).reshape(2, 18, 2 * FC * P)
    C = np.ascontiguousarray
    return (C(yp.reshape(1, NP, D)), C(ys.reshape(SEQS, DEC, D)), C(r["o_av"].reshape(1, SEQS, DEC, 512)),
            C(b[:2].reshape(1, 1, 2, 512)), C(b[2:].reshape(1, SEQS, 2, 512)),
            C(c[:1].reshape(1, 1, PH, 512)), C(c[1:].reshape(1, SEQS, PH, 512)),
            C(kp.reshape(1, 1, NP, HEADS, HD)), C(vp.reshape(1, 1, NP, HEADS, HD)), C(kip.reshape(1, 1, NP, IDX)),
            C(ks.reshape(1, SEQS, DEC, HEADS, HD)), C(r["o_vs"].reshape(1, SEQS, DEC, HEADS, HD)),
            C(kis.reshape(1, SEQS, DEC, IDX)),
            C(f[:, :2].reshape(2, 1, 2, 2 * FC * P)), C(f[:, 2:].reshape(2, SEQS, 2, 2 * FC * P)))
```
